# Optimizing a Trainium2 kernel written in Bass

```python
import math
import jax, jax.numpy as jnp
from jax import lax
import numpy as np

D_MODEL = 1024
BATCH = 1
SEQ = 1024
DEPTH = 1

MIX_WIDTH = D_MODEL
GLA_HEADS = 4
GLA_WIDTH = MIX_WIDTH // 2
GLA_DV = GLA_WIDTH // GLA_HEADS
GLA_DK = GLA_DV // 2
GLA_RANK = 16
GLA_TAU = 16.0
HG_HEADS = 4
HG_WIDTH = MIX_WIDTH - GLA_WIDTH
HG_DK = HG_WIDTH // HG_HEADS
HG_DV = HG_DK
CHUNK = 64
IN_SIZES = (GLA_HEADS * GLA_DK, GLA_HEADS * GLA_DK, GLA_WIDTH, GLA_WIDTH, GLA_RANK,
            HG_WIDTH, HG_WIDTH, HG_WIDTH, HG_WIDTH)
IN_COLS = GLA_HEADS * GLA_DK * 2 + GLA_WIDTH * 2 + GLA_RANK + HG_WIDTH * 4
N_GROUPS = 4
EXPERTS_PER_GROUP = 8
N_EXPERTS = N_GROUPS * EXPERTS_PER_GROUP
EXPERT_FF = D_MODEL // 4
TOP_K = 2
EPS = 1e-6

kernel_name = "hymba_gla_hgrn2_hmoe_adaln"

def rmsnorm(x, g):
    xf = x.astype(jnp.float32)
    r = lax.rsqrt(jnp.mean(xf * xf, axis=-1, keepdims=True) + EPS)
    return xf * r * g.astype(jnp.float32)

def modulate(hf, shift, scale, dtype):
    return (hf * (1.0 + scale[:, None, :].astype(jnp.float32)) + shift[:, None, :].astype(jnp.float32)).astype(dtype)

def chunk_gated_linear_attention(q, k, v, log_g):
    B, S, H, dk = q.shape
    dv = v.shape[-1]
    nc = S // CHUNK

    def to_chunks(t):
        return t.astype(jnp.float32).reshape(B, nc, CHUNK, H, t.shape[-1]).transpose(1, 0, 3, 2, 4)

    causal = jnp.tril(jnp.ones((CHUNK, CHUNK), dtype=bool))

    def step(state, inp):
        qc, kc, vc, gc = inp
        b = jnp.cumsum(gc, axis=2)
        diff = jnp.where(causal[:, :, None], b[:, :, :, None, :] - b[:, :, None, :, :], -jnp.inf)
        attn = jnp.sum(qc[:, :, :, None, :] * kc[:, :, None, :, :] * jnp.exp(diff), axis=-1)
        o = jnp.einsum('bhij,bhjv->bhiv', attn, vc) + jnp.einsum('bhik,bhkv->bhiv', qc * jnp.exp(b), state)
        b_last = b[:, :, -1:, :]
        state = jnp.exp(b_last[:, :, 0, :])[..., None] * state + jnp.einsum(
            'bhjk,bhjv->bhkv', kc * jnp.exp(b_last - b), vc)
        return state, o

    s0 = jnp.zeros((B, H, dk, dv), jnp.float32)
    _, o = lax.scan(step, s0, (to_chunks(q), to_chunks(k), to_chunks(v), to_chunks(log_g)))
    return o.transpose(1, 0, 3, 2, 4).reshape(B, S, H, dv)

def head_rmsnorm(o, g):
    r = lax.rsqrt(jnp.mean(o * o, axis=-1, keepdims=True) + EPS)
    return o * r * g.astype(jnp.float32)

def hybrid_mixer(h, w_in, gla_w_a2, gla_b_a, gla_norm_g, hg_norm_g, lb, w_out):
    B, S, _ = h.shape
    proj = h @ w_in
    offs = []
    acc = 0
    for s in IN_SIZES[:-1]:
        acc += s
        offs.append(acc)
    gq, gk, gv, gg, ga, hq, hf, hi, hg = jnp.split(proj, offs, axis=-1)

    q = gq.reshape(B, S, GLA_HEADS, GLA_DK).astype(jnp.float32) * (GLA_DK ** -0.5)
    k = gk.reshape(B, S, GLA_HEADS, GLA_DK)
    v = gv.reshape(B, S, GLA_HEADS, GLA_DV)
    a_logit = (ga @ gla_w_a2 + gla_b_a).astype(jnp.float32)
    log_alpha = (jax.nn.log_sigmoid(a_logit) / GLA_TAU).reshape(B, S, GLA_HEADS, GLA_DK)
    o_a = chunk_gated_linear_attention(q, k, v, log_alpha)
    o_a = head_rmsnorm(o_a, gla_norm_g) * jax.nn.silu(gg.astype(jnp.float32)).reshape(B, S, GLA_HEADS, GLA_DV)
    o_a = o_a.reshape(B, S, GLA_WIDTH)

    f = lb + (1.0 - lb) * jax.nn.sigmoid(hf.astype(jnp.float32))
    k_h = (1.0 - f).reshape(B, S, HG_HEADS, HG_DK)
    log_f = jnp.log(f).reshape(B, S, HG_HEADS, HG_DK)
    q_h = hq.reshape(B, S, HG_HEADS, HG_DK).astype(jnp.float32) * (HG_DK ** -0.5)
    i_h = hi.reshape(B, S, HG_HEADS, HG_DV)
    o_b = chunk_gated_linear_attention(q_h, k_h, i_h, log_f)
    o_b = head_rmsnorm(o_b, hg_norm_g) * jax.nn.silu(hg.astype(jnp.float32)).reshape(B, S, HG_HEADS, HG_DV)
    o_b = o_b.reshape(B, S, HG_WIDTH)

    o = jnp.concatenate([o_a, o_b], axis=-1).astype(h.dtype)
    return o @ w_out

def hierarchical_moe(h, w_rg, b_rg, w_re, b_re, w_gate, w_up, w_down):
    B, S, D = h.shape
    hf = h.reshape(B * S, D)
    g_probs = jax.nn.softmax((hf @ w_rg + b_rg).astype(jnp.float32), axis=-1)
    g_p, g_idx = lax.top_k(g_probs, 1)
    e_logits = (hf @ w_re + b_re).astype(jnp.float32).reshape(B * S, N_GROUPS, EXPERTS_PER_GROUP)
    sel = jnp.take_along_axis(e_logits, g_idx[:, :, None], axis=1)[:, 0]
    e_probs = jax.nn.softmax(sel, axis=-1)
    e_p, e_idx = lax.top_k(e_probs, TOP_K)
    e_p = e_p / jnp.sum(e_p, axis=-1, keepdims=True)
    weights = g_p * e_p
    expert_ids = g_idx * EXPERTS_PER_GROUP + e_idx
    combine = jnp.sum(jax.nn.one_hot(expert_ids, N_EXPERTS, dtype=jnp.float32) * weights[..., None], axis=1)
    combine = combine.reshape(B, S, N_EXPERTS).astype(h.dtype)

    def per_sequence(args):
        xs, cw = args
        a = jax.nn.silu(jnp.einsum('sd,edf->sef', xs, w_gate)) * jnp.einsum('sd,edf->sef', xs, w_up)
        return jnp.einsum('sef,efd->sd', a * cw[..., None], w_down)

    return lax.map(per_sequence, (h, combine))

def setup_inputs(seed: int = 0) -> dict:
    key = jax.random.key(seed)
    ks = jax.random.split(key, 24)
    f32 = jnp.float32

    def nrm(k, shape, fan_in, mult=1.0):
        return jax.random.normal(k, shape, f32) * (mult * fan_in ** -0.5)

    L, D = DEPTH, D_MODEL
    return {
        "x": jax.random.normal(ks[0], (BATCH, SEQ, D), f32),
        "c": jax.random.normal(ks[1], (BATCH, D), f32),
        "w_ada": nrm(ks[2], (L, D, 6 * D), D, 0.5),
        "b_ada": 0.02 * jax.random.normal(ks[3], (L, 6 * D), f32),
        "norm1_g": 1.0 + 0.02 * jax.random.normal(ks[4], (L, D), f32),
        "w_in": nrm(ks[5], (L, D, IN_COLS), D),
        "gla_w_a2": nrm(ks[6], (L, GLA_RANK, GLA_HEADS * GLA_DK), GLA_RANK),
        "gla_b_a": 0.1 * jax.random.normal(ks[7], (L, GLA_HEADS * GLA_DK), f32),
        "gla_norm_g": 1.0 + 0.02 * jax.random.normal(ks[8], (L, GLA_DV), f32),
        "hg_norm_g": 1.0 + 0.02 * jax.random.normal(ks[9], (L, HG_DV), f32),
        "hg_lb_logits": 0.1 * jax.random.normal(ks[10], (L + 1, HG_WIDTH), f32),
        "w_out": nrm(ks[11], (L, MIX_WIDTH, D), MIX_WIDTH),
        "norm2_g": 1.0 + 0.02 * jax.random.normal(ks[12], (L, D), f32),
        "w_rg": nrm(ks[13], (L, D, N_GROUPS), D),
        "b_rg": 0.01 * jax.random.normal(ks[14], (L, N_GROUPS), f32),
        "w_re": nrm(ks[15], (L, D, N_EXPERTS), D),
        "b_re": 0.01 * jax.random.normal(ks[16], (L, N_EXPERTS), f32),
        "w_exp_gate": nrm(ks[17], (L, N_EXPERTS, D, EXPERT_FF), D),
        "w_exp_up": nrm(ks[18], (L, N_EXPERTS, D, EXPERT_FF), D),
        "w_exp_down": nrm(ks[19], (L, N_EXPERTS, EXPERT_FF, D), EXPERT_FF),
        "w_ada_final": nrm(ks[20], (D, 2 * D), D, 0.5),
        "b_ada_final": 0.02 * jax.random.normal(ks[21], (2 * D,), f32),
        "norm_f_g": 1.0 + 0.02 * jax.random.normal(ks[22], (D,), f32),
    }

def reference(x, c, w_ada, b_ada, norm1_g, w_in, gla_w_a2, gla_b_a, gla_norm_g, hg_norm_g,
              hg_lb_logits, w_out, norm2_g, w_rg, b_rg, w_re, b_re, w_exp_gate, w_exp_up,
              w_exp_down, w_ada_final, b_ada_final, norm_f_g):
    dt = x.dtype
    c_act = jax.nn.silu(c)
    lb_all = jnp.cumsum(jax.nn.softmax(hg_lb_logits.astype(jnp.float32), axis=0), axis=0)
    for l in range(DEPTH):
        mod = c_act @ w_ada[l] + b_ada[l]
        sh1, sc1, gt1, sh2, sc2, gt2 = jnp.split(mod, 6, axis=-1)
        h = modulate(rmsnorm(x, norm1_g[l]), sh1, sc1, dt)
        mix = hybrid_mixer(h, w_in[l], gla_w_a2[l], gla_b_a[l], gla_norm_g[l], hg_norm_g[l],
                           lb_all[l], w_out[l])
        x = x + gt1[:, None, :] * mix
        h2 = modulate(rmsnorm(x, norm2_g[l]), sh2, sc2, dt)
        ffn = hierarchical_moe(h2, w_rg[l], b_rg[l], w_re[l], b_re[l],
                               w_exp_gate[l], w_exp_up[l], w_exp_down[l])
        x = x + gt2[:, None, :] * ffn
    mod_f = c_act @ w_ada_final + b_ada_final
    sh_f, sc_f = jnp.split(mod_f, 2, axis=-1)
    return modulate(rmsnorm(x, norm_f_g), sh_f, sc_f, dt)


_drawn_inputs = setup_inputs


def setup_inputs(seed=0):
    import zlib

    import numpy as np

    out = dict(_drawn_inputs(seed))
    spreads = {}
    factors = {'norm1_g': 5.477,
     'gla_b_a': 5.729,
     'gla_norm_g': 8.0,
     'hg_norm_g': 8.0,
     'hg_lb_logits': 4.004,
     'norm2_g': 5.421,
     'b_rg': 8.0,
     'b_re': 8.0,
     'norm_f_g': 8.839,
     'b_ada_final': 2.698}
    for name, (base, spread) in spreads.items():
        noise = np.random.default_rng([zlib.crc32(name.encode()), seed]).standard_normal(out[name].shape)
        drawn = base * np.exp(spread * noise) if base else spread * noise
        out[name] = __import__('jax').numpy.asarray(drawn.astype(out[name].dtype))
    for name, factor in factors.items():
        out[name] = (out[name] * factor).astype(out[name].dtype)
    return out
```

```python
from contextlib import ExitStack

import concourse.bass as bass
from concourse import mybir

F32 = mybir.dt.float32
BF16 = mybir.dt.bfloat16
I32 = mybir.dt.int32
U32 = mybir.dt.uint32
U8 = mybir.dt.uint8
ALU = mybir.AluOpType
ACT = mybir.ActivationFunctionType
AX = mybir.AxisListType.X

P = 128
EPS = 1e-6
C = 96
BIG = 1e30
GMIN = -40.0
LEVELS = [64, 32, 16, 8, 4]
NL = len(LEVELS)
KB = 1024
BASE = 16512


def layer_kernel(nc, x, c, w_ada, b_ada, norm1_g, w_in, gla_w_a2, gla_b_a, gla_norm_g, hg_norm_g,
                 hg_lb_logits, w_out, norm2_g, w_rg, b_rg, w_re, b_re, w_exp_gate, w_exp_up,
                 w_exp_down, w_ada_final, b_ada_final, norm_f_g, out):
    T, D = x.shape[1], x.shape[2]
    NT = T // P
    KD = D // P
    HALF = 512
    NE, FF = w_exp_gate.shape[1], w_exp_gate.shape[3]
    NG = w_rg.shape[2]
    EG = NE // NG
    FB = FF // P
    RANK = gla_w_a2.shape[1]
    NX = (2 * T) // C
    MX = (T - 1) // C
    NSLOT = (NE + NX) * C
    GLA_UNITS, HG_UNITS = 2, 4
    UNITS = GLA_UNITS + HG_UNITS
    GW = gla_norm_g.shape[1]
    GQ, GK, GV, GG, GA_COL, HQ, HF, HI, HG = 0, 256, 512, 1024, 1536, 1552, 2064, 2576, 3088

    def is_gla(u):
        return u < GLA_UNITS

    def heads(u):
        return 2 if is_gla(u) else 1

    WRING = 8
    chunks, chunk_at = [], {}
    for u in range(UNITS):
        if is_gla(u):
            cols = [("q", GQ + u * P), ("k", GK + u * P), ("g0", GG + 2 * u * P), ("g1", GG + (2 * u + 1) * P),
                    ("v0", GV + 2 * u * P), ("v1", GV + (2 * u + 1) * P)]
        else:
            h = u - GLA_UNITS
            cols = [("q", HQ + h * P), ("f", HF + h * P), ("g0", HG + h * P), ("v0", HI + h * P)]
        for name, col in cols:
            chunk_at[(u, name)] = len(chunks)
            chunks.append(col)

    jobs = []

    def k_jobs(u):
        if is_gla(u):
            names = [("q", 0), ("q", 1), ("k", 0), ("k", 1)]
            if u == 0:
                names += [("ga", 0), ("ga", 1)]
            return names + [("a", 0), ("a", 1)]
        return [("q", 0), ("q", 1), ("f", 0), ("f", 1)]

    GVT = [1 if is_gla(u) else 2 for u in range(UNITS)]

    def gv_jobs(u):
        return [("gv", i) for i in range(NT // GVT[u])]

    def ada_row_jobs(v):
        return [("row", v, 0), ("row", v, 1)]

    ADA = {"sh1": (0, 0), "sc1": (0, D), "gt1": (0, 2 * D), "sh2": (0, 3 * D), "sc2": (0, 4 * D),
           "gt2": (0, 5 * D), "shf": (1, 0), "scf": (1, D)}
    EARLY = ["sc1", "sh1"]
    UNIT_ADA = {0: "gt1", 1: "sh2", 2: "sc2"}
    LATE = ["gt2", "shf", "scf"]
    ADA_ORDER = EARLY + [UNIT_ADA[0], UNIT_ADA[1], UNIT_ADA[2]] + LATE

    def ada_jobs(v):
        return [("col", v)] if v in ("sc1", "sh1", "sh2", "sc2") else ada_row_jobs(v)

    for g in range(2):
        for k in range(KD):
            jobs.append(("xT", g, k))
    for v in EARLY:
        jobs += ada_jobs(v)
    jobs += [(0,) + j for j in k_jobs(0) + gv_jobs(0)]
    for u in range(UNITS):
        if u + 1 < UNITS:
            jobs += [(u + 1,) + j for j in k_jobs(u + 1)]
        if u in UNIT_ADA:
            jobs += ada_jobs(UNIT_ADA[u])
        jobs += [("khT", u, 0), ("khT", u, 1)]
        if u + 1 < UNITS:
            jobs += [(u + 1,) + j for j in gv_jobs(u + 1)]
        jobs += [("oT", u, h, g) for h in range(heads(u)) for g in range(2)]
    jobs += ada_jobs("gt2")
    for g in range(2):
        for t in range(4 * g, 4 * g + 4):
            jobs += [("wo", t, 0), ("wo", t, 1), ("h2T", t, 0), ("h2T", t, 1)]
        jobs.append(("lg", g))
    jobs += [("lgT",), ("rank",)]
    jobs += ada_jobs("shf") + ada_jobs("scf")
    number = {j: n for n, j in enumerate(jobs)}
    assert len(number) == len(jobs)

    steps, step_at = [], {}
    for u in range(UNITS):
        for t in range(NT):
            for h in range(heads(u)):
                step_at[(u, t, h)] = len(steps)
                steps.append((u, t, h))
    first_step = [step_at[(u, 0, 0)] for u in range(UNITS)] + [len(steps)]
    ITEMS = NL + 3

    with ExitStack() as ctx:
        def at(name, kb, shape, dt=F32):
            return nc.alloc_sbuf_tensor_at(name, shape, dt, offset=BASE + int(kb * KB))

        def sem(name):
            return ctx.enter_context(nc.semaphore(name))

        HT = at("HT", 0, [P, KD, T])
        X1 = at("X1", 0, [P, NT, D])
        OT = at("OT", 32, [P, 8, T])
        WGA = at("WGA", 60, [P, KD, RANK])
        WA2 = at("WA2", 60.5, [RANK, 2 * P])
        BCOL = at("BCOL", 61.5, [P, 4, KD])
        GCOL = at("GCOL", 61.75, [P, 2, KD])
        C8 = at("C8", 61.875, [P, KD])
        IOI = at("IOI", 40, [P, P], I32)
        IOJ = at("IOJ", 40.5, [P, P], I32)
        XOR = at("XOR", 41, [P, P], I32)
        MT1 = at("MT1", 41.5, [P, P])
        MT2 = at("MT2", 42, [P, P])
        WR = at("WR", 64, [P, WRING, KD, P])
        WOUT = at("WOUT", 64, [P, 8, D])
        Q = at("Q", 96, [P, 2, T])
        K = at("K", 104, [P, 2, T])
        FD = at("FD", 112, [P, T])
        B = at("B", 116, [P, T])
        GVB = at("GVB", 120, [P, NT, HALF])
        GVH = at("GVH", 120, [P, NT, 2 * P])
        AST = at("AST", 96, [P, 8, D])
        XT = at("XT", 96, [P, 2, D])
        H2T = at("H2T", 104, [P, KD, T])
        XR = at("XR", 136, [P, NT, D])
        XL = at("XL", 136, [P, NL, T])
        BA = at("BA", 156, [P, T])
        BB = at("BB", 160, [P, T])
        QE = at("QE", 164, [P, T])
        KH = at("KH", 168, [P, NT, P])
        KHT = at("KHT", 172, [P, T])
        O = at("O", 172, [P, 2, NT, P])
        GA = at("GA", 180, [RANK, T])
        AR = at("AR", 184, [P, 2, D])
        ACC = at("ACC", 192, [P, D])
        IDENT = at("IDENT", 196, [P, P])
        GT1B = at("GT1B", 196.5, [P, D])
        MASK = at("MASK", 200.5, [P, NL + 1, P], U8)
        GT2B = at("GT2B", 201.25, [P, D])
        RESET = at("RESET", 201.25, [P, T], U8)
        AT2 = at("AT2", 202.25, [P, 2, P])
        S = at("S", 203.25, [P, 2, P])
        SG = at("SG", 204.25, [P, HALF])
        ONESF = at("ONESF", 206.25, [P, P])
        UT = at("UT", 206.75, [P, P], BF16)
        small_at = [207.0]

        def small(name, shape, dt=F32):
            n = 1
            for s_ in shape[1:]:
                n *= s_
            h_ = at(name, small_at[0], shape, dt)
            small_at[0] += ((n * 4 + 31) // 32) * 32 / KB
            return h_

        GS1 = small("GS1", [P, KD])
        SH1 = small("SH1", [P, KD])
        GS2 = small("GS2", [P, KD])
        SH2 = small("SH2", [P, KD])
        CA = small("CA", [P, KD])
        LB = small("LB", [P, 3, HG_UNITS])
        BAN = small("BAN", [P, 2, GLA_UNITS])
        GN = small("GN", [P, 2])
        SS = small("SS", [P, 16])
        RR = small("RR", [P, 16])
        TA = small("TA", [P, 16])
        EBL = small("EBL", [P, NT])
        LBT = small("LBT", [P, 2, HG_UNITS])
        TICK = small("TICK", [P, 1])
        TOCK = small("TOCK", [P, 1])
        assert BASE + small_at[0] * KB <= nc.sbuf_usable_end
        SHF = at("SHF", 80, [P, D])
        GSF = at("GSF", 84, [P, D])
        XGT = at("XGT", 88, [P, 2, KD, C])
        YB = at("YB", 96, [P, 2, D])
        WGU = [at(f"WGU{s}", o, [P, 2, KD, FF]) for s, o in enumerate([136, 160, 32, 56])]
        WDN = [at(f"WDN{s}", o + 16, [P, FB, D]) for s, o in enumerate([136, 160, 32, 56])]
        XG = at("XG", 120, [P, 4, D])
        AF = at("AF", 184, [P, 2, D])
        SIL = at("SIL", 118, [P, 2, FB, C])
        ATT = at("ATT", 116, [P, 2, FB, C])
        WRT = at("WRT", 188, [P, KD, NG + NE])
        LGS = at("LGS", 184, [NG + NE, T])
        rt = [104.0]

        def rtmp(name, shape, dt=F32):
            n = 1
            for s_ in shape[1:]:
                n *= s_
            h_ = at(name, rt[0], shape, dt)
            rt[0] += ((n * 4 + 31) // 32) * 32 / KB
            return h_

        LG = rtmp("LG", [P, NT, NG + NE])
        EM = rtmp("EM", [P, NT, NE])
        SCR = rtmp("SCR", [P, NT, NE])
        M1 = rtmp("M1", [P, NT, NE])
        M2 = rtmp("M2", [P, NT, NE])
        MB = rtmp("MB", [P, NT * NE], BF16)
        RK = rtmp("RK", [P, NT, NE])
        TOT = rtmp("TOT", [P, NT, NE])
        PRE = rtmp("PRE", [P, NT + 1, NE])
        OHG = rtmp("OHG", [P, NT, NG])
        GD = rtmp("GD", [P, NT, NG])
        PEN = rtmp("PEN", [P, NT, NG])
        V8 = rtmp("V8", [P, 10, NT])
        NXE = rtmp("NXE", [P, NE])
        XINC = rtmp("XINC", [P, NE])
        DX = rtmp("DX", [P, NE])
        CMP = rtmp("CMP", [1, NX, NE])
        XEF = rtmp("XEF", [1, NX])
        assert rt[0] <= 120
        PR = at("PR", 95.25, [P, NE])
        EC = at("EC", 95.375, [P, NE])
        ONEB = at("ONEB", 95.5, [P, P], BF16)
        XS = at("XS", 95.75, [1, NX])
        BR = at("BR", 205.25, [P, NG + NE])
        WPAIR = at("WPAIR", 205.5, [P, 2, NT])
        SLOT = at("SLOT", 205.5625, [P, 2, NT], U32)
        TID = at("TID", 205.625, [P, NT], U32)
        IDX = at("IDX", 200.5, [C, NE + NX], U32)
        IDXC = at("IDXC", 200.75, [C, 4], U32)
        XE = at("XE", 200.8125, [1, NX], I32)
        NXI = at("NXI", 200.9375, [1, 1], I32)
        ZT = at("ZT", 43, [C, NE + NX], U32)
        YG = at("YG", 32, [P, 2, 2, D])
        OUTT = at("OUTT", 48, [P, 2, D])
        GFB = at("GFB", 88, [P, D])

        PS = ctx.enter_context(nc.psum_tensor("PS", [P, 8 * HALF], F32))
        PJ = [PS[:, i * HALF:(i + 1) * HALF] for i in range(2)]
        LV = [PS[:, (2 + 2 * i) * HALF:(4 + 2 * i) * HALF] for i in range(2)]
        OP = [PS[:, (6 + i) * HALF:(6 + i) * HALF + P] for i in range(2)]
        TP = PS[:, 0:2 * HALF].rearrange("p (b n) -> p b n", b=2)
        SQ = PS[:, 2 * HALF:4 * HALF]
        GU = [PS[:, (2 + i) * HALF:(3 + i) * HALF] for i in range(2)]
        YP = [PS[:, (4 + 2 * i) * HALF:(6 + 2 * i) * HALF] for i in range(2)]

        xn_d = nc.dram_tensor("xn_rows", [T, D], F32, kind="Internal").ap()
        tab_d = nc.dram_tensor("slot_tokens", [NSLOT, 1], U32, kind="Internal").ap()
        ys_d = nc.dram_tensor("expert_rows", [NSLOT, D], F32, kind="Internal").ap()

        x_in = [sem("x_in0"), sem("x_in1")]
        small_in = sem("small_in")
        wga_in = sem("wga_in")
        rows_in = sem("rows_in")
        gt2_row = sem("gt2_row")
        br_in = sem("br_in")
        late_rows = sem("late_rows")
        ast_in = [sem(f"ast_in{i}") for i in range(8)]
        ar_in = [sem(f"ar_in{i}") for i in range(2)]
        ar_used = sem("ar_used")
        af_in = [sem(f"af_in{i}") for i in range(2)]
        af_used = sem("af_used")
        ast_used = sem("ast_used")
        w_in_s = [sem(f"w_in{i}") for i in range(WRING)]
        ios = sem("iotas")
        consts = sem("consts")
        pj_ready = sem("pj_ready")
        pj_free = [sem("pj_free0"), sem("pj_free1")]
        ss_ready = sem("ss_ready")
        rr_ready = sem("rr_ready")
        xr_ready = sem("xr_ready")
        ca_ready = sem("ca_ready")
        acc_ready = sem("acc_ready")
        ht_raw = sem("ht_raw")
        ht_ready = sem("ht_ready")
        q_ev = sem("q_ev")
        f_ready = sem("f_ready")
        f_used = sem("f_used")
        kf_ready = sem("kf_ready")
        lf_ready = sem("lf_ready")
        b_ready = sem("b_ready")
        e_sub = sem("e_sub")
        e_exp = sem("e_exp")
        e_mul = sem("e_mul")
        lv_ready = sem("lv_ready")
        at_ready = sem("at_ready")
        o_ready = sem("o_ready")
        o_free = sem("o_free")
        silu_g = sem("silu_g")
        rr_h = sem("rr_h")
        og_ready = sem("og_ready")
        dve = sem("dve_order")
        act_o = sem("act_order")
        wout_in = sem("wout_in")
        xt_in = [sem("xt_in0"), sem("xt_in1")]
        xn_st = [sem("xn_st0"), sem("xn_st1")]
        x1_ready = sem("x1_ready")
        ss2 = sem("ss2")
        r2 = sem("r2")
        xn_ready = sem("xn_ready")
        h2_ready = sem("h2_ready")
        wrt_in = sem("wrt_in")
        lgs_ready = sem("lgs_ready")
        gd_ready = sem("gd_ready")
        eg_ready = sem("eg_ready")
        mb_ready = sem("mb_ready")
        slots_ready = sem("slots_ready")
        table_zero = sem("table_zero")
        zt_ready = sem("zt_ready")
        table_st = sem("table_st")
        idx_in = sem("idx_in")
        wexp_in = [sem(f"wexp_in{s}") for s in range(4)]
        xg_in = [sem(f"xg_in{s}") for s in range(4)]
        idxc = sem("idxc")
        t_ready = sem("t_ready")
        xgt_scaled = sem("xgt_scaled")
        xxgt_scaled = sem("xxgt_scaled")
        xgt_ready = sem("xgt_ready")
        gu_ready = sem("gu_ready")
        sil_ready = sem("sil_ready")
        att_ready = sem("att_ready")
        y_ready = sem("y_ready")
        y_ev = sem("y_ev")
        y_st = [sem("y_st0"), sem("y_st1")]
        late_ready = sem("late_ready")
        xw_in, xxg_in, xt_ready, xxgt, xgu, xsil, xatt, xy, xyev, x_done, xidx = (
            sem(n) for n in ("xw_in", "xxg_in", "xt_ready", "xxgt", "xgu", "xsil", "xatt", "xy", "xyev",
                             "x_done", "xidx"))
        extras_done = sem("extras_done")
        ys_filled = sem("ys_filled")
        yg_in = [sem(f"yg_in{s}") for s in range(2)]
        x2_ready = sem("x2_ready")
        ss3 = sem("ss3")
        r3 = sem("r3")
        out_ready = sem("out_ready")
        out_st = [sem("out_st0"), sem("out_st1")]

        x_rows = x.rearrange("a (t p) d -> p (a t) d", p=P)
        out_rows = out.rearrange("a (t p) d -> p (a t) d", p=P)
        win = w_in.rearrange("a (p k) n -> p (a k) n", k=KD)
        wo_rows = w_out.rearrange("a (v p) n -> p (a v) n", p=P)
        ada_w = [w_ada.rearrange("a (p k) n -> p (a k) n", k=KD), w_ada_final.rearrange("(p k) n -> p k n", k=KD)]
        ada_b = [b_ada, b_ada_final.rearrange("(a n) -> a n", a=1)]

        def ada_slice(v, k):
            src, col = ADA[v]
            return ada_w[src][:, k, col:col + D]

        def ada_row(v):
            src, col = ADA[v]
            return ada_b[src][:, col:col + D]

        def col_view(vec):
            return vec.rearrange("a (p k) -> p (a k)", k=KD)

        BCOL_OF = {"sc1": 0, "sh1": 1, "sh2": 2, "sc2": 3}
        block = ctx.enter_context(nc.Block())

        def pj_wait(pe, n):
            if n >= 2:
                pe.wait_ge(pj_free[n % 2], n // 2)

        @block.sync
        def _(sp):
            for g in range(2):
                sp.dma_start(XR[:, 4 * g:4 * g + 4, :], x_rows[:, 4 * g:4 * g + 4, :]).then_inc(x_in[g], 16)
            n = 0
            for v in EARLY:
                for k in range(KD):
                    if n >= 8:
                        sp.wait_ge(ast_used, n - 7)
                    sp.dma_start(AST[:, n % 8, :], ada_slice(v, k)).then_inc(ast_in[n % 8], 16)
                    n += 1
            last_use = {}
            for u in range(UNITS):
                for name in ("q", "k", "f"):
                    if (u, name) in chunk_at:
                        last_use[chunk_at[(u, name)]] = number[(u, name, 1)]
                for name in ("g0", "g1", "v0", "v1"):
                    if (u, name) in chunk_at:
                        last_use[chunk_at[(u, name)]] = number[(u,) + gv_jobs(u)[-1]]
            for n, col in enumerate(chunks):
                if n >= WRING:
                    sp.wait_ge(pj_ready, last_use[n - WRING] + 1)
                sp.dma_start(WR[:, n % WRING, :, :], win[:, :, col:col + P]).then_inc(w_in_s[n % WRING], 16)
            sp.wait_ge(pj_ready, number[(UNITS - 1,) + gv_jobs(UNITS - 1)[-1]] + 1)
            for v in range(2):
                sp.dma_start(WOUT[:, 4 * v:4 * v + 4, :], wo_rows[:, 4 * v:4 * v + 4, :]).then_inc(wout_in, 16)
            sp.wait_ge(e_mul, ITEMS * UNITS)
            for t in range(2):
                sp.dma_start(XT[:, t, :], x_rows[:, t, :]).then_inc(xt_in[t], 16)
            sp.wait_ge(pj_ready, number[("oT", UNITS - 1, 0, 1)] + 1)

            def load_expert(e, s, done):
                sp.dma_start(WGU[s][:, 0], w_exp_gate[0, bass.ds(e, 1)].rearrange("a (p k) f -> p (a k) f", k=KD)).then_inc(done, 16)
                sp.dma_start(WGU[s][:, 1], w_exp_up[0, bass.ds(e, 1)].rearrange("a (p k) f -> p (a k) f", k=KD)).then_inc(done, 16)
                sp.dma_start(WDN[s][:, :, :], w_exp_down[0, bass.ds(e, 1)].rearrange("a (j p) n -> p (a j) n", p=P)).then_inc(done, 16)

            load_expert(0, 0, wexp_in[0])
            load_expert(1, 1, wexp_in[1])
            for t in range(NT):
                sp.wait_ge(xn_ready, t + 1)
                sp.dma_start(xn_d[t * P:(t + 1) * P, :], XT[:, t % 2, :]).then_inc(xn_st[t % 2], 16)
                if t + 2 < NT:
                    sp.wait_ge(xn_st[t % 2], 16 * (t // 2 + 1))
                    sp.wait_ge(pj_ready, number[("h2T", t, 1)] + 1)
                    sp.dma_start(XT[:, t % 2, :], x_rows[:, t + 2, :]).then_inc(xt_in[t % 2], 16)
            sp.wait_ge(pj_ready, number[("wo", NT - 1, 1)] + 1)
            load_expert(2, 2, wexp_in[2])
            load_expert(3, 3, wexp_in[3])
            sp.dma_start(SHF[:, :], ada_row("shf").to_broadcast([P, D])).then_inc(late_rows, 16)
            sp.dma_start(GSF[:, :], ada_row("scf").to_broadcast([P, D])).then_inc(late_rows, 16)
            sp.dma_start(GFB[:, :], norm_f_g.rearrange("(a n) -> a n", a=1).to_broadcast([P, D])).then_inc(late_rows, 16)
            n = 0
            sp.wait_ge(pj_ready, number[("lgT",)] + 1)
            for v in ("shf", "scf"):
                for k in range(KD):
                    if n >= 2:
                        sp.wait_ge(af_used, n - 1)
                    sp.dma_start(AF[:, n % 2, :], ada_slice(v, k)).then_inc(af_in[n % 2], 16)
                    n += 1
            with sp.Fori(1, NE // 4) as it:
                for s in range(4):
                    sp.wait_ge(y_ready, 4 * it + (s - 3))
                    load_expert(4 * it + s, s, wexp_in[s])
            sp.wait_ge(y_ready, NE)
            sp.wait_ge(slots_ready, 1)
            nx = sp.value_load(NXI[:, :], min_val=0, max_val=NX)
            with sp.If(nx > 0):
                sp.sem_inc(x_done, 16)
                with sp.Fori(0, NX) as i:
                    with sp.If(nx > i):
                        sp.wait_ge(x_done, 16 * i + 16)
                        e = sp.value_load(XE[:, bass.ds(i, 1)], min_val=0, max_val=NE - 1)
                        load_expert(e, 0, xw_in)
                sp.nop()
            for t in range(NT):
                sp.wait_ge(out_ready, t + 1)
                sp.dma_start(out_rows[:, t, :], OUTT[:, t % 2, :]).then_inc(out_st[t % 2], 16)
            for s in range(2):
                sp.wait_ge(out_st[s], 16 * NT // 2)

        @block.gpsimd
        def _(pool):
            nc.gpsimd.memset(IDENT[:], 0.0).then_inc(ios, 1)
            nc.gpsimd.memset(ONESF[:], 1.0).then_inc(ios, 1)
            nc.gpsimd.memset(ZT[:], 0).then_inc(zt_ready, 1)
            pool.iota(IOI[:], [[1, P]], base=0, channel_multiplier=0).then_inc(ios, 1)
            pool.iota(IOJ[:], [[0, P]], base=0, channel_multiplier=1).then_inc(ios, 1)
            pool.wait_ge(ios, 4)
            nc.gpsimd.affine_select(out=IDENT[:], in_=IDENT[:], compare_op=ALU.not_equal, fill=1.0, base=0,
                                    pattern=[[-1, P]], channel_multiplier=1).then_inc(ios, 1)
            pool.wait_ge(zt_ready, 1)
            pool.dma_start(tab_d.rearrange("(p n) a -> p (n a)", p=C), ZT[:]).then_inc(table_zero, 16)
            pool.dma_start(GT1B[:, :], ada_row("gt1").to_broadcast([P, D])).then_inc(rows_in, 16)
            for r in range(0, NX * C, T):
                rows = min(T, NX * C - r)
                pool.dma_start(ys_d[NE * C + r:NE * C + r + rows, :], x[0, 0:rows, :]).then_inc(ys_filled, 16)
            n = 0
            for v in [UNIT_ADA[u] for u in range(3)] + ["gt2"]:
                for k in range(KD):
                    if n >= 2:
                        pool.wait_ge(ar_used, n - 1)
                    pool.dma_start(AR[:, n % 2, :], ada_slice(v, k)).then_inc(ar_in[n % 2], 16)
                    n += 1
            pool.wait_ge(og_ready, UNITS)
            pool.dma_start(GT2B[:, :], ada_row("gt2").to_broadcast([P, D])).then_inc(gt2_row, 16)
            pool.dma_start(BR[:, 0:NG], b_rg.to_broadcast([P, NG])).then_inc(br_in, 16)
            pool.dma_start(BR[:, NG:], b_re.to_broadcast([P, NE])).then_inc(br_in, 16)
            pool.iota(TID[:], [[P, NT]], base=0, channel_multiplier=1).then_inc(ios, 1)
            pool.wait_ge(pj_ready, number[("wo", NT - 1, 1)] + 1)
            pool.iota(PR[:], [[-1, NE]], base=NE, channel_multiplier=0,
                      allow_small_or_imprecise_dtypes=True).then_inc(ios, 1)
            pool.iota(EC[:], [[C, NE]], base=0, channel_multiplier=0,
                      allow_small_or_imprecise_dtypes=True).then_inc(ios, 1)
            pool.iota(XS[:], [[1, NX]], base=0, channel_multiplier=0,
                      allow_small_or_imprecise_dtypes=True).then_inc(ios, 1)
            nc.gpsimd.memset(ONEB[:], 1.0).then_inc(ios, 1)
            pool.wait_ge(slots_ready, 1)
            pool.wait_ge(table_zero, 16)
            pool.wait_ge(ios, 10)
            for k in range(2):
                for t in range(NT):
                    pool.indirect_dma_start(
                        out=tab_d, out_offset=bass.IndirectOffsetOnAxis(ap=SLOT[:, k, t:t + 1], axis=0),
                        in_=TID[:, t:t + 1], in_offset=None).then_inc(table_st, 16)
            pool.wait_ge(table_st, 16 * 2 * NT)
            with nc.allow_non_contiguous_dma(reason="one index a slot"):
                pool.dma_start(IDX[:, :], tab_d.rearrange("(s c) a -> c (s a)", c=C)).then_inc(idx_in, 16)
            pool.wait_ge(idx_in, 16)
            for s in range(2):
                pool.wait_ge(xn_st[s], 16 * NT // 2)

            def gather(it, s, first):
                if not first:
                    pool.wait_ge(t_ready, 4 * it + (s - 3))
                nc.gpsimd.tensor_copy(IDXC[:, s:s + 1], IDX[:, bass.ds(4 * it + s, 1)]).then_inc(idxc, 1)
                pool.wait_ge(idxc, 4 * it + (s + 1))
                nc.gpsimd.tensor_tensor(TICK[:], IDENT[:, 0:1], IDENT[:, 0:1], ALU.add)
                pool.indirect_dma_start(
                    out=XG[0:C, s, :], out_offset=None, in_=xn_d,
                    in_offset=bass.IndirectOffsetOnAxis(ap=IDXC[:, s:s + 1], axis=0)).then_inc(xg_in[s], 16)

            for s in range(4):
                gather(0, s, True)
            with pool.Fori(1, NE // 4) as it:
                for s in range(4):
                    gather(it, s, False)
            pool.wait_ge(t_ready, NE)
            nx = pool.value_load(NXI[:, :], min_val=0, max_val=NX)
            with pool.If(nx > 0):
                with pool.Fori(0, NX) as i:
                    with pool.If(nx > i):
                        pool.wait_ge(x_done, 16 * i + 16)
                        nc.gpsimd.tensor_copy(IDXC[:, 0:1], IDX[:, bass.ds(i + NE, 1)]).then_inc(xidx, 1)
                        pool.wait_ge(xidx, i + 1)
                        nc.gpsimd.tensor_tensor(TICK[:], IDENT[:, 0:1], IDENT[:, 0:1], ALU.add)
                        pool.indirect_dma_start(
                            out=XG[0:C, 0, :], out_offset=None, in_=xn_d,
                            in_offset=bass.IndirectOffsetOnAxis(ap=IDXC[:, 0:1], axis=0)).then_inc(xxg_in, 16)
                pool.nop()
            for s in range(2):
                pool.wait_ge(y_st[s], 16 * NE // 2)
            pool.wait_ge(extras_done, 1)
            pool.wait_ge(ys_filled, 16 * ((NX * C + T - 1) // T))
            for t in range(NT):
                if t >= 2:
                    pool.wait_ge(x2_ready, t - 1)
                for k in range(2):
                    pool.indirect_dma_start(
                        out=YG[:, t % 2, k, :], out_offset=None, in_=ys_d,
                        in_offset=bass.IndirectOffsetOnAxis(ap=SLOT[:, k, t:t + 1], axis=0)).then_inc(yg_in[t % 2], 16)

        @block.scalar
        def _(act):
            A = nc.scalar.activation
            act.dma_start(C8[:], col_view(c)).then_inc(small_in, 16)
            for v, i in BCOL_OF.items():
                act.dma_start(BCOL[:, i, :], col_view(ada_row(v))).then_inc(small_in, 16)
            act.dma_start(GCOL[:, 0, :], col_view(norm1_g)).then_inc(small_in, 16)
            act.dma_start(GCOL[:, 1, :], col_view(norm2_g)).then_inc(small_in, 16)
            with nc.allow_non_contiguous_dma(reason="short vectors"):
                act.dma_start(LBT[:, :, :], hg_lb_logits.rearrange("r (h p) -> p r h", p=P)).then_inc(small_in, 16)
                act.dma_start(BAN[:, 0, :], gla_b_a.rearrange("a (u p) -> p (a u)", p=P)).then_inc(small_in, 16)
                act.dma_start(GN[:, 0:1], gla_norm_g.rearrange("a p -> p a")).then_inc(small_in, 16)
                act.dma_start(GN[:, 1:2], hg_norm_g.rearrange("a p -> p a")).then_inc(small_in, 16)
                act.dma_start(WGA[:], win[:, :, GA_COL:GA_COL + RANK]).then_inc(wga_in, 16)
            act.dma_start(WA2[:], gla_w_a2[0]).then_inc(wga_in, 16)
            act.wait_ge(small_in, 16 * 11)
            A(CA[:], C8[:], ACT.Silu).then_inc(ca_ready, 1)
            for t in range(NT):
                if t % 4 == 0:
                    act.wait_ge(x_in[t // 4], 16)
                if t:
                    act.wait_ge(ss_ready, t)
                A(SQ, XR[:, t, :], ACT.Square, accum_out=SS[:, t:t + 1]).then_inc(ss_ready, 1)
            act.wait_ge(ss_ready, NT)

            act_n = [0]

            def chain(ins):
                act_n[0] += 1
                ins.then_inc(act_o, 1)
                act.wait_ge(act_o, act_n[0])

            def rsqrt_of(n, width):
                chain(A(TA[:, 0:n], SS[:, 0:n], ACT.Copy, scale=1.0 / width, bias=EPS))
                chain(A(RR[:, 0:n], TA[:, 0:n], ACT.Ln))
                return A(RR[:, 0:n], RR[:, 0:n], ACT.Exp, scale=-0.5)

            rsqrt_of(NT, D).then_inc(rr_ready, 1)
            act.wait_ge(consts, 1)
            A(LBT[:], LBT[:], ACT.Exp).then_inc(lf_ready, 1)
            act.wait_ge(table_zero, 16)

            def evac(job):
                n = number[job]
                act.wait_ge(pj_ready, n + 1)
                return pj_free[n % 2]

            for g in range(2):
                for k in range(KD):
                    f = evac(("xT", g, k))
                    A(HT[:, k, g * HALF:(g + 1) * HALF], PJ[number[("xT", g, k)] % 2], ACT.Copy).then_inc(f, 1)

            def item(u, i):
                if i == NL + 1:
                    act.wait_ge(b_ready, u + 1)
                else:
                    act.wait_ge(e_sub, (ITEMS - 1) * u + min(i, NL + 1) + 1)
                if i < NL:
                    A(XL[:, i, :], XL[:, i, :], ACT.Exp).then_inc(e_exp, 1)
                elif i == NL:
                    chain(A(BB[:], BA[:], ACT.Exp, scale=-1.0))
                    A(BA[:], BA[:], ACT.Exp).then_inc(e_exp, 1)
                elif i == NL + 1:
                    A(QE[:], B[:], ACT.Exp).then_inc(e_exp, 1)
                else:
                    chain(A(EBL[:], B[:, P - 1::P], ACT.Exp))
                    A(KHT[:], KHT[:], ACT.Exp).then_inc(e_exp, 1)

            def k_evac(u, name, half):
                hs = slice(half * HALF, (half + 1) * HALF)
                f = evac((u, name, half))
                src = PJ[number[(u, name, half)] % 2]
                if u >= 2 and name in "qk":
                    act.wait_ge(e_mul, ITEMS * (u - 1))
                if name == "q":
                    dk = P // heads(u)
                    A(Q[:, u % 2, hs], src, ACT.Copy, scale=float(dk) ** -0.5).then_inc(f, 1)
                elif name == "k":
                    A(K[:, u % 2, hs], src, ACT.Copy).then_inc(f, 1)
                elif name == "ga":
                    A(GA[:, hs], src[0:RANK, :], ACT.Copy).then_inc(f, 1)
                elif name == "f":
                    if u > 0:
                        act.wait_ge(b_ready, u)
                    chain(A(FD[:, hs], src, ACT.Sigmoid))
                    act.sem_inc(f, 1)
                    act.sem_inc(f_ready, 1)
                else:
                    if u > 0:
                        act.wait_ge(b_ready, u)
                    if 2 * u + half > 0:
                        act.wait_ge(f_used, 2 * u + half)
                    chain(A(SG[:], src, ACT.Abs, bias=BAN[:, 0, u:u + 1]))
                    chain(A(FD[:, hs], src, ACT.Relu, scale=-1.0, bias=BAN[:, 1, u:u + 1]))
                    act.sem_inc(f, 1)
                    chain(A(SG[:], SG[:], ACT.Exp, scale=-1.0))
                    chain(A(SG[:], SG[:], ACT.Ln, bias=1.0))
                    act.sem_inc(f_ready, 1)

            def log_f(u):
                if not is_gla(u):
                    h = u - GLA_UNITS
                    act.wait_ge(kf_ready, h + 1)
                    A(FD[:], FD[:], ACT.Ln, scale=LB[:, 1, h:h + 1], bias=LB[:, 0, h:h + 1]).then_inc(lf_ready, 1)

            def gv_evac(u, i):
                job = (u, "gv", i)
                f = evac(job)
                src = PJ[number[job] % 2]
                if is_gla(u):
                    A(GVB[:, i, :], src, ACT.Copy).then_inc(f, 1)
                else:
                    A(GVH[:, 2 * i:2 * i + 2, :], src.rearrange("p (t n) -> p t n", t=2), ACT.Copy).then_inc(f, 1)

            def spread(main, extra):
                done = 0
                for i, m in enumerate(main):
                    m()
                    want = len(extra) * (i + 1) // len(main)
                    while done < want:
                        extra[done]()
                        done += 1
                for e in extra[done:]:
                    e()

            for name, half in k_jobs(0):
                k_evac(0, name, half)
            log_f(0)
            its = {u: [lambda u=u, i=i: item(u, i) for i in range(ITEMS)] for u in range(UNITS)}
            spread([lambda i=i: gv_evac(0, i) for _, i in gv_jobs(0)], its[0][:NL])
            for u in range(UNITS):
                rest = its[u][NL:]
                if u + 1 < UNITS:
                    ks = k_jobs(u + 1)
                    early = [j for j in ks if j[0] in ("q", "k", "ga")]
                    spread([lambda j=j: k_evac(u + 1, *j) for j in early], rest)
                    for j in ks[len(early):]:
                        k_evac(u + 1, *j)
                    log_f(u + 1)
                else:
                    for e in rest:
                        e()
                for g in range(2):
                    f = evac(("khT", u, g))
                    A(KH[:, 4 * g:4 * g + 4, :], PJ[number[("khT", u, g)] % 2].rearrange("p (t n) -> p t n", t=4),
                      ACT.Copy).then_inc(f, 1)
                nh = heads(u)
                gates = GVB[:, :, 0:nh * P] if is_gla(u) else GVH[:, :, 0:P]
                A(gates, gates, ACT.Silu).then_inc(silu_g, 1)
                for n in range(first_step[u], first_step[u + 1]):
                    _, t, h = steps[n]
                    act.wait_ge(o_ready, n + 1)
                    A(O[:, h, t, :], OP[n % 2], ACT.Copy)
                    A(OP[n % 2], OP[n % 2], ACT.Square, accum_out=SS[:, h * NT + t:h * NT + t + 1]).then_inc(o_free, 1)
                act.wait_ge(o_free, first_step[u + 1])
                rsqrt_of(nh * NT, P).then_inc(rr_h, 1)
                if u + 1 < UNITS:
                    act.wait_ge(og_ready, u + 1)
                    spread([lambda i=i: gv_evac(u + 1, i) for _, i in gv_jobs(u + 1)], its[u + 1][:NL])
                for h in range(nh):
                    vb = 2 * u + h if is_gla(u) else 4 + u - GLA_UNITS
                    for g in range(2):
                        job = ("oT", u, h, g)
                        f = evac(job)
                        A(OT[:, vb, g * HALF:(g + 1) * HALF], PJ[number[job] % 2], ACT.Copy,
                          scale=GN[:, 0:1] if is_gla(u) else GN[:, 1:2]).then_inc(f, 1)
            act.wait_ge(ar_used, 4 * KD)
            act.dma_start(WRT[:, :, 0:NG], w_rg.rearrange("a (p k) n -> p (a k) n", k=KD)).then_inc(wrt_in, 16)
            act.dma_start(WRT[:, :, NG:], w_re.rearrange("a (p k) n -> p (a k) n", k=KD)).then_inc(wrt_in, 16)
            for t in range(NT):
                act.wait_ge(x1_ready, t + 1)
                chain(A(SQ, X1[:, t, :], ACT.Square, accum_out=SS[:, 0:1]))
                rsqrt_of(1, D).then_inc(ss2, 1)
                act.wait_ge(r2, t + 1)
                A(XT[:, t % 2, :], X1[:, t, :], ACT.Copy, scale=RR[:, 1:2]).then_inc(xn_ready, 1)
                if t % 4 == 3:
                    g = t // 4
                    f = evac(("lg", g))
                    A(LGS[:, g * HALF:(g + 1) * HALF], PJ[number[("lg", g)] % 2][0:NG + NE, :], ACT.Copy).then_inc(f, 1)
            act.wait_ge(gd_ready, 1)
            A(GD[:], GD[:], ACT.Exp).then_inc(eg_ready, 1)
            act.wait_ge(gd_ready, 2)
            A(V8[:, 4, :], V8[:, 3, :], ACT.Exp).then_inc(eg_ready, 1)

            def store(m, par, row):
                act.wait_ge(y_ev, m + 1)
                act.dma_start(ys_d[bass.ds(row, C), :], YB[0:C, par, :]).then_inc(y_st[par], 16)

            def gates_up(it, s, first):
                n = 4 * it + s
                act.wait_ge(gu_ready, n + 1)
                if not (first and s < 2):
                    act.wait_ge(att_ready, 4 * it + (s - 1))
                A(SIL[:, s % 2], GU[s % 2][:, 0:FB * C].rearrange("p (j c) -> p j c", j=FB), ACT.Silu).then_inc(sil_ready, 1)
                if not (first and s == 0):
                    store(4 * it + (s - 1), (s + 1) % 2, (4 * it + (s - 1)) * C)

            for s in range(4):
                gates_up(0, s, True)
            with act.Fori(1, NE // 4) as it:
                for s in range(4):
                    gates_up(it, s, False)
            store(NE - 1, 1, (NE - 1) * C)
            nx = act.value_load(NXI[:, :], min_val=0, max_val=NX)
            for s in range(2):
                act.wait_ge(y_st[s], 16 * NE // 2)
            act.wait_ge(ys_filled, 16 * ((NX * C + T - 1) // T))
            with act.If(nx > 0):
                with act.Fori(0, NX) as i:
                    with act.If(nx > i):
                        act.wait_ge(xgu, i + 1)
                        A(SIL[:, 0], GU[0][:, 0:FB * C].rearrange("p (j c) -> p j c", j=FB), ACT.Silu).then_inc(xsil, 1)
                        act.wait_ge(xyev, i + 1)
                        act.dma_start(ys_d[bass.ds((i + NE) * C, C), :], YB[0:C, 0, :]).then_inc(x_done, 16)
                        act.wait_ge(x_done, 16 * i + 32)
                        A(TOCK[:], RR[:, 0:1], ACT.Copy)
                act.nop()
            act.sem_inc(extras_done, 1)
            for t in range(NT):
                act.wait_ge(x2_ready, t + 1)
                chain(A(SQ, X1[:, t, :], ACT.Square, accum_out=SS[:, 0:1]))
                rsqrt_of(1, D).then_inc(ss3, 1)
                act.wait_ge(r3, t + 1)

        @block.vector
        def _(v_):
            V = nc.vector
            cnt = [0]

            def link(ins):
                cnt[0] += 1
                ins.then_inc(dve, 1)
                v_.wait_ge(dve, cnt[0])

            def polish(n):
                r, m = RR[:, 0:n], TA[:, 0:n]
                link(V.tensor_tensor(m, m, r, ALU.mult))
                link(V.tensor_tensor(m, m, r, ALU.mult))
                link(V.tensor_scalar(m, m, -0.5, 1.5, ALU.mult, ALU.add))

            v_.wait_ge(ios, 5)
            link(V.tensor_tensor(XOR[:], IOI[:], IOJ[:], ALU.bitwise_xor))
            for l, s in enumerate(LEVELS):
                link(V.tensor_single_scalar(MT1[:], XOR[:], s, op=ALU.is_ge))
                link(V.tensor_single_scalar(MT2[:], XOR[:], 2 * s, op=ALU.is_lt))
                link(V.tensor_tensor(MASK[:, l, :], MT1[:], MT2[:], ALU.mult))
            link(V.tensor_single_scalar(MT1[:], XOR[:], 4, op=ALU.is_lt))
            link(V.tensor_tensor(MT2[:], IOI[:], IOJ[:], ALU.is_ge))
            link(V.tensor_tensor(MASK[:, NL, :], MT1[:], MT2[:], ALU.mult))
            link(V.tensor_tensor(UT[:], IOI[:], IOJ[:], ALU.is_gt))
            link(V.memset(RESET[:], 1))
            link(V.memset(RESET[:, 0::P], 0))
            link(V.memset(AT2[:], 0.0))
            v_.wait_ge(small_in, 16 * 11)
            link(V.tensor_scalar(BAN[:, 1, :], BAN[:, 0, :], -1.0, None, ALU.mult))
            link(V.tensor_tensor(LB[:, 0, :], LBT[:, 0, :], LBT[:, 1, :], ALU.max))
            link(V.tensor_tensor(LBT[:, 0, :], LBT[:, 0, :], LB[:, 0, :], ALU.subtract))
            V.tensor_tensor(LBT[:, 1, :], LBT[:, 1, :], LB[:, 0, :], ALU.subtract).then_inc(consts, 1)
            v_.wait_ge(rr_ready, 1)
            polish(NT)
            link(V.tensor_tensor(RR[:, 0:NT], RR[:, 0:NT], TA[:, 0:NT], ALU.mult))
            for t in range(NT):
                V.tensor_scalar(XR[:, t, :], XR[:, t, :], RR[:, t:t + 1], None, ALU.mult).then_inc(xr_ready, 1)
            v_.wait_ge(lf_ready, 1)
            link(V.tensor_tensor(LB[:, 1, :], LBT[:, 0, :], LBT[:, 1, :], ALU.add))
            link(V.reciprocal(LB[:, 1, :], LB[:, 1, :]))
            link(V.tensor_tensor(LB[:, 0, :], LBT[:, 0, :], LB[:, 1, :], ALU.mult))
            link(V.tensor_scalar(LB[:, 0, :], LB[:, 0, :], 4.3e-18, None, ALU.max))
            link(V.tensor_scalar(LB[:, 1, :], LB[:, 0, :], -1.0, 1.0, ALU.mult, ALU.add))
            link(V.tensor_scalar(LB[:, 2, :], LB[:, 1, :], -1.0, None, ALU.mult))
            v_.wait_ge(ca_ready, 1)

            ast_n = [0]
            ar_n = [0]
            af_n = [0]

            def accumulate(slot_of, arrived, used, count):
                for k in range(KD):
                    slot, want = arrived(count[0])
                    v_.wait_ge(slot, want)
                    w = slot_of(count[0])
                    if k == 0:
                        i = V.tensor_scalar(ACC[:], w, CA[:, 0:1], None, ALU.mult)
                    else:
                        i = V.scalar_tensor_tensor(out=ACC[:], in0=w, scalar=CA[:, k:k + 1], in1=ACC[:],
                                                   op0=ALU.mult, op1=ALU.add)
                    count[0] += 1
                    i.then_inc(used, 1)
                    v_.wait_ge(used, count[0])

            def ada_early(v):
                accumulate(lambda n: AST[:, n % 8, :], lambda n: (ast_in[n % 8], 16 * (n // 8 + 1)), ast_used, ast_n)

            def ada_unit(v):
                accumulate(lambda n: AR[:, n % 2, :], lambda n: (ar_in[n % 2], 16 * (n // 2 + 1)), ar_used, ar_n)

            def ada_final(v):
                accumulate(lambda n: AF[:, n % 2, :], lambda n: (af_in[n % 2], 16 * (n // 2 + 1)), af_used, af_n)

            def col_done(v, dst, gcol):
                n = number[("col", v)]
                v_.sem_inc(acc_ready, 1)
                v_.wait_ge(pj_ready, n + 1)
                src, b = PJ[n % 2][:, 0:KD], BCOL[:, BCOL_OF[v], :]
                if gcol is None:
                    link(V.tensor_tensor(dst, src, b, ALU.add))
                else:
                    link(V.tensor_tensor(dst, src, b, ALU.add))
                    link(V.scalar_tensor_tensor(out=dst, in0=dst, scalar=1.0, in1=gcol, op0=ALU.add, op1=ALU.mult))
                v_.sem_inc(pj_free[n % 2], 1)

            def row_done(v, dst, after=None):
                v_.sem_inc(acc_ready, 1)
                for half in range(2):
                    n = number[("row", v, half)]
                    hs = slice(half * HALF, (half + 1) * HALF)
                    v_.wait_ge(pj_ready, n + 1)
                    link(V.tensor_tensor(dst[:, hs], PJ[n % 2], dst[:, hs], ALU.add))
                    v_.sem_inc(pj_free[n % 2], 1)

            ada_early("sc1")
            col_done("sc1", GS1[:], GCOL[:, 0, :])
            ada_early("sh1")
            col_done("sh1", SH1[:], None)
            for b in range(2):
                v_.wait_ge(pj_free[b], KD)
            for k in range(KD):
                V.tensor_scalar(HT[:, k, :], HT[:, k, :], GS1[:, k:k + 1], SH1[:, k:k + 1],
                                ALU.mult, ALU.add).then_inc(ht_ready, 1)

            def level(ap, s):
                return ap.rearrange("p (c a s) -> p c a s", a=2, s=s)

            def sub(u, i):
                if i < NL:
                    s = LEVELS[i]
                    x_, b_ = level(XL[:, i, :], s), level(B[:], s)
                    nb = T // (2 * s)
                    ref = b_[:, :, 0, s - 1:s].to_broadcast([P, nb, s])
                    V.tensor_tensor(x_[:, :, 0, :], ref, b_[:, :, 0, :], ALU.subtract)
                    V.tensor_tensor(x_[:, :, 1, :], b_[:, :, 1, :], ref, ALU.subtract).then_inc(e_sub, 1)
                elif i == NL:
                    b_ = B[:].rearrange("p (c s) -> p c s", s=4)
                    V.tensor_tensor(BA[:].rearrange("p (c s) -> p c s", s=4), b_,
                                    b_[:, :, 1:2].to_broadcast([P, T // 4, 4]), ALU.subtract).then_inc(e_sub, 1)
                elif i == NL + 2:
                    b_ = B[:].rearrange("p (c s) -> p c s", s=P)
                    V.tensor_tensor(KHT[:].rearrange("p (c s) -> p c s", s=P),
                                    b_[:, :, P - 1:P].to_broadcast([P, NT, P]), b_, ALU.subtract).then_inc(e_sub, 1)

            def mul(u, i):
                v_.wait_ge(e_exp, ITEMS * u + i + 1)
                q_, k_ = Q[:, u % 2, :], K[:, u % 2, :]
                if i < NL:
                    s = LEVELS[i]
                    x_ = level(XL[:, i, :], s)
                    V.tensor_tensor(x_[:, :, 0, :], x_[:, :, 0, :], level(k_, s)[:, :, 0, :], ALU.mult)
                    V.tensor_tensor(x_[:, :, 1, :], x_[:, :, 1, :], level(q_, s)[:, :, 1, :], ALU.mult).then_inc(e_mul, 1)
                elif i == NL:
                    V.tensor_tensor(BB[:], BB[:], k_, ALU.mult)
                    V.tensor_tensor(BA[:], BA[:], q_, ALU.mult).then_inc(e_mul, 1)
                elif i == NL + 1:
                    V.tensor_tensor(QE[:], QE[:], q_, ALU.mult).then_inc(e_mul, 1)
                else:
                    V.tensor_tensor(KHT[:], KHT[:], k_, ALU.mult).then_inc(e_mul, 1)

            def decay(u):
                if is_gla(u):
                    for half in range(2):
                        hs = slice(half * HALF, (half + 1) * HALF)
                        v_.wait_ge(f_ready, 2 * u + half + 1)
                        link(V.tensor_tensor(FD[:, hs], FD[:, hs], SG[:], ALU.add))
                        v_.sem_inc(f_used, 1)
                        link(V.tensor_scalar(FD[:, hs], FD[:, hs], -1.0 / 16.0, GMIN, ALU.mult, ALU.max))
                else:
                    h = u - GLA_UNITS
                    v_.wait_ge(f_ready, 2 * u + 2)
                    V.tensor_scalar(K[:, u % 2, :], FD[:], LB[:, 2, h:h + 1], LB[:, 1, h:h + 1],
                                    ALU.mult, ALU.add).then_inc(kf_ready, 1)
                    v_.wait_ge(lf_ready, h + 2)
                V.tensor_tensor_scan(B[:], RESET[:], FD[:], 0.0, ALU.mult, ALU.add).then_inc(b_ready, 1)
                v_.wait_ge(b_ready, u + 1)

            def attention_step(n):
                u, t, h = steps[n]
                rows = slice(64 * h, 64 * h + 64) if is_gla(u) else slice(0, P)
                lv, a = LV[n % 2], AT2[:, n % 2, :]
                v_.wait_ge(lv_ready, n + 1)
                if n >= 2:
                    v_.wait_ge(o_ready, n - 1)
                for l, s in enumerate(LEVELS):
                    src = lv[:, l * P:(l + 1) * P]
                    link(V.copy_predicated(level(a, s)[:, :, 1, :], level(MASK[:, l, :], s)[:, :, 1, :],
                                           level(src, s)[:, :, 1, :]))
                last = V.copy_predicated(a, MASK[:, NL, :], lv[:, NL * P:(NL + 1) * P])
                if t < NT - 1:
                    if t >= 1:
                        v_.wait_ge(o_ready, step_at[(u, t - 1, h)] + 1)
                    st = lv[rows, (NL + 1) * P:(NL + 2) * P]
                    if t == 0:
                        last = V.tensor_copy(S[rows, 1, :], st)
                    else:
                        last = V.scalar_tensor_tensor(out=S[rows, (t + 1) % 2, :], in0=S[rows, t % 2, :],
                                                      scalar=EBL[rows, t:t + 1], in1=st, op0=ALU.mult, op1=ALU.add)
                last.then_inc(at_ready, 1)

            def o_post(u):
                nh = heads(u)
                v_.wait_ge(rr_h, u + 1)
                v_.wait_ge(silu_g, u + 1)
                polish(nh * NT)
                link(V.tensor_tensor(RR[:, 0:nh * NT], RR[:, 0:nh * NT], TA[:, 0:nh * NT], ALU.mult))
                for h in range(nh):
                    for t in range(NT):
                        gate = GVB[:, t, h * P:(h + 1) * P] if is_gla(u) else GVH[:, t, 0:P]
                        i = h * NT + t
                        last = V.scalar_tensor_tensor(out=O[:, h, t, :], in0=O[:, h, t, :], scalar=RR[:, i:i + 1],
                                                      in1=gate, op0=ALU.mult, op1=ALU.mult)
                last.then_inc(og_ready, 1)

            decay(0)
            for i in range(NL):
                sub(0, i)
            for i in range(NL):
                mul(0, i)
            for u in range(UNITS):
                sub(u, NL)
                sub(u, NL + 1)
                if u > 0:
                    v_.wait_ge(pj_ready, number[("oT", u - 1, heads(u - 1) - 1, 1)] + 1)
                sub(u, NL + 2)
                for i in range(NL, ITEMS):
                    mul(u, i)
                if u in UNIT_ADA:
                    ada_unit(UNIT_ADA[u])
                if u + 1 < UNITS:
                    decay(u + 1)
                if u in UNIT_ADA:
                    v = UNIT_ADA[u]
                    if v == "gt1":
                        v_.wait_ge(rows_in, 16)
                        row_done(v, GT1B)
                    elif v == "sh2":
                        col_done(v, SH2[:], None)
                    else:
                        col_done(v, GS2[:], GCOL[:, 1, :])
                for n in range(first_step[u], first_step[u + 1]):
                    attention_step(n)
                o_post(u)
                if u + 1 < UNITS:
                    for i in range(NL):
                        sub(u + 1, i)
                    for i in range(NL):
                        mul(u + 1, i)
            ada_unit("gt2")
            v_.wait_ge(gt2_row, 16)
            row_done("gt2", GT2B)
            for t in range(NT):
                v_.wait_ge(xt_in[t % 2], 16 * (t // 2 + 1))
                for half in range(2):
                    n = number[("wo", t, half)]
                    hs = slice(half * HALF, (half + 1) * HALF)
                    v_.wait_ge(pj_ready, n + 1)
                    link(V.tensor_tensor(X1[:, t, hs], PJ[n % 2], GT1B[:, hs], ALU.mult))
                    v_.sem_inc(pj_free[n % 2], 1)
                    i = V.tensor_tensor(X1[:, t, hs], X1[:, t, hs], XT[:, t % 2, hs], ALU.add)
                i.then_inc(x1_ready, 1)
                v_.wait_ge(ss2, t + 1)
                polish(1)
                V.tensor_tensor(RR[:, 1:2], RR[:, 0:1], TA[:, 0:1], ALU.mult).then_inc(r2, 1)
                for half in range(2):
                    n = number[("h2T", t, half)]
                    v_.wait_ge(pj_ready, n + 1)
                    dst = H2T[:, 4 * half:4 * half + 4, t * P:(t + 1) * P]
                    ks = slice(4 * half, 4 * half + 4)
                    link(V.tensor_tensor(dst, PJ[n % 2].rearrange("p (k n) -> p k n", k=4),
                                         GS2[:, ks].rearrange("p (k a) -> p k a", a=1).to_broadcast([P, 4, P]), ALU.mult))
                    v_.sem_inc(pj_free[n % 2], 1)
                    V.tensor_tensor(dst, dst, SH2[:, ks].rearrange("p (k a) -> p k a", a=1).to_broadcast([P, 4, P]),
                                    ALU.add).then_inc(h2_ready, 1)
            v_.wait_ge(ios, 10)
            v_.wait_ge(br_in, 32)
            n = number[("lgT",)]
            v_.wait_ge(pj_ready, n + 1)
            W = NG + NE

            def bc_t(ap, w):
                return ap.rearrange("p (a w) -> p a w", a=1).to_broadcast([P, NT, w])

            def bc_w(ap, w):
                return ap.rearrange("p (t a) -> p t a", a=1).to_broadcast([P, NT, w])

            link(V.tensor_tensor(LG[:], PJ[n % 2][:, 0:NT * W].rearrange("p (t w) -> p t w", t=NT),
                                 bc_t(BR[:], W), ALU.add))
            v_.sem_inc(pj_free[n % 2], 1)
            g_, e_ = LG[:, :, 0:NG], LG[:, :, NG:W]
            vm, vs, vp, vd, ve, v1, v2, vq = (V8[:, i, :] for i in range(8))
            link(V.tensor_reduce(vm, g_, AX, ALU.max))
            link(V.tensor_tensor(GD[:], g_, bc_w(vm, NG), ALU.subtract))
            link(V.scalar_tensor_tensor(out=OHG[:], in0=GD[:], scalar=0.0, in1=bc_t(PR[:, NE - NG:NE], NG),
                                        op0=ALU.is_ge, op1=ALU.mult))
            v_.sem_inc(gd_ready, 1)
            link(V.tensor_reduce(vm, OHG[:], AX, ALU.max))
            link(V.tensor_tensor(OHG[:], OHG[:], bc_w(vm, NG), ALU.is_equal))
            link(V.tensor_scalar(PEN[:], OHG[:], -1.0, BIG, ALU.add, ALU.mult))
            em4 = EM[:].rearrange("p t (g e) -> p (t g) e", g=NG)

            def bc_g(ap):
                return ap.rearrange("p t (g a) -> p (t g) a", a=1).to_broadcast([P, NT * NG, EG])

            link(V.tensor_copy(EM[:], e_))
            link(V.tensor_tensor(em4, em4, bc_g(OHG[:]), ALU.mult))
            link(V.tensor_tensor(em4, em4, bc_g(PEN[:]), ALU.add))

            def pick(mx, oh):
                link(V.tensor_reduce(mx, EM[:], AX, ALU.max))
                link(V.tensor_tensor(SCR[:], EM[:], bc_w(mx, NE), ALU.is_ge))
                link(V.tensor_tensor(SCR[:], SCR[:], bc_t(PR[:], NE), ALU.mult))
                link(V.tensor_reduce(vq, SCR[:], AX, ALU.max))
                link(V.tensor_tensor(oh, SCR[:], bc_w(vq, NE), ALU.is_equal))

            pick(v1, M1[:])
            link(V.scalar_tensor_tensor(out=EM[:], in0=M1[:], scalar=-3.0 * BIG, in1=EM[:], op0=ALU.mult, op1=ALU.add))
            pick(v2, M2[:])
            link(V.tensor_tensor(MB[:].rearrange("p (t e) -> p t e", t=NT), M1[:], M2[:], ALU.add))
            v_.sem_inc(mb_ready, 1)
            link(V.tensor_tensor(vd, v2, v1, ALU.subtract))
            v_.sem_inc(gd_ready, 1)
            v_.wait_ge(eg_ready, 2)
            link(V.tensor_reduce(vs, GD[:], AX, ALU.add))
            link(V.reciprocal(vp, vs))
            link(V.tensor_scalar(vs, ve, 1.0, None, ALU.add))
            link(V.reciprocal(vs, vs))
            link(V.tensor_tensor(WPAIR[:, 0, :], vp, vs, ALU.mult))
            link(V.tensor_tensor(WPAIR[:, 1, :], WPAIR[:, 0, :], ve, ALU.mult))
            n = number[("rank",)]
            v_.wait_ge(pj_ready, n + 1)
            half_ = NT * NE
            link(V.tensor_copy(TOT[:].rearrange("p t e -> p (t e)"), PJ[n % 2][:, half_:2 * half_]))
            link(V.memset(PRE[:, 0, :], 0.0))
            for t in range(NT):
                link(V.tensor_tensor(PRE[:, t + 1, :], PRE[:, t, :], TOT[:, t, :], ALU.add))
            link(V.tensor_tensor(RK[:].rearrange("p t e -> p (t e)"), PJ[n % 2][:, 0:half_],
                                 PRE[:, 0:NT, :].rearrange("p t e -> p (t e)"), ALU.add))
            v_.sem_inc(pj_free[n % 2], 1)
            cnt_ = PRE[:, NT, :]
            link(V.tensor_single_scalar(NXE[:], cnt_, float(C), op=ALU.is_gt))
            for m in range(2, MX + 1):
                link(V.scalar_tensor_tensor(out=NXE[:], in0=cnt_, scalar=float(C * m), in1=NXE[:],
                                            op0=ALU.is_gt, op1=ALU.add))
            link(V.memset(DX[:], 1.0))
            link(V.tensor_tensor_scan(XINC[:], DX[:], NXE[:], 0.0, ALU.mult, ALU.add))
            link(V.tensor_tensor(DX[:], XINC[:], NXE[:], ALU.subtract))
            link(V.tensor_scalar(DX[:], DX[:], float(NE - 1), float(C), ALU.add, ALU.mult))
            link(V.tensor_tensor(DX[:], DX[:], EC[:], ALU.subtract))
            link(V.tensor_single_scalar(SCR[:], RK[:], float(C), op=ALU.is_ge))
            link(V.tensor_tensor(SCR[:], SCR[:], bc_t(DX[:], NE), ALU.mult))
            link(V.tensor_tensor(SCR[:], SCR[:], RK[:], ALU.add))
            link(V.tensor_tensor(SCR[:], SCR[:], bc_t(EC[:], NE), ALU.add))
            for k, mk in enumerate((M1, M2)):
                link(V.tensor_tensor(EM[:], SCR[:], mk[:], ALU.mult))
                link(V.tensor_reduce(vq, EM[:], AX, ALU.add))
                link(V.tensor_copy(SLOT[:, k, :], vq))
            link(V.tensor_tensor(CMP[:], XINC[0:1, :].rearrange("p (a e) -> p a e", a=1).to_broadcast([1, NX, NE]),
                                 XS[:].rearrange("p (x a) -> p x a", a=1).to_broadcast([1, NX, NE]), ALU.is_le))
            link(V.tensor_reduce(XEF[:], CMP[:], AX, ALU.add))
            link(V.tensor_scalar(XE[:], XEF[:], float(NE - 1), None, ALU.min))
            V.tensor_copy(NXI[:], XINC[0:1, NE - 1:NE]).then_inc(slots_ready, 1)
            v_.wait_ge(late_rows, 48)
            ada_final("shf")
            row_done("shf", SHF)
            ada_final("scf")
            row_done("scf", GSF)
            link(V.scalar_tensor_tensor(out=GSF[:], in0=GSF[:], scalar=1.0, in1=GFB[:], op0=ALU.add, op1=ALU.mult))

            def xgt_evac(slot, scaled, count, done):
                for b in range(2):
                    dst = XGT[:, slot, 4 * b:4 * b + 4, :]
                    ks = slice(4 * b, 4 * b + 4)
                    i = V.tensor_tensor(dst, TP[:, b, 0:4 * C].rearrange("p (k n) -> p k n", k=4),
                                        GS2[:, ks].rearrange("p (k a) -> p k a", a=1).to_broadcast([P, 4, C]), ALU.mult)
                i.then_inc(scaled, 1)
                v_.wait_ge(scaled, count)
                for b in range(2):
                    dst = XGT[:, slot, 4 * b:4 * b + 4, :]
                    ks = slice(4 * b, 4 * b + 4)
                    i = V.tensor_tensor(dst, dst, SH2[:, ks].rearrange("p (k a) -> p k a", a=1).to_broadcast([P, 4, C]),
                                        ALU.add)
                i.then_inc(done, 1)

            def act_mul(par, done):
                V.tensor_tensor(ATT[:, par], SIL[:, par],
                                GU[par][:, FB * C:2 * FB * C].rearrange("p (j c) -> p j c", j=FB), ALU.mult).then_inc(done, 1)

            def y_evac(par, done):
                V.tensor_tensor(YB[0:C, par, 0:HALF], YP[par][0:C, 0:HALF], GT2B[0:C, 0:HALF], ALU.mult)
                V.tensor_tensor(YB[0:C, par, HALF:D], YP[par][0:C, HALF:D], GT2B[0:C, HALF:D], ALU.mult).then_inc(done, 1)

            def expert_step(it, s, first, last):
                n = 4 * it + s
                if not (last and s == 3):
                    v_.wait_ge(t_ready, 4 * it + (s + 2))
                    if not (first and s == 0):
                        v_.wait_ge(gu_ready, 4 * it + s)
                    xgt_evac((s + 1) % 2, xgt_scaled, 4 * it + (s + 2), xgt_ready)
                v_.wait_ge(sil_ready, 4 * it + (s + 1))
                if not (first and s < 2):
                    v_.wait_ge(y_ready, 4 * it + (s - 1))
                act_mul(s % 2, att_ready)
                if not (first and s == 0):
                    par = (s + 1) % 2
                    v_.wait_ge(y_ready, 4 * it + s)
                    if not (first and s < 3):
                        v_.wait_ge(y_st[par], 16 * (2 * it) + 16 * ((s - 1) // 2))
                    y_evac(par, y_ev)

            v_.wait_ge(t_ready, 1)
            xgt_evac(0, xgt_scaled, 1, xgt_ready)
            for s in range(4):
                expert_step(0, s, True, False)
            with v_.Fori(1, NE // 4 - 1) as it:
                for s in range(4):
                    expert_step(it, s, False, False)
            for s in range(4):
                expert_step(NE // 4 - 1, s, False, True)
            v_.wait_ge(y_ready, NE)
            v_.wait_ge(y_st[1], 16 * (NE // 2 - 1))
            y_evac(1, y_ev)
            v_.wait_ge(y_st[0], 16 * (NE // 2))
            nx = v_.value_load(NXI[:, :], min_val=0, max_val=NX)
            with v_.If(nx > 0):
                with v_.Fori(0, NX) as i:
                    with v_.If(nx > i):
                        v_.wait_ge(xt_ready, i + 1)
                        xgt_evac(0, xxgt_scaled, i + 1, xxgt)
                        v_.wait_ge(xsil, i + 1)
                        act_mul(0, xatt)
                        v_.wait_ge(xy, i + 1)
                        y_evac(0, xyev)
                v_.nop()
            for t in range(NT):
                v_.wait_ge(yg_in[t % 2], 32 * (t // 2 + 1))
                link(V.scalar_tensor_tensor(out=X1[:, t, :], in0=YG[:, t % 2, 0, :], scalar=WPAIR[:, 0, t:t + 1],
                                            in1=X1[:, t, :], op0=ALU.mult, op1=ALU.add))
                V.scalar_tensor_tensor(out=X1[:, t, :], in0=YG[:, t % 2, 1, :], scalar=WPAIR[:, 1, t:t + 1],
                                       in1=X1[:, t, :], op0=ALU.mult, op1=ALU.add).then_inc(x2_ready, 1)
                v_.wait_ge(ss3, t + 1)
                polish(1)
                link(V.tensor_tensor(RR[:, 1:2], RR[:, 0:1], TA[:, 0:1], ALU.mult))
                v_.sem_inc(r3, 1)
                if t >= 2:
                    v_.wait_ge(out_st[t % 2], 16 * (t // 2))
                link(V.scalar_tensor_tensor(out=OUTT[:, t % 2, :], in0=X1[:, t, :], scalar=RR[:, 1:2], in1=GSF[:],
                                            op0=ALU.mult, op1=ALU.mult))
                V.tensor_tensor(OUTT[:, t % 2, :], OUTT[:, t % 2, :], SHF[:], ALU.add).then_inc(out_ready, 1)

        @block.tensor
        def _(pe):
            MM, TR = nc.tensor.matmul, nc.tensor.transpose

            def begin(job):
                n = number[job]
                if n >= 2:
                    pe.wait_ge(pj_free[n % 2], n // 2)
                return PJ[n % 2]

            def evacuated(job):
                n = number[job]
                pe.wait_ge(pj_free[n % 2], n // 2 + 1)

            pe.wait_ge(ios, 5)
            for g in range(2):
                pe.wait_ge(xr_ready, 4 * g + 4)
                for k in range(KD):
                    ps = begin(("xT", g, k))
                    for t in range(4):
                        last = TR(ps[:, t * P:(t + 1) * P], XR[:, 4 * g + t, k::KD], IDENT[:])
                    last.then_inc(pj_ready, 1)

            def ada(v):
                pe.wait_ge(acc_ready, ADA_ORDER.index(v) + 1)
                if ada_jobs(v)[0][0] == "col":
                    ps = begin(("col", v))
                    for k in range(KD):
                        last = MM(ps[:, k:k + 1], ACC[:, k::KD], ONESF[:, 0:1], start=True, stop=True)
                    last.then_inc(pj_ready, 1)
                else:
                    for half in range(2):
                        ps = begin(("row", v, half))
                        MM(ps, ONESF[:], ACC[:, half * HALF:(half + 1) * HALF], start=True, stop=True).then_inc(pj_ready, 1)

            for v in EARLY:
                ada(v)

            def chunk(u, name):
                n = chunk_at[(u, name)]
                pe.wait_ge(w_in_s[n % WRING], 16 * (n // WRING + 1))
                return n % WRING

            def k_job(u, name, half):
                hs = slice(half * HALF, (half + 1) * HALF)
                if name == "a":
                    if half == 0:
                        for h in range(2):
                            evacuated((0, "ga", h))
                    ps = begin((u, name, half))
                    MM(ps, WA2[:, u * P:(u + 1) * P], GA[:, hs], start=True, stop=True).then_inc(pj_ready, 1)
                    return
                if name == "ga":
                    pe.wait_ge(wga_in, 32)
                    ps = begin((u, name, half))[0:RANK, :]
                else:
                    slot = chunk(u, name)
                    ps = begin((u, name, half))
                for k in range(KD):
                    if (u, name, half) == (0, "q", 0):
                        pe.wait_ge(ht_ready, k + 1)
                    w = WGA[:, k, :] if name == "ga" else WR[:, slot, k, :]
                    last = MM(ps, w, HT[:, k, hs], start=(k == 0), stop=(k == KD - 1))
                last.then_inc(pj_ready, 1)

            def gv_job(u, i):
                names = ["g0", "g1", "v0", "v1"] if is_gla(u) else ["g0", "v0"]
                s0 = [chunk(u, nm) for nm in names][0]
                nc_ = len(names)
                ps = begin((u, "gv", i))
                for tt in range(GVT[u]):
                    t = i * GVT[u] + tt
                    dst = ps[:, tt * nc_ * P:(tt + 1) * nc_ * P].rearrange("p (c n) -> p c n", c=nc_)
                    for k in range(KD):
                        last = MM(dst, HT[:, k, t * P:(t + 1) * P], WR[:, s0:s0 + nc_, k, :],
                                  start=(k == 0), stop=(k == KD - 1))
                last.then_inc(pj_ready, 1)

            def levels(n):
                u, t, h = steps[n]
                rows = slice(64 * h, 64 * h + 64) if is_gla(u) else slice(0, P)
                ts = slice(t * P, (t + 1) * P)
                if n >= 2:
                    pe.wait_ge(at_ready, n - 1)
                lv = LV[n % 2]
                for l in range(NL):
                    MM(lv[:, l * P:(l + 1) * P], XL[rows, l, ts], XL[rows, l, ts], start=True, stop=True)
                last = MM(lv[:, NL * P:(NL + 1) * P], BB[rows, ts], BA[rows, ts], start=True, stop=True)
                if t < NT - 1:
                    last = MM(lv[rows, (NL + 1) * P:(NL + 2) * P], KH[:, t, rows], values(u, t, h), start=True, stop=True)
                last.then_inc(lv_ready, 1)

            def values(u, t, h):
                return GVB[:, t, (2 + h) * P:(3 + h) * P] if is_gla(u) else GVH[:, t, P:2 * P]

            def output(n):
                u, t, h = steps[n]
                rows = slice(64 * h, 64 * h + 64) if is_gla(u) else slice(0, P)
                pe.wait_ge(at_ready, n + 1)
                if n >= 2:
                    pe.wait_ge(o_free, n - 1)
                last = MM(OP[n % 2], AT2[:, n % 2, :], values(u, t, h), start=True, stop=(t == 0))
                if t > 0:
                    last = MM(OP[n % 2], QE[rows, t * P:(t + 1) * P], S[rows, t % 2, :], start=False, stop=True)
                last.then_inc(o_ready, 1)

            for name, half in k_jobs(0):
                k_job(0, name, half)
            for _, i in gv_jobs(0):
                gv_job(0, i)
            for u in range(UNITS):
                if u + 1 < UNITS:
                    for name, half in k_jobs(u + 1):
                        k_job(u + 1, name, half)
                if u in UNIT_ADA:
                    ada(UNIT_ADA[u])
                pe.wait_ge(e_mul, ITEMS * (u + 1))
                for g in range(2):
                    ps = begin(("khT", u, g))
                    for t in range(4):
                        last = TR(ps[:, t * P:(t + 1) * P], KHT[:, (4 * g + t) * P:(4 * g + t + 1) * P], IDENT[:])
                    last.then_inc(pj_ready, 1)
                for g in range(2):
                    evacuated(("khT", u, g))
                for _, i in gv_jobs(u)[-2:]:
                    evacuated((u, "gv", i))
                lo, hi = first_step[u], first_step[u + 1]
                levels(lo)
                for n in range(lo + 1, hi):
                    levels(n)
                    output(n - 1)
                output(hi - 1)
                if u + 1 < UNITS:
                    for _, i in gv_jobs(u + 1):
                        gv_job(u + 1, i)
                pe.wait_ge(og_ready, u + 1)
                for h in range(heads(u)):
                    for g in range(2):
                        ps = begin(("oT", u, h, g))
                        for t in range(4):
                            last = TR(ps[:, t * P:(t + 1) * P], O[:, h, 4 * g + t, :], IDENT[:])
                        last.then_inc(pj_ready, 1)
            ada("gt2")
            for g in range(2):
                evacuated(("oT", UNITS - 1, 0, g))
            pe.wait_ge(wout_in, 32)

            def transpose_xn(t):
                pe.wait_ge(xn_ready, t + 1)
                for half in range(2):
                    ps = begin(("h2T", t, half))
                    for k in range(4):
                        last = TR(ps[:, k * P:(k + 1) * P], XT[:, t % 2, 4 * half + k::KD], IDENT[:])
                    last.then_inc(pj_ready, 1)

            for g in range(2):
                for t in range(4 * g, 4 * g + 4):
                    for half in range(2):
                        ps = begin(("wo", t, half))
                        for v in range(8):
                            last = MM(ps, OT[:, v, t * P:(t + 1) * P], WOUT[:, v, half * HALF:(half + 1) * HALF],
                                      start=(v == 0), stop=(v == 7))
                        last.then_inc(pj_ready, 1)
                    transpose_xn(t)
                pe.wait_ge(h2_ready, 8 * (g + 1))
                pe.wait_ge(wrt_in, 32)
                ps = begin(("lg", g))
                for k in range(KD):
                    last = MM(ps[0:NG + NE, :], WRT[:, k, :], H2T[:, k, g * HALF:(g + 1) * HALF],
                              start=(k == 0), stop=(k == KD - 1))
                last.then_inc(pj_ready, 1)
            for g in range(2):
                evacuated(("lg", g))
            ps = begin(("lgT",))
            W = NG + NE
            for t in range(NT):
                last = TR(ps[:, t * W:(t + 1) * W], LGS[:, t * P:(t + 1) * P], IDENT[0:W, 0:W])
            last.then_inc(pj_ready, 1)
            pe.wait_ge(mb_ready, 1)
            ps = begin(("rank",))
            MM(ps[:, 0:NT * NE], UT[:], MB[:], start=True, stop=True)
            MM(ps[:, NT * NE:2 * NT * NE], ONEB[:], MB[:], start=True, stop=True).then_inc(pj_ready, 1)
            ada("shf")
            ada("scf")
            evacuated(("row", "scf", 1))
            evacuated(("row", "scf", 0))

            def xg_transposes(slot, done):
                for k in range(KD):
                    last = TR(TP[:, k // 4, (k % 4) * C:(k % 4 + 1) * C], XG[0:C, slot, k::KD], IDENT[0:C, 0:C])
                last.then_inc(done, 1)

            def gate_up(par, slot, done):
                for m in range(2):
                    for j in range(FB):
                        col = (m * FB + j) * C
                        for k in range(KD):
                            last = MM(GU[par][:, col:col + C], WGU[slot][:, m, k, j * P:(j + 1) * P],
                                      XGT[:, par, k, :], start=(k == 0), stop=(k == KD - 1))
                last.then_inc(done, 1)

            def down(par, slot, done):
                for half in range(2):
                    for j in range(FB):
                        last = MM(YP[par][0:C, half * HALF:(half + 1) * HALF], ATT[:, par, j, :],
                                  WDN[slot][:, j, half * HALF:(half + 1) * HALF], start=(j == 0), stop=(j == FB - 1))
                last.then_inc(done, 1)

            def expert_step(it, s, first, last):
                if not (last and s == 3):
                    pe.wait_ge(xg_in[(s + 1) % 4], 16 * it + 16 * ((s + 1) // 4 + 1))
                    pe.wait_ge(xgt_ready, 4 * it + (s + 1))
                    xg_transposes((s + 1) % 4, t_ready)
                pe.wait_ge(wexp_in[s], 48 * it + 48)
                pe.wait_ge(xgt_ready, 4 * it + (s + 1))
                if not (first and s < 2):
                    pe.wait_ge(att_ready, 4 * it + (s - 1))
                gate_up(s % 2, s, gu_ready)
                if not (first and s == 0):
                    pe.wait_ge(att_ready, 4 * it + s)
                    if not (first and s < 3):
                        pe.wait_ge(y_ev, 4 * it + (s - 2))
                    down((s + 1) % 2, (s + 3) % 4, y_ready)

            pe.wait_ge(xg_in[0], 16)
            xg_transposes(0, t_ready)
            for s in range(4):
                expert_step(0, s, True, False)
            with pe.Fori(1, NE // 4 - 1) as it:
                for s in range(4):
                    expert_step(it, s, False, False)
            for s in range(4):
                expert_step(NE // 4 - 1, s, False, True)
            pe.wait_ge(att_ready, NE)
            pe.wait_ge(y_ev, NE - 2)
            down(1, 3, y_ready)
            nx = pe.value_load(NXI[:, :], min_val=0, max_val=NX)
            with pe.If(nx > 0):
                with pe.Fori(0, NX) as i:
                    with pe.If(nx > i):
                        pe.wait_ge(xxg_in, 16 * i + 16)
                        xg_transposes(0, xt_ready)
                        pe.wait_ge(xw_in, 48 * i + 48)
                        pe.wait_ge(xxgt, i + 1)
                        gate_up(0, 0, xgu)
                        pe.wait_ge(xatt, i + 1)
                        down(0, 0, xy)
                pe.nop()


_INS = ["x", "c", "w_ada", "b_ada", "norm1_g", "w_in", "gla_w_a2", "gla_b_a", "gla_norm_g", "hg_norm_g",
        "hg_lb_logits", "w_out", "norm2_g", "w_rg", "b_rg", "w_re", "b_re", "w_exp_gate", "w_exp_up",
        "w_exp_down", "w_ada_final", "b_ada_final", "norm_f_g"]


def kernel(**inputs):
    import numpy as np
    import concourse.bacc as bacc
    from concourse.bass_utils import run_bass_kernel_spmd

    nc = bacc.Bacc("TRN2", target_bir_lowering=False, num_devices=1)
    arrays, args = {}, []
    for name in _INS:
        a = np.ascontiguousarray(inputs[name])
        arrays[f"in_{name}"] = a
        args.append(nc.dram_tensor(f"in_{name}", a.shape, mybir.dt.from_np(a.dtype), kind="ExternalInput").ap())
    shape = np.asarray(inputs["x"]).shape
    args.append(nc.dram_tensor("out_x", shape, F32, kind="ExternalOutput").ap())
    layer_kernel(nc, *args)
    r = run_bass_kernel_spmd(nc, [arrays], core_ids=[0])
    return r.results[0]["out_x"]
```

```python
from contextlib import ExitStack

import concourse.bass as bass
from concourse import mybir

F32 = mybir.dt.float32
BF16 = mybir.dt.bfloat16
I32 = mybir.dt.int32
U32 = mybir.dt.uint32
U8 = mybir.dt.uint8
ALU = mybir.AluOpType
ACT = mybir.ActivationFunctionType
AX = mybir.AxisListType.X

P = 128
EPS = 1e-6
C = 96
BIG = 1e30
GMIN = -40.0
LEVELS = [64, 32, 16, 8, 4]
NL = len(LEVELS)
KB = 1024
BASE = 16512


def layer_kernel(nc, x, c, w_ada, b_ada, norm1_g, w_in, gla_w_a2, gla_b_a, gla_norm_g, hg_norm_g,
                 hg_lb_logits, w_out, norm2_g, w_rg, b_rg, w_re, b_re, w_exp_gate, w_exp_up,
                 w_exp_down, w_ada_final, b_ada_final, norm_f_g, out):
    T, D = x.shape[1], x.shape[2]
    NT = T // P
    KD = D // P
    HALF = 512
    NE, FF = w_exp_gate.shape[1], w_exp_gate.shape[3]
    NG = w_rg.shape[2]
    EG = NE // NG
    FB = FF // P
    RANK = gla_w_a2.shape[1]
    NX = (2 * T) // C
    MX = (T - 1) // C
    NSLOT = (NE + NX) * C
    GLA_UNITS, HG_UNITS = 2, 4
    UNITS = GLA_UNITS + HG_UNITS
    GW = gla_norm_g.shape[1]
    GQ, GK, GV, GG, GA_COL, HQ, HF, HI, HG = 0, 256, 512, 1024, 1536, 1552, 2064, 2576, 3088

    def is_gla(u):
        return u < GLA_UNITS

    def heads(u):
        return 2 if is_gla(u) else 1

    WRING = 8
    chunks, chunk_at = [], {}
    for u in range(UNITS):
        if is_gla(u):
            cols = [("q", GQ + u * P), ("k", GK + u * P), ("g0", GG + 2 * u * P), ("g1", GG + (2 * u + 1) * P),
                    ("v0", GV + 2 * u * P), ("v1", GV + (2 * u + 1) * P)]
        else:
            h = u - GLA_UNITS
            cols = [("q", HQ + h * P), ("f", HF + h * P), ("g0", HG + h * P), ("v0", HI + h * P)]
        for name, col in cols:
            chunk_at[(u, name)] = len(chunks)
            chunks.append(col)

    jobs = []

    def k_jobs(u):
        if is_gla(u):
            if u == 0:
                return [("q", 0), ("k", 0), ("ga", 0), ("q", 1), ("k", 1), ("ga", 1), ("a", 0), ("a", 1)]
            return [("q", 0), ("q", 1), ("k", 0), ("k", 1), ("a", 0), ("a", 1)]
        return [("q", 0), ("q", 1), ("f", 0), ("f", 1)]

    GVT = [1 if is_gla(u) else 2 for u in range(UNITS)]

    def gv_jobs(u):
        return [("gv", i) for i in range(NT // GVT[u])]

    ADA = {"sh1": (0, 0), "sc1": (0, D), "gt1": (0, 2 * D), "sh2": (0, 3 * D), "sc2": (0, 4 * D),
           "gt2": (0, 5 * D), "shf": (1, 0), "scf": (1, D)}
    EARLY = ["sc1", "sh1"]
    UNIT_ADA = ["gt1", "sh2", "sc2", "gt2", "shf", "scf"]

    def row_jobs(v):
        return [("row", v, 0), ("row", v, 1)]

    out_order = []
    for t in range(NT):
        out_order.append(("wo", t))
        if t == NT // 2 + 1:
            out_order.append(("lg", 0))
        if t >= 1:
            out_order.append(("h2T", t - 1))
    out_order += [("h2T", NT - 1), ("lg", 1)]

    jobs += [("col", v) for v in EARLY]
    for g in range(2):
        jobs += [("xT", g, k) for k in range(KD)]
        jobs += [(0,) + j for j in (k_jobs(0)[0:3] if g == 0 else k_jobs(0)[3:])]
    jobs += [(0,) + j for j in gv_jobs(0)]
    for u in range(UNITS):
        if u + 1 < UNITS:
            jobs += [(u + 1,) + j for j in k_jobs(u + 1)]
        jobs += [("khT", u, 0), ("khT", u, 1)]
        jobs.append(("col", UNIT_ADA[u]))
        if u + 1 < UNITS:
            jobs += [(u + 1,) + j for j in gv_jobs(u + 1)]
        jobs += [("oT", u, h, g) for h in range(heads(u)) for g in range(2)]
    jobs += row_jobs("gt1")
    for kind, i in out_order:
        jobs += [("lg", i)] if kind == "lg" else [(kind, i, 0), (kind, i, 1)]
    jobs += [("lgT",), ("rank",)] + row_jobs("gt2") + row_jobs("shf") + row_jobs("scf")
    number = {j: n for n, j in enumerate(jobs)}
    assert len(number) == len(jobs)

    steps, step_at = [], {}
    for u in range(UNITS):
        for t in range(NT):
            for h in range(heads(u)):
                step_at[(u, t, h)] = len(steps)
                steps.append((u, t, h))
    first_step = [step_at[(u, 0, 0)] for u in range(UNITS)] + [len(steps)]
    ITEMS = NL + 3

    with ExitStack() as ctx:
        def at(name, kb, shape, dt=F32):
            return nc.alloc_sbuf_tensor_at(name, shape, dt, offset=BASE + int(kb * KB))

        def sem(name):
            return ctx.enter_context(nc.semaphore(name))

        HT = at("HT", 0, [P, KD, T])
        X1 = at("X1", 0, [P, NT, D])
        OT = at("OT", 32, [P, 8, T])
        WGA = at("WGA", 60, [P, KD, RANK])
        WA2 = at("WA2", 60.5, [RANK, 2 * P])
        BCOL = at("BCOL", 61.5, [P, len(ADA), KD])
        GCOL = at("GCOL", 61.75, [P, 3, KD])
        C8 = at("C8", 61.875, [P, KD])
        IOI = at("IOI", 40, [P, P], I32)
        IOJ = at("IOJ", 40.5, [P, P], I32)
        XOR = at("XOR", 41, [P, P], I32)
        MT1 = at("MT1", 41.5, [P, P])
        MT2 = at("MT2", 42, [P, P])
        WR = at("WR", 64, [P, WRING, KD, P])
        WOUT = at("WOUT", 64, [P, 8, D])
        Q = at("Q", 96, [P, 2, T])
        K = at("K", 104, [P, 2, T])
        FD = at("FD", 112, [P, T])
        B = at("B", 116, [P, T])
        GVB = at("GVB", 120, [P, NT, HALF])
        GVH = at("GVH", 120, [P, NT, 2 * P])
        AST = at("AST", 96, [P, 8, D])
        XT = at("XT", 96, [P, 2, D])
        H2T = at("H2T", 104, [P, KD, T])
        XR = at("XR", 136, [P, NT, D])
        XL = at("XL", 136, [P, NL, T])
        BA = at("BA", 156, [P, T])
        BB = at("BB", 160, [P, T])
        QE = at("QE", 164, [P, T])
        KH = at("KH", 168, [P, NT, P])
        KHT = at("KHT", 172, [P, T])
        O = at("O", 172, [P, 2, NT, P])
        GA = at("GA", 180, [RANK, T])
        AR = at("AR", 184, [P, 2, D])
        ACC = at("ACC", 192, [P, D])
        IDENT = at("IDENT", 196, [P, P])
        ACCB = at("ACCB", 180, [P, D])
        GT1B = at("GT1B", 196.5, [P, D])
        MASK = at("MASK", 200.5, [P, NL + 1, P], U8)
        GT2B = at("GT2B", 201.25, [P, D])
        RESET = at("RESET", 201.25, [P, T], U8)
        AT2 = at("AT2", 202.25, [P, 2, P])
        S = at("S", 203.25, [P, 2, P])
        SG = at("SG", 204.25, [P, HALF])
        ONESF = at("ONESF", 206.25, [P, P])
        UT = at("UT", 206.75, [P, P], BF16)
        small_at = [207.0]

        def small(name, shape, dt=F32):
            n = 1
            for s_ in shape[1:]:
                n *= s_
            h_ = at(name, small_at[0], shape, dt)
            small_at[0] += ((n * 4 + 31) // 32) * 32 / KB
            return h_

        GS1 = small("GS1", [P, KD])
        SH1 = small("SH1", [P, KD])
        GS2 = small("GS2", [P, KD])
        SH2 = small("SH2", [P, KD])
        GT1 = small("GT1", [P, KD])
        GT2 = small("GT2", [P, KD])
        SHC = small("SHC", [P, KD])
        GSC = small("GSC", [P, KD])
        CA = small("CA", [P, KD])
        LB = small("LB", [P, 3, HG_UNITS])
        BAN = small("BAN", [P, 2, GLA_UNITS])
        GN = small("GN", [P, 2])
        SS = small("SS", [P, 16])
        RR = small("RR", [P, 16])
        TA = small("TA", [P, 16])
        EBL = small("EBL", [P, NT])
        LBT = small("LBT", [P, 2, HG_UNITS])
        TICK = small("TICK", [P, 1])
        TOCK = small("TOCK", [P, 1])
        assert BASE + small_at[0] * KB <= nc.sbuf_usable_end
        SHF = at("SHF", 80, [P, D])
        GSF = at("GSF", 84, [P, D])
        XGT = at("XGT", 88, [P, 2, KD, C])
        YB = at("YB", 96, [P, 2, D])
        WGU = [at(f"WGU{s}", o, [P, 2, KD, FF]) for s, o in enumerate([136, 160, 32, 56])]
        WDN = [at(f"WDN{s}", o + 16, [P, FB, D]) for s, o in enumerate([136, 160, 32, 56])]
        XG = at("XG", 120, [P, 4, D])
        SIL = at("SIL", 118, [P, 2, FB, C])
        ATT = at("ATT", 116, [P, 2, FB, C])
        WRT = at("WRT", 188, [P, KD, NG + NE])
        LGS = at("LGS", 184, [NG + NE, T])
        rt = [104.0]

        def rtmp(name, shape, dt=F32):
            n = 1
            for s_ in shape[1:]:
                n *= s_
            h_ = at(name, rt[0], shape, dt)
            rt[0] += ((n * 4 + 31) // 32) * 32 / KB
            return h_

        LG = rtmp("LG", [P, NT, NG + NE])
        EM = rtmp("EM", [P, NT, NE])
        SCR = rtmp("SCR", [P, NT, NE])
        M1 = rtmp("M1", [P, NT, NE])
        M2 = rtmp("M2", [P, NT, NE])
        MB = rtmp("MB", [P, NT * NE], BF16)
        RK = rtmp("RK", [P, NT, NE])
        TOT = rtmp("TOT", [P, NT, NE])
        PRE = rtmp("PRE", [P, NT + 1, NE])
        OHG = rtmp("OHG", [P, NT, NG])
        GD = rtmp("GD", [P, NT, NG])
        PEN = rtmp("PEN", [P, NT, NG])
        V8 = rtmp("V8", [P, 10, NT])
        NXE = rtmp("NXE", [P, NE])
        XINC = rtmp("XINC", [P, NE])
        DX = rtmp("DX", [P, NE])
        CMP = rtmp("CMP", [1, NX, NE])
        XEF = rtmp("XEF", [1, NX])
        assert rt[0] <= 120
        PR = at("PR", 95.25, [P, NE])
        EC = at("EC", 95.375, [P, NE])
        ONEB = at("ONEB", 95.5, [P, P], BF16)
        XS = at("XS", 95.75, [1, NX])
        BR = at("BR", 205.25, [P, NG + NE])
        WPAIR = at("WPAIR", 205.5, [P, 2, NT])
        SLOT = at("SLOT", 205.5625, [P, 2, NT], U32)
        TID = at("TID", 205.625, [P, NT], U32)
        IDX = at("IDX", 200.5, [C, NE + NX], U32)
        IDXC = at("IDXC", 200.75, [C, 4], U32)
        XE = at("XE", 200.8125, [1, NX], I32)
        NXI = at("NXI", 200.9375, [1, 1], I32)
        ZT = at("ZT", 43, [C, NE + NX], U32)
        YG = at("YG", 32, [P, 4, 2, D])
        OUTT = at("OUTT", 64, [P, 2, D])

        PS = ctx.enter_context(nc.psum_tensor("PS", [P, 8 * HALF], F32))
        PJ = [PS[:, i * HALF:(i + 1) * HALF] for i in range(2)]
        LV = [PS[:, (2 + 2 * i) * HALF:(4 + 2 * i) * HALF] for i in range(2)]
        OP = [PS[:, (6 + i) * HALF:(6 + i) * HALF + P] for i in range(2)]
        TP = PS[:, 0:2 * HALF].rearrange("p (b n) -> p b n", b=2)
        SQ = PS[:, 2 * HALF:4 * HALF]
        GU = [PS[:, (2 + i) * HALF:(3 + i) * HALF] for i in range(2)]
        YP = [PS[:, (4 + 2 * i) * HALF:(6 + 2 * i) * HALF] for i in range(2)]

        xn_d = nc.dram_tensor("xn_rows", [T, D], F32, kind="Internal").ap()
        tab_d = nc.dram_tensor("slot_tokens", [NSLOT, 1], U32, kind="Internal").ap()
        ys_d = nc.dram_tensor("expert_rows", [NSLOT, D], F32, kind="Internal").ap()

        x_in = [sem(f"x_in{i}") for i in range(NT // 2)]
        small_in = sem("small_in")
        wga_in = sem("wga_in")
        br_in = sem("br_in")
        ast_in = [sem(f"ast_in{i}") for i in range(8)]
        ar_in = [sem(f"ar_in{i}") for i in range(2)]
        ar_used = sem("ar_used")
        ast_used = sem("ast_used")
        w_in_s = [sem(f"w_in{i}") for i in range(WRING)]
        ios = sem("iotas")
        consts = sem("consts")
        pj_ready = sem("pj_ready")
        pj_free = [sem("pj_free0"), sem("pj_free1")]
        ss_ready = sem("ss_ready")
        rr_ready = sem("rr_ready")
        xr_ready = sem("xr_ready")
        ca_ready = sem("ca_ready")
        mod1_ready = sem("mod1_ready")
        f_ready = sem("f_ready")
        f_used = sem("f_used")
        kf_ready = sem("kf_ready")
        lf_ready = sem("lf_ready")
        b_ready = sem("b_ready")
        e_sub = sem("e_sub")
        e_exp = sem("e_exp")
        e_mul = sem("e_mul")
        lv_ready = sem("lv_ready")
        at_ready = sem("at_ready")
        o_ready = sem("o_ready")
        o_free = sem("o_free")
        silu_g = sem("silu_g")
        rr_h = sem("rr_h")
        og_ready = sem("og_ready")
        dve = sem("dve_order")
        act_o = sem("act_order")
        wout_in = sem("wout_in")
        xt_in = [sem("xt_in0"), sem("xt_in1")]
        xn_st = [sem("xn_st0"), sem("xn_st1")]
        x1_ready = sem("x1_ready")
        ss2 = sem("ss2")
        r2 = sem("r2")
        xn_ready = sem("xn_ready")
        h2_ready = sem("h2_ready")
        wrt_in = sem("wrt_in")
        lgs_ready = sem("lgs_ready")
        gd_ready = sem("gd_ready")
        eg_ready = sem("eg_ready")
        mb_ready = sem("mb_ready")
        slots_ready = sem("slots_ready")
        table_zero = sem("table_zero")
        zt_ready = sem("zt_ready")
        table_st = sem("table_st")
        idx_in = sem("idx_in")
        wexp_in = [sem(f"wexp_in{s}") for s in range(4)]
        xg_in = [sem(f"xg_in{s}") for s in range(4)]
        idxc = sem("idxc")
        t_ready = sem("t_ready")
        xgt_scaled = sem("xgt_scaled")
        xxgt_scaled = sem("xxgt_scaled")
        xgt_ready = sem("xgt_ready")
        gu_ready = sem("gu_ready")
        sil_ready = sem("sil_ready")
        att_ready = sem("att_ready")
        y_ready = sem("y_ready")
        y_ev = sem("y_ev")
        y_st = [sem("y_st0"), sem("y_st1")]
        late_ready = sem("late_ready")
        xw_in, xxg_in, xt_ready, xxgt, xgu, xsil, xatt, xy, xyev, x_done, xidx = (
            sem(n) for n in ("xw_in", "xxg_in", "xt_ready", "xxgt", "xgu", "xsil", "xatt", "xy", "xyev",
                             "x_done", "xidx"))
        extras_done = sem("extras_done")
        ys_filled = sem("ys_filled")
        yg_in = [sem(f"yg_in{s}") for s in range(4)]
        x2_ready = sem("x2_ready")
        ss3 = sem("ss3")
        r3 = sem("r3")
        out_ready = sem("out_ready")
        out_st = [sem("out_st0"), sem("out_st1")]

        x_rows = x.rearrange("a (t p) d -> p (a t) d", p=P)
        out_rows = out.rearrange("a (t p) d -> p (a t) d", p=P)
        win = w_in.rearrange("a (p k) n -> p (a k) n", k=KD)
        wo_rows = w_out.rearrange("a (v p) n -> p (a v) n", p=P)
        ada_w = [w_ada.rearrange("a (p k) n -> p (a k) n", k=KD), w_ada_final.rearrange("(p k) n -> p k n", k=KD)]
        ada_b = [b_ada, b_ada_final.rearrange("(a n) -> a n", a=1)]

        def ada_slice(v, k):
            src, col = ADA[v]
            return ada_w[src][:, k, col:col + D]

        def ada_row(v):
            src, col = ADA[v]
            return ada_b[src][:, col:col + D]

        def col_view(vec):
            return vec.rearrange("a (p k) -> p (a k)", k=KD)

        block = ctx.enter_context(nc.Block())

        @block.sync
        def _(sp):
            def load_x(g):
                sp.dma_start(XR[:, 2 * g:2 * g + 2, :], x_rows[:, 2 * g:2 * g + 2, :]).then_inc(x_in[g], 16)

            def load_early(v):
                for k in range(KD):
                    n = EARLY.index(v) * KD + k
                    if n >= 8:
                        sp.wait_ge(ast_used, n - 7)
                    sp.dma_start(AST[:, n % 8, :], ada_slice(v, k)).then_inc(ast_in[n % 8], 16)

            def load_chunk(n):
                sp.dma_start(WR[:, n % WRING, :, :], win[:, :, chunks[n]:chunks[n] + P]).then_inc(w_in_s[n % WRING], 16)

            load_early("sc1")
            load_x(0)
            load_early("sh1")
            load_x(1)
            for n in range(2):
                load_chunk(n)
            for g in range(2, NT // 2):
                load_x(g)
            last_use = {}
            for u in range(UNITS):
                for name in ("q", "k", "f"):
                    if (u, name) in chunk_at:
                        last_use[chunk_at[(u, name)]] = number[(u, name, 1)]
                for name in ("g0", "g1", "v0", "v1"):
                    if (u, name) in chunk_at:
                        last_use[chunk_at[(u, name)]] = number[(u,) + gv_jobs(u)[-1]]
            for n in range(2, len(chunks)):
                if n >= WRING:
                    sp.wait_ge(pj_ready, last_use[n - WRING] + 1)
                load_chunk(n)
            sp.wait_ge(pj_ready, number[(UNITS - 1,) + gv_jobs(UNITS - 1)[-1]] + 1)
            for v in range(2):
                sp.dma_start(WOUT[:, 4 * v:4 * v + 4, :], wo_rows[:, 4 * v:4 * v + 4, :]).then_inc(wout_in, 16)
            sp.wait_ge(e_mul, ITEMS * UNITS)
            for t in range(2):
                sp.dma_start(XT[:, t, :], x_rows[:, t, :]).then_inc(xt_in[t], 16)
            sp.wait_ge(pj_ready, number[("oT", UNITS - 1, 0, 1)] + 1)

            def load_expert(e, s, done):
                sp.dma_start(WGU[s][:, 0], w_exp_gate[0, bass.ds(e, 1)].rearrange("a (p k) f -> p (a k) f", k=KD)).then_inc(done, 16)
                sp.dma_start(WGU[s][:, 1], w_exp_up[0, bass.ds(e, 1)].rearrange("a (p k) f -> p (a k) f", k=KD)).then_inc(done, 16)
                sp.dma_start(WDN[s][:, :, :], w_exp_down[0, bass.ds(e, 1)].rearrange("a (j p) n -> p (a j) n", p=P)).then_inc(done, 16)

            load_expert(0, 0, wexp_in[0])
            load_expert(1, 1, wexp_in[1])
            for t in range(NT):
                sp.wait_ge(xn_ready, t + 1)
                sp.dma_start(xn_d[t * P:(t + 1) * P, :], XT[:, t % 2, :]).then_inc(xn_st[t % 2], 16)
                if t + 2 < NT:
                    sp.wait_ge(xn_st[t % 2], 16 * (t // 2 + 1))
                    sp.wait_ge(pj_ready, number[("h2T", t, 1)] + 1)
                    sp.dma_start(XT[:, t % 2, :], x_rows[:, t + 2, :]).then_inc(xt_in[t % 2], 16)
            sp.wait_ge(pj_ready, number[("wo", NT - 1, 1)] + 1)
            load_expert(2, 2, wexp_in[2])
            load_expert(3, 3, wexp_in[3])
            with sp.Fori(1, NE // 4) as it:
                for s in range(4):
                    sp.wait_ge(y_ready, 4 * it + (s - 3))
                    load_expert(4 * it + s, s, wexp_in[s])
            sp.wait_ge(y_ready, NE)
            sp.wait_ge(slots_ready, 1)
            nx = sp.value_load(NXI[:, :], min_val=0, max_val=NX)
            with sp.If(nx > 0):
                sp.sem_inc(x_done, 16)
                with sp.Fori(0, NX) as i:
                    with sp.If(nx > i):
                        sp.wait_ge(x_done, 16 * i + 16)
                        e = sp.value_load(XE[:, bass.ds(i, 1)], min_val=0, max_val=NE - 1)
                        load_expert(e, 0, xw_in)
                sp.nop()
            for t in range(NT):
                sp.wait_ge(out_ready, t + 1)
                sp.dma_start(out_rows[:, t, :], OUTT[:, t % 2, :]).then_inc(out_st[t % 2], 16)
            for s in range(2):
                sp.wait_ge(out_st[s], 16 * NT // 2)

        @block.gpsimd
        def _(pool):
            nc.gpsimd.memset(IDENT[:], 0.0).then_inc(ios, 1)
            nc.gpsimd.memset(ONESF[:], 1.0).then_inc(ios, 1)
            nc.gpsimd.memset(ZT[:], 0).then_inc(zt_ready, 1)
            pool.iota(IOI[:], [[1, P]], base=0, channel_multiplier=0).then_inc(ios, 1)
            pool.iota(IOJ[:], [[0, P]], base=0, channel_multiplier=1).then_inc(ios, 1)
            pool.wait_ge(ios, 4)
            nc.gpsimd.affine_select(out=IDENT[:], in_=IDENT[:], compare_op=ALU.not_equal, fill=1.0, base=0,
                                    pattern=[[-1, P]], channel_multiplier=1).then_inc(ios, 1)
            pool.wait_ge(zt_ready, 1)
            pool.dma_start(tab_d.rearrange("(p n) a -> p (n a)", p=C), ZT[:]).then_inc(table_zero, 16)
            n = 0
            for v in UNIT_ADA:
                for k in range(KD):
                    if n >= 2:
                        pool.wait_ge(ar_used, n - 1)
                    pool.dma_start(AR[:, n % 2, :], ada_slice(v, k)).then_inc(ar_in[n % 2], 16)
                    n += 1
                if v == UNIT_ADA[0]:
                    for r in range(0, NX * C, T):
                        rows = min(T, NX * C - r)
                        pool.dma_start(ys_d[NE * C + r:NE * C + r + rows, :], x[0, 0:rows, :]).then_inc(ys_filled, 16)
            pool.wait_ge(og_ready, UNITS)
            pool.dma_start(BR[:, 0:NG], b_rg.to_broadcast([P, NG])).then_inc(br_in, 16)
            pool.dma_start(BR[:, NG:], b_re.to_broadcast([P, NE])).then_inc(br_in, 16)
            pool.iota(TID[:], [[P, NT]], base=0, channel_multiplier=1).then_inc(ios, 1)
            pool.wait_ge(pj_ready, number[("wo", NT - 1, 1)] + 1)
            pool.iota(PR[:], [[-1, NE]], base=NE, channel_multiplier=0,
                      allow_small_or_imprecise_dtypes=True).then_inc(ios, 1)
            pool.iota(EC[:], [[C, NE]], base=0, channel_multiplier=0,
                      allow_small_or_imprecise_dtypes=True).then_inc(ios, 1)
            pool.iota(XS[:], [[1, NX]], base=0, channel_multiplier=0,
                      allow_small_or_imprecise_dtypes=True).then_inc(ios, 1)
            nc.gpsimd.memset(ONEB[:], 1.0).then_inc(ios, 1)
            pool.wait_ge(slots_ready, 1)
            pool.wait_ge(table_zero, 16)
            pool.wait_ge(ios, 9 + 1)
            for k in range(2):
                for t in range(NT):
                    pool.indirect_dma_start(
                        out=tab_d, out_offset=bass.IndirectOffsetOnAxis(ap=SLOT[:, k, t:t + 1], axis=0),
                        in_=TID[:, t:t + 1], in_offset=None).then_inc(table_st, 16)
            pool.wait_ge(table_st, 16 * 2 * NT)
            with nc.allow_non_contiguous_dma(reason="one index a slot"):
                pool.dma_start(IDX[:, :], tab_d.rearrange("(s c) a -> c (s a)", c=C)).then_inc(idx_in, 16)
            pool.wait_ge(idx_in, 16)
            for s in range(2):
                pool.wait_ge(xn_st[s], 16 * NT // 2)

            def gather(it, s, first):
                if not first:
                    pool.wait_ge(t_ready, 4 * it + (s - 3))
                nc.gpsimd.tensor_copy(IDXC[:, s:s + 1], IDX[:, bass.ds(4 * it + s, 1)]).then_inc(idxc, 1)
                pool.wait_ge(idxc, 4 * it + (s + 1))
                nc.gpsimd.tensor_tensor(TICK[:], IDENT[:, 0:1], IDENT[:, 0:1], ALU.add)
                pool.indirect_dma_start(
                    out=XG[0:C, s, :], out_offset=None, in_=xn_d,
                    in_offset=bass.IndirectOffsetOnAxis(ap=IDXC[:, s:s + 1], axis=0)).then_inc(xg_in[s], 16)

            for s in range(4):
                gather(0, s, True)
            with pool.Fori(1, NE // 4) as it:
                for s in range(4):
                    gather(it, s, False)
            pool.wait_ge(t_ready, NE)
            nx = pool.value_load(NXI[:, :], min_val=0, max_val=NX)
            with pool.If(nx > 0):
                with pool.Fori(0, NX) as i:
                    with pool.If(nx > i):
                        pool.wait_ge(x_done, 16 * i + 16)
                        nc.gpsimd.tensor_copy(IDXC[:, 0:1], IDX[:, bass.ds(i + NE, 1)]).then_inc(xidx, 1)
                        pool.wait_ge(xidx, i + 1)
                        nc.gpsimd.tensor_tensor(TICK[:], IDENT[:, 0:1], IDENT[:, 0:1], ALU.add)
                        pool.indirect_dma_start(
                            out=XG[0:C, 0, :], out_offset=None, in_=xn_d,
                            in_offset=bass.IndirectOffsetOnAxis(ap=IDXC[:, 0:1], axis=0)).then_inc(xxg_in, 16)
                pool.nop()
            for s in range(2):
                pool.wait_ge(y_st[s], 16 * NE // 2)
            pool.wait_ge(extras_done, 1)
            pool.wait_ge(ys_filled, 16 * ((NX * C + T - 1) // T))
            for t in range(NT):
                if t >= 4:
                    pool.wait_ge(x2_ready, t - 3)
                for k in range(2):
                    pool.indirect_dma_start(
                        out=YG[:, t % 4, k, :], out_offset=None, in_=ys_d,
                        in_offset=bass.IndirectOffsetOnAxis(ap=SLOT[:, k, t:t + 1], axis=0)).then_inc(yg_in[t % 4], 16)

        @block.scalar
        def _(act):
            A = nc.scalar.activation
            act.dma_start(C8[:], col_view(c)).then_inc(small_in, 16)
            act.dma_start(BCOL[:, 0:6, :], b_ada.rearrange("a (v p k) -> p (a v) k", v=6, k=KD)).then_inc(small_in, 16)
            act.dma_start(BCOL[:, 6:8, :], b_ada_final.rearrange("(v p k) -> p v k", v=2, k=KD)).then_inc(small_in, 16)
            act.dma_start(GCOL[:, 0, :], col_view(norm1_g)).then_inc(small_in, 16)
            act.dma_start(GCOL[:, 1, :], col_view(norm2_g)).then_inc(small_in, 16)
            act.dma_start(GCOL[:, 2, :], norm_f_g.rearrange("(p k) -> p k", k=KD)).then_inc(small_in, 16)
            with nc.allow_non_contiguous_dma(reason="short vectors"):
                act.dma_start(LBT[:, :, :], hg_lb_logits.rearrange("r (h p) -> p r h", p=P)).then_inc(small_in, 16)
                act.dma_start(BAN[:, 0, :], gla_b_a.rearrange("a (u p) -> p (a u)", p=P)).then_inc(small_in, 16)
                act.dma_start(GN[:, 0:1], gla_norm_g.rearrange("a p -> p a")).then_inc(small_in, 16)
                act.dma_start(GN[:, 1:2], hg_norm_g.rearrange("a p -> p a")).then_inc(small_in, 16)
                act.dma_start(WGA[:], win[:, :, GA_COL:GA_COL + RANK]).then_inc(wga_in, 16)
            act.dma_start(WA2[:], gla_w_a2[0]).then_inc(wga_in, 16)
            act.wait_ge(small_in, 16 * 10)
            A(CA[:], C8[:], ACT.Silu).then_inc(ca_ready, 1)
            act_n = [0]

            def chain(ins):
                act_n[0] += 1
                ins.then_inc(act_o, 1)
                act.wait_ge(act_o, act_n[0])

            def rsqrt_of(lo, hi, width):
                chain(A(TA[:, lo:hi], SS[:, lo:hi], ACT.Copy, scale=1.0 / width, bias=EPS))
                chain(A(RR[:, lo:hi], TA[:, lo:hi], ACT.Ln))
                return A(RR[:, lo:hi], RR[:, lo:hi], ACT.Exp, scale=-0.5)

            for g in range(2):
                for t in range(4 * g, 4 * g + 4):
                    act.wait_ge(x_in[t // 2], 16)
                    chain(A(SQ, XR[:, t, :], ACT.Square, accum_out=SS[:, t:t + 1]))
                rsqrt_of(4 * g, 4 * g + 4, D).then_inc(rr_ready, 1)
            act.wait_ge(consts, 1)
            A(LBT[:], LBT[:], ACT.Exp).then_inc(lf_ready, 1)
            act.wait_ge(table_zero, 16)

            def evac(job):
                n = number[job]
                act.wait_ge(pj_ready, n + 1)
                return pj_free[n % 2]

            act.wait_ge(mod1_ready, 2)

            def x_evac(g):
                for k in range(KD):
                    f = evac(("xT", g, k))
                    A(HT[:, k, g * HALF:(g + 1) * HALF], PJ[number[("xT", g, k)] % 2], ACT.Identity,
                      scale=GS1[:, k:k + 1], bias=SH1[:, k:k + 1]).then_inc(f, 1)

            def item(u, i):
                if i == NL + 1:
                    act.wait_ge(b_ready, u + 1)
                else:
                    act.wait_ge(e_sub, (ITEMS - 1) * u + min(i, NL + 1) + 1)
                if i < NL:
                    A(XL[:, i, :], XL[:, i, :], ACT.Exp).then_inc(e_exp, 1)
                elif i == NL:
                    chain(A(BB[:], BA[:], ACT.Exp, scale=-1.0))
                    A(BA[:], BA[:], ACT.Exp).then_inc(e_exp, 1)
                elif i == NL + 1:
                    A(QE[:], B[:], ACT.Exp).then_inc(e_exp, 1)
                else:
                    chain(A(EBL[:], B[:, P - 1::P], ACT.Exp))
                    A(KHT[:], KHT[:], ACT.Exp).then_inc(e_exp, 1)

            def k_evac(u, name, half):
                hs = slice(half * HALF, (half + 1) * HALF)
                f = evac((u, name, half))
                src = PJ[number[(u, name, half)] % 2]
                if u >= 2 and name in "qk":
                    act.wait_ge(e_mul, ITEMS * (u - 1))
                if name == "q":
                    dk = P // heads(u)
                    A(Q[:, u % 2, hs], src, ACT.Copy, scale=float(dk) ** -0.5).then_inc(f, 1)
                elif name == "k":
                    A(K[:, u % 2, hs], src, ACT.Copy).then_inc(f, 1)
                elif name == "ga":
                    A(GA[:, hs], src[0:RANK, :], ACT.Copy).then_inc(f, 1)
                elif name == "f":
                    if u > 0:
                        act.wait_ge(b_ready, u)
                    A(FD[:, hs], src, ACT.Sigmoid).then_inc(f, 1)
                else:
                    if u > 0:
                        act.wait_ge(b_ready, u)
                    if 2 * u + half > 0:
                        act.wait_ge(f_used, 2 * u + half)
                    chain(A(SG[:], src, ACT.Abs, bias=BAN[:, 0, u:u + 1]))
                    A(FD[:, hs], src, ACT.Relu, scale=-1.0, bias=BAN[:, 1, u:u + 1]).then_inc(f, 1)
                    chain(A(SG[:], SG[:], ACT.Exp, scale=-1.0))
                    A(SG[:], SG[:], ACT.Ln, bias=1.0).then_inc(f_ready, 1)

            def log_f(u):
                if not is_gla(u):
                    h = u - GLA_UNITS
                    act.wait_ge(kf_ready, h + 1)
                    A(FD[:], FD[:], ACT.Ln, scale=LB[:, 1, h:h + 1], bias=LB[:, 0, h:h + 1]).then_inc(lf_ready, 1)

            def gv_evac(u, i):
                job = (u, "gv", i)
                f = evac(job)
                src = PJ[number[job] % 2]
                if is_gla(u):
                    A(GVB[:, i, :], src, ACT.Copy).then_inc(f, 1)
                else:
                    A(GVH[:, 2 * i:2 * i + 2, :], src.rearrange("p (t n) -> p t n", t=2), ACT.Copy).then_inc(f, 1)

            def spread(main, extra):
                done = 0
                for i, m in enumerate(main):
                    m()
                    want = len(extra) * (i + 1) // len(main)
                    while done < want:
                        extra[done]()
                        done += 1
                for e in extra[done:]:
                    e()

            x_evac(0)
            for name, half in k_jobs(0)[0:3]:
                k_evac(0, name, half)
            x_evac(1)
            for name, half in k_jobs(0)[3:]:
                k_evac(0, name, half)
            its = {u: [lambda u=u, i=i: item(u, i) for i in range(ITEMS)] for u in range(UNITS)}
            spread([lambda i=i: gv_evac(0, i) for _, i in gv_jobs(0)], its[0][:NL])
            for u in range(UNITS):
                rest = its[u][NL:]
                if u + 1 < UNITS:
                    ks = k_jobs(u + 1)
                    early = [j for j in ks if j[0] in ("q", "k", "ga")]
                    spread([lambda j=j: k_evac(u + 1, *j) for j in early], rest)
                    for j in ks[len(early):]:
                        k_evac(u + 1, *j)
                    log_f(u + 1)
                else:
                    for e in rest:
                        e()
                for g in range(2):
                    f = evac(("khT", u, g))
                    A(KH[:, 4 * g:4 * g + 4, :], PJ[number[("khT", u, g)] % 2].rearrange("p (t n) -> p t n", t=4),
                      ACT.Copy).then_inc(f, 1)
                nh = heads(u)
                gates = GVB[:, :, 0:nh * P] if is_gla(u) else GVH[:, :, 0:P]
                A(gates, gates, ACT.Silu).then_inc(silu_g, 1)
                for n in range(first_step[u], first_step[u + 1]):
                    _, t, h = steps[n]
                    act.wait_ge(o_ready, n + 1)
                    A(O[:, h, t, :], OP[n % 2], ACT.Copy)
                    A(OP[n % 2], OP[n % 2], ACT.Square, accum_out=SS[:, h * NT + t:h * NT + t + 1]).then_inc(o_free, 1)
                act.wait_ge(o_free, first_step[u + 1])
                rsqrt_of(0, nh * NT, P).then_inc(rr_h, 1)
                if u + 1 < UNITS:
                    act.wait_ge(og_ready, u + 1)
                    spread([lambda i=i: gv_evac(u + 1, i) for _, i in gv_jobs(u + 1)], its[u + 1][:NL])
                for h in range(nh):
                    vb = 2 * u + h if is_gla(u) else 4 + u - GLA_UNITS
                    for g in range(2):
                        job = ("oT", u, h, g)
                        f = evac(job)
                        A(OT[:, vb, g * HALF:(g + 1) * HALF], PJ[number[job] % 2], ACT.Copy,
                          scale=GN[:, 0:1] if is_gla(u) else GN[:, 1:2]).then_inc(f, 1)
            def row_evac(v, dst):
                for half in range(2):
                    job = ("row", v, half)
                    f = evac(job)
                    A(dst.rearrange("p (n k) -> p k n", k=KD)[:, 4 * half:4 * half + 4, :],
                      PJ[number[job] % 2].rearrange("p (k n) -> p k n", k=4), ACT.Copy).then_inc(f, 1)

            row_evac("gt1", GT1B[:])
            act.wait_ge(ar_used, UNITS * KD)
            act.dma_start(WRT[:, :, 0:NG], w_rg.rearrange("a (p k) n -> p (a k) n", k=KD)).then_inc(wrt_in, 16)
            act.dma_start(WRT[:, :, NG:], w_re.rearrange("a (p k) n -> p (a k) n", k=KD)).then_inc(wrt_in, 16)
            for t in range(NT):
                act.wait_ge(x1_ready, t + 1)
                chain(A(SQ, X1[:, t, :], ACT.Square, accum_out=SS[:, 0:1]))
                rsqrt_of(0, 1, D).then_inc(ss2, 1)
                act.wait_ge(r2, t + 1)
                A(XT[:, t % 2, :], X1[:, t, :], ACT.Copy, scale=RR[:, 1:2]).then_inc(xn_ready, 1)
                if t in (NT // 2 + 1, NT - 1):
                    g = t // (NT - 1)
                    f = evac(("lg", g))
                    A(LGS[:, g * HALF:(g + 1) * HALF], PJ[number[("lg", g)] % 2][0:NG + NE, :], ACT.Copy).then_inc(f, 1)
            act.wait_ge(gd_ready, 1)
            A(GD[:], GD[:], ACT.Exp).then_inc(eg_ready, 1)
            act.wait_ge(gd_ready, 2)
            A(V8[:, 4, :], V8[:, 3, :], ACT.Exp).then_inc(eg_ready, 1)
            row_evac("gt2", GT2B[:])
            row_evac("shf", SHF[:])
            row_evac("scf", GSF[:])

            def store(m, par, row):
                act.wait_ge(y_ev, m + 1)
                act.dma_start(ys_d[bass.ds(row, C), :], YB[0:C, par, :]).then_inc(y_st[par], 16)

            def gates_up(it, s, first):
                n = 4 * it + s
                act.wait_ge(gu_ready, n + 1)
                if not (first and s < 2):
                    act.wait_ge(att_ready, 4 * it + (s - 1))
                A(SIL[:, s % 2], GU[s % 2][:, 0:FB * C].rearrange("p (j c) -> p j c", j=FB), ACT.Silu).then_inc(sil_ready, 1)
                if not (first and s == 0):
                    store(4 * it + (s - 1), (s + 1) % 2, (4 * it + (s - 1)) * C)

            for s in range(4):
                gates_up(0, s, True)
            with act.Fori(1, NE // 4) as it:
                for s in range(4):
                    gates_up(it, s, False)
            store(NE - 1, 1, (NE - 1) * C)
            nx = act.value_load(NXI[:, :], min_val=0, max_val=NX)
            for s in range(2):
                act.wait_ge(y_st[s], 16 * NE // 2)
            act.wait_ge(ys_filled, 16 * ((NX * C + T - 1) // T))
            with act.If(nx > 0):
                with act.Fori(0, NX) as i:
                    with act.If(nx > i):
                        act.wait_ge(xgu, i + 1)
                        A(SIL[:, 0], GU[0][:, 0:FB * C].rearrange("p (j c) -> p j c", j=FB), ACT.Silu).then_inc(xsil, 1)
                        act.wait_ge(xyev, i + 1)
                        act.dma_start(ys_d[bass.ds((i + NE) * C, C), :], YB[0:C, 0, :]).then_inc(x_done, 16)
                        act.wait_ge(x_done, 16 * i + 32)
                        A(TOCK[:], RR[:, 0:1], ACT.Copy)
                act.nop()
            act.sem_inc(extras_done, 1)
            for t in range(NT):
                act.wait_ge(x2_ready, t + 1)
                chain(A(SQ, X1[:, t, :], ACT.Square, accum_out=SS[:, 0:1]))
                rsqrt_of(0, 1, D).then_inc(ss3, 1)
                act.wait_ge(r3, t + 1)

        @block.vector
        def _(v_):
            V = nc.vector
            cnt = [0]

            def link(ins):
                cnt[0] += 1
                ins.then_inc(dve, 1)
                v_.wait_ge(dve, cnt[0])

            def polish(lo, hi, dst=None):
                r, m = RR[:, lo:hi], TA[:, lo:hi]
                link(V.tensor_tensor(m, m, r, ALU.mult))
                link(V.tensor_tensor(m, m, r, ALU.mult))
                link(V.tensor_scalar(m, m, -0.5, 1.5, ALU.mult, ALU.add))
                return V.tensor_tensor(r if dst is None else dst, r, m, ALU.mult)

            v_.wait_ge(ios, 5)
            link(V.tensor_tensor(XOR[:], IOI[:], IOJ[:], ALU.bitwise_xor))
            for l, s in enumerate(LEVELS):
                link(V.tensor_single_scalar(MT1[:], XOR[:], s, op=ALU.is_ge))
                link(V.tensor_single_scalar(MT2[:], XOR[:], 2 * s, op=ALU.is_lt))
                link(V.tensor_tensor(MASK[:, l, :], MT1[:], MT2[:], ALU.mult))
            link(V.tensor_single_scalar(MT1[:], XOR[:], 4, op=ALU.is_lt))
            link(V.tensor_tensor(MT2[:], IOI[:], IOJ[:], ALU.is_ge))
            link(V.tensor_tensor(MASK[:, NL, :], MT1[:], MT2[:], ALU.mult))
            link(V.tensor_tensor(UT[:], IOI[:], IOJ[:], ALU.is_gt))
            link(V.memset(RESET[:], 1))
            link(V.memset(RESET[:, 0::P], 0))
            link(V.memset(AT2[:], 0.0))
            v_.wait_ge(small_in, 16 * 10)
            link(V.tensor_scalar(BAN[:, 1, :], BAN[:, 0, :], -1.0, None, ALU.mult))
            link(V.tensor_tensor(LB[:, 0, :], LBT[:, 0, :], LBT[:, 1, :], ALU.max))
            link(V.tensor_tensor(LBT[:, 0, :], LBT[:, 0, :], LB[:, 0, :], ALU.subtract))
            V.tensor_tensor(LBT[:, 1, :], LBT[:, 1, :], LB[:, 0, :], ALU.subtract).then_inc(consts, 1)
            v_.wait_ge(ca_ready, 1)

            ada_n = [0]

            def add_slice(w, arrived, count, acc, k, used, n):
                v_.wait_ge(arrived, count)
                if k == 0:
                    i = V.tensor_scalar(acc, w, CA[:, 0:1], None, ALU.mult)
                else:
                    i = V.scalar_tensor_tensor(out=acc, in0=w, scalar=CA[:, k:k + 1], in1=acc,
                                               op0=ALU.mult, op1=ALU.add)
                i.then_inc(used, 1)
                v_.wait_ge(used, n + 1)

            def unit_slice():
                n = ada_n[0]
                ada_n[0] += 1
                add_slice(AR[:, n % 2, :], ar_in[n % 2], 16 * (n // 2 + 1), ACC[:], n % KD, ar_used, n)

            def column(v, dst, gcol=None):
                n = number[("col", v)]
                v_.wait_ge(pj_ready, n + 1)
                V.tensor_tensor(dst, PJ[n % 2][:, 0:KD], BCOL[:, list(ADA).index(v), :], ALU.add).then_inc(pj_free[n % 2], 1)
                v_.wait_ge(pj_free[n % 2], n // 2 + 1)
                if gcol is not None:
                    link(V.scalar_tensor_tensor(out=dst, in0=dst, scalar=1.0, in1=gcol, op0=ALU.add, op1=ALU.mult))

            COLUMN = {"gt1": (GT1[:], None), "sh2": (SH2[:], None), "sc2": (GS2[:], GCOL[:, 1, :]),
                      "gt2": (GT2[:], None), "shf": (SHC[:], None), "scf": (GSC[:], GCOL[:, 2, :])}

            for i, acc in enumerate((ACC, ACCB)):
                for k in range(KD):
                    n = i * KD + k
                    add_slice(AST[:, n % 8, :], ast_in[n % 8], 16 * (n // 8 + 1), acc[:], k, ast_used, n)
            column("sc1", GS1[:], GCOL[:, 0, :])
            v_.sem_inc(mod1_ready, 1)
            column("sh1", SH1[:])
            v_.sem_inc(mod1_ready, 1)
            for g in range(2):
                v_.wait_ge(rr_ready, g + 1)
                link(polish(4 * g, 4 * g + 4))
                for t in range(4 * g, 4 * g + 4):
                    V.tensor_scalar(XR[:, t, :], XR[:, t, :], RR[:, t:t + 1], None, ALU.mult).then_inc(xr_ready, 1)

            v_.wait_ge(lf_ready, 1)
            link(V.tensor_tensor(LB[:, 1, :], LBT[:, 0, :], LBT[:, 1, :], ALU.add))
            link(V.reciprocal(LB[:, 1, :], LB[:, 1, :]))
            link(V.tensor_tensor(LB[:, 0, :], LBT[:, 0, :], LB[:, 1, :], ALU.mult))
            link(V.tensor_scalar(LB[:, 0, :], LB[:, 0, :], 4.3e-18, None, ALU.max))
            link(V.tensor_scalar(LB[:, 1, :], LB[:, 0, :], -1.0, 1.0, ALU.mult, ALU.add))
            link(V.tensor_scalar(LB[:, 2, :], LB[:, 1, :], -1.0, None, ALU.mult))

            def level(ap, s):
                return ap.rearrange("p (c a s) -> p c a s", a=2, s=s)

            def sub(u, i):
                if i < NL:
                    s = LEVELS[i]
                    x_, b_ = level(XL[:, i, :], s), level(B[:], s)
                    nb = T // (2 * s)
                    ref = b_[:, :, 0, s - 1:s].to_broadcast([P, nb, s])
                    V.tensor_tensor(x_[:, :, 0, :], ref, b_[:, :, 0, :], ALU.subtract)
                    V.tensor_tensor(x_[:, :, 1, :], b_[:, :, 1, :], ref, ALU.subtract).then_inc(e_sub, 1)
                elif i == NL:
                    b_ = B[:].rearrange("p (c s) -> p c s", s=4)
                    V.tensor_tensor(BA[:].rearrange("p (c s) -> p c s", s=4), b_,
                                    b_[:, :, 1:2].to_broadcast([P, T // 4, 4]), ALU.subtract).then_inc(e_sub, 1)
                elif i == NL + 2:
                    b_ = B[:].rearrange("p (c s) -> p c s", s=P)
                    V.tensor_tensor(KHT[:].rearrange("p (c s) -> p c s", s=P),
                                    b_[:, :, P - 1:P].to_broadcast([P, NT, P]), b_, ALU.subtract).then_inc(e_sub, 1)

            def mul(u, i):
                v_.wait_ge(e_exp, ITEMS * u + i + 1)
                q_, k_ = Q[:, u % 2, :], K[:, u % 2, :]
                if i < NL:
                    s = LEVELS[i]
                    x_ = level(XL[:, i, :], s)
                    V.tensor_tensor(x_[:, :, 0, :], x_[:, :, 0, :], level(k_, s)[:, :, 0, :], ALU.mult)
                    V.tensor_tensor(x_[:, :, 1, :], x_[:, :, 1, :], level(q_, s)[:, :, 1, :], ALU.mult).then_inc(e_mul, 1)
                elif i == NL:
                    V.tensor_tensor(BB[:], BB[:], k_, ALU.mult)
                    V.tensor_tensor(BA[:], BA[:], q_, ALU.mult).then_inc(e_mul, 1)
                elif i == NL + 1:
                    V.tensor_tensor(QE[:], QE[:], q_, ALU.mult).then_inc(e_mul, 1)
                else:
                    V.tensor_tensor(KHT[:], KHT[:], k_, ALU.mult).then_inc(e_mul, 1)

            def decay(u):
                if is_gla(u):
                    for half in range(2):
                        hs = slice(half * HALF, (half + 1) * HALF)
                        v_.wait_ge(f_ready, 2 * u + half + 1)
                        V.tensor_tensor(FD[:, hs], FD[:, hs], SG[:], ALU.add).then_inc(f_used, 1)
                        v_.wait_ge(f_used, 2 * u + half + 1)
                        link(V.tensor_scalar(FD[:, hs], FD[:, hs], -1.0 / 16.0, GMIN, ALU.mult, ALU.max))
                else:
                    h = u - GLA_UNITS
                    for half in range(2):
                        n = number[(u, "f", half)]
                        v_.wait_ge(pj_free[n % 2], n // 2 + 1)
                    V.tensor_scalar(K[:, u % 2, :], FD[:], LB[:, 2, h:h + 1], LB[:, 1, h:h + 1],
                                    ALU.mult, ALU.add).then_inc(kf_ready, 1)
                    v_.wait_ge(lf_ready, h + 2)
                V.tensor_tensor_scan(B[:], RESET[:], FD[:], 0.0, ALU.mult, ALU.add).then_inc(b_ready, 1)
                v_.wait_ge(b_ready, u + 1)

            def attention_step(n):
                u, t, h = steps[n]
                rows = slice(64 * h, 64 * h + 64) if is_gla(u) else slice(0, P)
                lv, a = LV[n % 2], AT2[:, n % 2, :]
                v_.wait_ge(lv_ready, n + 1)
                if n >= 2:
                    v_.wait_ge(o_ready, n - 1)
                for l, s in enumerate(LEVELS):
                    src = lv[:, l * P:(l + 1) * P]
                    link(V.copy_predicated(level(a, s)[:, :, 1, :], level(MASK[:, l, :], s)[:, :, 1, :],
                                           level(src, s)[:, :, 1, :]))
                last = V.copy_predicated(a, MASK[:, NL, :], lv[:, NL * P:(NL + 1) * P])
                if t < NT - 1:
                    if t >= 1:
                        v_.wait_ge(o_ready, step_at[(u, t - 1, h)] + 1)
                    st = lv[rows, (NL + 1) * P:(NL + 2) * P]
                    if t == 0:
                        last = V.tensor_copy(S[rows, 1, :], st)
                    else:
                        last = V.scalar_tensor_tensor(out=S[rows, (t + 1) % 2, :], in0=S[rows, t % 2, :],
                                                      scalar=EBL[rows, t:t + 1], in1=st, op0=ALU.mult, op1=ALU.add)
                last.then_inc(at_ready, 1)

            def o_post(u):
                nh = heads(u)
                v_.wait_ge(rr_h, u + 1)
                v_.wait_ge(silu_g, u + 1)
                link(polish(0, nh * NT))
                for h in range(nh):
                    for t in range(NT):
                        gate = GVB[:, t, h * P:(h + 1) * P] if is_gla(u) else GVH[:, t, 0:P]
                        i = h * NT + t
                        last = V.scalar_tensor_tensor(out=O[:, h, t, :], in0=O[:, h, t, :], scalar=RR[:, i:i + 1],
                                                      in1=gate, op0=ALU.mult, op1=ALU.mult)
                last.then_inc(og_ready, 1)

            decay(0)
            for i in range(NL):
                sub(0, i)
            for i in range(NL):
                mul(0, i)
            for u in range(UNITS):
                sub(u, NL)
                sub(u, NL + 1)
                if u > 0:
                    v_.wait_ge(pj_ready, number[("oT", u - 1, heads(u - 1) - 1, 1)] + 1)
                sub(u, NL + 2)
                for i in range(NL, ITEMS):
                    mul(u, i)
                if u + 1 < UNITS:
                    decay(u + 1)
                lo, hi = first_step[u], first_step[u + 1]
                for n in range(lo, hi):
                    attention_step(n)
                    if (n + 1 - lo) % heads(u) == 0:
                        unit_slice()
                column(UNIT_ADA[u], *COLUMN[UNIT_ADA[u]])
                o_post(u)
                if u + 1 < UNITS:
                    for i in range(NL):
                        sub(u + 1, i)
                    for i in range(NL):
                        mul(u + 1, i)
            for half in range(2):
                n = number[("row", "gt1", half)]
                v_.wait_ge(pj_free[n % 2], n // 2 + 1)

            def residual(t):
                v_.wait_ge(xt_in[t % 2], 16 * (t // 2 + 1))
                for half in range(2):
                    n = number[("wo", t, half)]
                    hs = slice(half * HALF, (half + 1) * HALF)
                    v_.wait_ge(pj_ready, n + 1)
                    V.tensor_tensor(X1[:, t, hs], PJ[n % 2], GT1B[:, hs], ALU.mult).then_inc(pj_free[n % 2], 1)
                    v_.wait_ge(pj_free[n % 2], n // 2 + 1)
                    i = V.tensor_tensor(X1[:, t, hs], X1[:, t, hs], XT[:, t % 2, hs], ALU.add)
                i.then_inc(x1_ready, 1)

            def h2_evac(t):
                for half in range(2):
                    n = number[("h2T", t, half)]
                    v_.wait_ge(pj_ready, n + 1)
                    dst = H2T[:, 4 * half:4 * half + 4, t * P:(t + 1) * P]
                    ks = slice(4 * half, 4 * half + 4)
                    V.tensor_tensor(dst, PJ[n % 2].rearrange("p (k n) -> p k n", k=4),
                                    GS2[:, ks].rearrange("p (k a) -> p k a", a=1).to_broadcast([P, 4, P]),
                                    ALU.mult).then_inc(pj_free[n % 2], 1)
                    v_.wait_ge(pj_free[n % 2], n // 2 + 1)
                    V.tensor_tensor(dst, dst, SH2[:, ks].rearrange("p (k a) -> p k a", a=1).to_broadcast([P, 4, P]),
                                    ALU.add).then_inc(h2_ready, 1)

            for t in range(NT):
                residual(t)
                v_.wait_ge(ss2, t + 1)
                polish(0, 1, RR[:, 1:2]).then_inc(r2, 1)
                if t >= 1:
                    h2_evac(t - 1)
            h2_evac(NT - 1)
            v_.wait_ge(ios, 10)
            v_.wait_ge(br_in, 32)
            n = number[("lgT",)]
            v_.wait_ge(pj_ready, n + 1)
            W = NG + NE

            def bc_t(ap, w):
                return ap.rearrange("p (a w) -> p a w", a=1).to_broadcast([P, NT, w])

            def bc_w(ap, w):
                return ap.rearrange("p (t a) -> p t a", a=1).to_broadcast([P, NT, w])

            link(V.tensor_tensor(LG[:], PJ[n % 2][:, 0:NT * W].rearrange("p (t w) -> p t w", t=NT),
                                 bc_t(BR[:], W), ALU.add))
            v_.sem_inc(pj_free[n % 2], 1)
            g_, e_ = LG[:, :, 0:NG], LG[:, :, NG:W]
            vm, vs, vp, vd, ve, v1, v2, vq = (V8[:, i, :] for i in range(8))
            link(V.tensor_reduce(vm, g_, AX, ALU.max))
            link(V.tensor_tensor(GD[:], g_, bc_w(vm, NG), ALU.subtract))
            link(V.scalar_tensor_tensor(out=OHG[:], in0=GD[:], scalar=0.0, in1=bc_t(PR[:, NE - NG:NE], NG),
                                        op0=ALU.is_ge, op1=ALU.mult))
            v_.sem_inc(gd_ready, 1)
            link(V.tensor_reduce(vm, OHG[:], AX, ALU.max))
            link(V.tensor_tensor(OHG[:], OHG[:], bc_w(vm, NG), ALU.is_equal))
            link(V.tensor_scalar(PEN[:], OHG[:], -1.0, BIG, ALU.add, ALU.mult))
            em4 = EM[:].rearrange("p t (g e) -> p (t g) e", g=NG)

            def bc_g(ap):
                return ap.rearrange("p t (g a) -> p (t g) a", a=1).to_broadcast([P, NT * NG, EG])

            link(V.tensor_copy(EM[:], e_))
            link(V.tensor_tensor(em4, em4, bc_g(OHG[:]), ALU.mult))
            link(V.tensor_tensor(em4, em4, bc_g(PEN[:]), ALU.add))

            def pick(mx, oh):
                link(V.tensor_reduce(mx, EM[:], AX, ALU.max))
                link(V.tensor_tensor(SCR[:], EM[:], bc_w(mx, NE), ALU.is_ge))
                link(V.tensor_tensor(SCR[:], SCR[:], bc_t(PR[:], NE), ALU.mult))
                link(V.tensor_reduce(vq, SCR[:], AX, ALU.max))
                link(V.tensor_tensor(oh, SCR[:], bc_w(vq, NE), ALU.is_equal))

            pick(v1, M1[:])
            link(V.scalar_tensor_tensor(out=EM[:], in0=M1[:], scalar=-3.0 * BIG, in1=EM[:], op0=ALU.mult, op1=ALU.add))
            pick(v2, M2[:])
            link(V.tensor_tensor(MB[:].rearrange("p (t e) -> p t e", t=NT), M1[:], M2[:], ALU.add))
            v_.sem_inc(mb_ready, 1)
            link(V.tensor_tensor(vd, v2, v1, ALU.subtract))
            v_.sem_inc(gd_ready, 1)
            v_.wait_ge(eg_ready, 2)
            link(V.tensor_reduce(vs, GD[:], AX, ALU.add))
            link(V.reciprocal(vp, vs))
            link(V.tensor_scalar(vs, ve, 1.0, None, ALU.add))
            link(V.reciprocal(vs, vs))
            link(V.tensor_tensor(WPAIR[:, 0, :], vp, vs, ALU.mult))
            link(V.tensor_tensor(WPAIR[:, 1, :], WPAIR[:, 0, :], ve, ALU.mult))
            n = number[("rank",)]
            v_.wait_ge(pj_ready, n + 1)
            half_ = NT * NE
            link(V.tensor_copy(TOT[:].rearrange("p t e -> p (t e)"), PJ[n % 2][:, half_:2 * half_]))
            link(V.memset(PRE[:, 0, :], 0.0))
            for t in range(NT):
                link(V.tensor_tensor(PRE[:, t + 1, :], PRE[:, t, :], TOT[:, t, :], ALU.add))
            link(V.tensor_tensor(RK[:].rearrange("p t e -> p (t e)"), PJ[n % 2][:, 0:half_],
                                 PRE[:, 0:NT, :].rearrange("p t e -> p (t e)"), ALU.add))
            v_.sem_inc(pj_free[n % 2], 1)
            cnt_ = PRE[:, NT, :]
            link(V.tensor_single_scalar(NXE[:], cnt_, float(C), op=ALU.is_gt))
            for m in range(2, MX + 1):
                link(V.scalar_tensor_tensor(out=NXE[:], in0=cnt_, scalar=float(C * m), in1=NXE[:],
                                            op0=ALU.is_gt, op1=ALU.add))
            link(V.memset(DX[:], 1.0))
            link(V.tensor_tensor_scan(XINC[:], DX[:], NXE[:], 0.0, ALU.mult, ALU.add))
            link(V.tensor_tensor(DX[:], XINC[:], NXE[:], ALU.subtract))
            link(V.tensor_scalar(DX[:], DX[:], float(NE - 1), float(C), ALU.add, ALU.mult))
            link(V.tensor_tensor(DX[:], DX[:], EC[:], ALU.subtract))
            link(V.tensor_single_scalar(SCR[:], RK[:], float(C), op=ALU.is_ge))
            link(V.tensor_tensor(SCR[:], SCR[:], bc_t(DX[:], NE), ALU.mult))
            link(V.tensor_tensor(SCR[:], SCR[:], RK[:], ALU.add))
            link(V.tensor_tensor(SCR[:], SCR[:], bc_t(EC[:], NE), ALU.add))
            for k, mk in enumerate((M1, M2)):
                link(V.tensor_tensor(EM[:], SCR[:], mk[:], ALU.mult))
                link(V.tensor_reduce(vq, EM[:], AX, ALU.add))
                link(V.tensor_copy(SLOT[:, k, :], vq))
            link(V.tensor_tensor(CMP[:], XINC[0:1, :].rearrange("p (a e) -> p a e", a=1).to_broadcast([1, NX, NE]),
                                 XS[:].rearrange("p (x a) -> p x a", a=1).to_broadcast([1, NX, NE]), ALU.is_le))
            link(V.tensor_reduce(XEF[:], CMP[:], AX, ALU.add))
            link(V.tensor_scalar(XE[:], XEF[:], float(NE - 1), None, ALU.min))
            V.tensor_copy(NXI[:], XINC[0:1, NE - 1:NE]).then_inc(slots_ready, 1)
            for v in ("gt2", "shf", "scf"):
                for half in range(2):
                    n = number[("row", v, half)]
                    v_.wait_ge(pj_free[n % 2], n // 2 + 1)

            def xgt_evac(slot, scaled, count, done):
                for b in range(2):
                    dst = XGT[:, slot, 4 * b:4 * b + 4, :]
                    ks = slice(4 * b, 4 * b + 4)
                    i = V.tensor_tensor(dst, TP[:, b, 0:4 * C].rearrange("p (k n) -> p k n", k=4),
                                        GS2[:, ks].rearrange("p (k a) -> p k a", a=1).to_broadcast([P, 4, C]), ALU.mult)
                i.then_inc(scaled, 1)
                v_.wait_ge(scaled, count)
                for b in range(2):
                    dst = XGT[:, slot, 4 * b:4 * b + 4, :]
                    ks = slice(4 * b, 4 * b + 4)
                    i = V.tensor_tensor(dst, dst, SH2[:, ks].rearrange("p (k a) -> p k a", a=1).to_broadcast([P, 4, C]),
                                        ALU.add)
                i.then_inc(done, 1)

            def act_mul(par, done):
                V.tensor_tensor(ATT[:, par], SIL[:, par],
                                GU[par][:, FB * C:2 * FB * C].rearrange("p (j c) -> p j c", j=FB), ALU.mult).then_inc(done, 1)

            def y_evac(par, done):
                V.tensor_tensor(YB[0:C, par, 0:HALF], YP[par][0:C, 0:HALF], GT2B[0:C, 0:HALF], ALU.mult)
                V.tensor_tensor(YB[0:C, par, HALF:D], YP[par][0:C, HALF:D], GT2B[0:C, HALF:D], ALU.mult).then_inc(done, 1)

            def expert_step(it, s, first, last):
                n = 4 * it + s
                if not (last and s == 3):
                    v_.wait_ge(t_ready, 4 * it + (s + 2))
                    if not (first and s == 0):
                        v_.wait_ge(gu_ready, 4 * it + s)
                    xgt_evac((s + 1) % 2, xgt_scaled, 4 * it + (s + 2), xgt_ready)
                v_.wait_ge(sil_ready, 4 * it + (s + 1))
                if not (first and s < 2):
                    v_.wait_ge(y_ready, 4 * it + (s - 1))
                act_mul(s % 2, att_ready)
                if not (first and s == 0):
                    par = (s + 1) % 2
                    v_.wait_ge(y_ready, 4 * it + s)
                    if not (first and s < 3):
                        v_.wait_ge(y_st[par], 16 * (2 * it) + 16 * ((s - 1) // 2))
                    y_evac(par, y_ev)

            v_.wait_ge(t_ready, 1)
            xgt_evac(0, xgt_scaled, 1, xgt_ready)
            for s in range(4):
                expert_step(0, s, True, False)
            with v_.Fori(1, NE // 4 - 1) as it:
                for s in range(4):
                    expert_step(it, s, False, False)
            for s in range(4):
                expert_step(NE // 4 - 1, s, False, True)
            v_.wait_ge(y_ready, NE)
            v_.wait_ge(y_st[1], 16 * (NE // 2 - 1))
            y_evac(1, y_ev)
            v_.wait_ge(y_st[0], 16 * (NE // 2))
            nx = v_.value_load(NXI[:, :], min_val=0, max_val=NX)
            with v_.If(nx > 0):
                with v_.Fori(0, NX) as i:
                    with v_.If(nx > i):
                        v_.wait_ge(xt_ready, i + 1)
                        xgt_evac(0, xxgt_scaled, i + 1, xxgt)
                        v_.wait_ge(xsil, i + 1)
                        act_mul(0, xatt)
                        v_.wait_ge(xy, i + 1)
                        y_evac(0, xyev)
                v_.nop()
            def add_rows(t):
                for k in range(2):
                    if k == 0:
                        v_.wait_ge(yg_in[t % 4], 32 * (t // 4 + 1))
                    i = V.scalar_tensor_tensor(out=X1[:, t, :], in0=YG[:, t % 4, k, :], scalar=WPAIR[:, k, t:t + 1],
                                               in1=X1[:, t, :], op0=ALU.mult, op1=ALU.add)
                    if k == 0:
                        link(i)
                    else:
                        i.then_inc(x2_ready, 1)

            add_rows(0)
            for t in range(NT):
                if t + 1 < NT:
                    add_rows(t + 1)
                v_.wait_ge(ss3, t + 1)
                polish(0, 1, RR[:, 1:2]).then_inc(r3, 1)
                v_.wait_ge(r3, t + 1)
                if t >= 2:
                    v_.wait_ge(out_st[t % 2], 16 * (t // 2))
                link(V.scalar_tensor_tensor(out=OUTT[:, t % 2, :], in0=X1[:, t, :], scalar=RR[:, 1:2], in1=GSF[:],
                                            op0=ALU.mult, op1=ALU.mult))
                V.tensor_tensor(OUTT[:, t % 2, :], OUTT[:, t % 2, :], SHF[:], ALU.add).then_inc(out_ready, 1)

        @block.tensor
        def _(pe):
            MM, TR = nc.tensor.matmul, nc.tensor.transpose

            def begin(job):
                n = number[job]
                if n >= 2:
                    pe.wait_ge(pj_free[n % 2], n // 2)
                return PJ[n % 2]

            def evacuated(job):
                n = number[job]
                pe.wait_ge(pj_free[n % 2], n // 2 + 1)

            def col_job(v, acc, summed, count):
                pe.wait_ge(summed, count)
                ps = begin(("col", v))
                for k in range(KD):
                    last = MM(ps[:, k:k + 1], acc[:, k::KD], ONESF[:, 0:1], start=True, stop=True)
                last.then_inc(pj_ready, 1)

            def row_job(v, col):
                for half in range(2):
                    ps = begin(("row", v, half))
                    for k in range(4):
                        kk = 4 * half + k
                        last = MM(ps[:, k * P:(k + 1) * P], col[:, kk:kk + 1].to_broadcast([P, P]), IDENT[:], start=True, stop=True)
                    last.then_inc(pj_ready, 1)

            pe.wait_ge(ios, 5)
            col_job("sc1", ACC, ast_used, KD)
            col_job("sh1", ACCB, ast_used, 2 * KD)

            def x_transposes(g):
                pe.wait_ge(xr_ready, 4 * g + 4)
                for k in range(KD):
                    ps = begin(("xT", g, k))
                    for t in range(4):
                        last = TR(ps[:, t * P:(t + 1) * P], XR[:, 4 * g + t, k::KD], IDENT[:])
                    last.then_inc(pj_ready, 1)

            def chunk(u, name):
                n = chunk_at[(u, name)]
                pe.wait_ge(w_in_s[n % WRING], 16 * (n // WRING + 1))
                return n % WRING

            def k_job(u, name, half):
                hs = slice(half * HALF, (half + 1) * HALF)
                if name == "a":
                    if half == 0:
                        for h in range(2):
                            evacuated((0, "ga", h))
                    ps = begin((u, name, half))
                    MM(ps, WA2[:, u * P:(u + 1) * P], GA[:, hs], start=True, stop=True).then_inc(pj_ready, 1)
                    return
                if name == "ga":
                    pe.wait_ge(wga_in, 32)
                    ps = begin((u, name, half))[0:RANK, :]
                else:
                    slot = chunk(u, name)
                    ps = begin((u, name, half))
                for k in range(KD):
                    if (u, name) == (0, "q"):
                        evacuated(("xT", half, k))
                    w = WGA[:, k, :] if name == "ga" else WR[:, slot, k, :]
                    last = MM(ps, w, HT[:, k, hs], start=(k == 0), stop=(k == KD - 1))
                last.then_inc(pj_ready, 1)

            def gv_job(u, i):
                names = ["g0", "g1", "v0", "v1"] if is_gla(u) else ["g0", "v0"]
                s0 = [chunk(u, nm) for nm in names][0]
                nc_ = len(names)
                ps = begin((u, "gv", i))
                for tt in range(GVT[u]):
                    t = i * GVT[u] + tt
                    dst = ps[:, tt * nc_ * P:(tt + 1) * nc_ * P].rearrange("p (c n) -> p c n", c=nc_)
                    for k in range(KD):
                        last = MM(dst, HT[:, k, t * P:(t + 1) * P], WR[:, s0:s0 + nc_, k, :],
                                  start=(k == 0), stop=(k == KD - 1))
                last.then_inc(pj_ready, 1)

            def levels(n):
                u, t, h = steps[n]
                rows = slice(64 * h, 64 * h + 64) if is_gla(u) else slice(0, P)
                ts = slice(t * P, (t + 1) * P)
                if n >= 2:
                    pe.wait_ge(at_ready, n - 1)
                lv = LV[n % 2]
                for l in range(NL):
                    MM(lv[:, l * P:(l + 1) * P], XL[rows, l, ts], XL[rows, l, ts], start=True, stop=True)
                last = MM(lv[:, NL * P:(NL + 1) * P], BB[rows, ts], BA[rows, ts], start=True, stop=True)
                if t < NT - 1:
                    last = MM(lv[rows, (NL + 1) * P:(NL + 2) * P], KH[:, t, rows], values(u, t, h), start=True, stop=True)
                last.then_inc(lv_ready, 1)

            def values(u, t, h):
                return GVB[:, t, (2 + h) * P:(3 + h) * P] if is_gla(u) else GVH[:, t, P:2 * P]

            def output(n):
                u, t, h = steps[n]
                rows = slice(64 * h, 64 * h + 64) if is_gla(u) else slice(0, P)
                pe.wait_ge(at_ready, n + 1)
                if n >= 2:
                    pe.wait_ge(o_free, n - 1)
                last = MM(OP[n % 2], AT2[:, n % 2, :], values(u, t, h), start=True, stop=(t == 0))
                if t > 0:
                    last = MM(OP[n % 2], QE[rows, t * P:(t + 1) * P], S[rows, t % 2, :], start=False, stop=True)
                last.then_inc(o_ready, 1)

            x_transposes(0)
            for name, half in k_jobs(0)[0:3]:
                k_job(0, name, half)
            x_transposes(1)
            for name, half in k_jobs(0)[3:]:
                k_job(0, name, half)
            for _, i in gv_jobs(0):
                gv_job(0, i)
            for u in range(UNITS):
                if u + 1 < UNITS:
                    for name, half in k_jobs(u + 1):
                        k_job(u + 1, name, half)
                pe.wait_ge(e_mul, ITEMS * (u + 1))
                for g in range(2):
                    ps = begin(("khT", u, g))
                    for t in range(4):
                        last = TR(ps[:, t * P:(t + 1) * P], KHT[:, (4 * g + t) * P:(4 * g + t + 1) * P], IDENT[:])
                    last.then_inc(pj_ready, 1)
                for g in range(2):
                    evacuated(("khT", u, g))
                for _, i in gv_jobs(u)[-2:]:
                    evacuated((u, "gv", i))
                lo, hi = first_step[u], first_step[u + 1]
                levels(lo)
                for n in range(lo + 1, hi):
                    levels(n)
                    output(n - 1)
                output(hi - 1)
                col_job(UNIT_ADA[u], ACC, ar_used, KD * (u + 1))
                if u + 1 < UNITS:
                    for _, i in gv_jobs(u + 1):
                        gv_job(u + 1, i)
                pe.wait_ge(og_ready, u + 1)
                for h in range(heads(u)):
                    for g in range(2):
                        ps = begin(("oT", u, h, g))
                        for t in range(4):
                            last = TR(ps[:, t * P:(t + 1) * P], O[:, h, 4 * g + t, :], IDENT[:])
                        last.then_inc(pj_ready, 1)
            row_job("gt1", GT1)
            for g in range(2):
                evacuated(("oT", UNITS - 1, 0, g))
            pe.wait_ge(wout_in, 32)

            def transpose_xn(t):
                pe.wait_ge(xn_ready, t + 1)
                for half in range(2):
                    ps = begin(("h2T", t, half))
                    for k in range(4):
                        last = TR(ps[:, k * P:(k + 1) * P], XT[:, t % 2, 4 * half + k::KD], IDENT[:])
                    last.then_inc(pj_ready, 1)

            for kind, i in out_order:
                if kind == "wo":
                    for half in range(2):
                        ps = begin(("wo", i, half))
                        for v in range(8):
                            last = MM(ps, OT[:, v, i * P:(i + 1) * P], WOUT[:, v, half * HALF:(half + 1) * HALF],
                                      start=(v == 0), stop=(v == 7))
                        last.then_inc(pj_ready, 1)
                elif kind == "h2T":
                    transpose_xn(i)
                else:
                    pe.wait_ge(h2_ready, 8 * (i + 1))
                    pe.wait_ge(wrt_in, 32)
                    ps = begin(("lg", i))
                    for k in range(KD):
                        last = MM(ps[0:NG + NE, :], WRT[:, k, :], H2T[:, k, i * HALF:(i + 1) * HALF],
                                  start=(k == 0), stop=(k == KD - 1))
                    last.then_inc(pj_ready, 1)
            for g in range(2):
                evacuated(("lg", g))
            ps = begin(("lgT",))
            W = NG + NE
            for t in range(NT):
                last = TR(ps[:, t * W:(t + 1) * W], LGS[:, t * P:(t + 1) * P], IDENT[0:W, 0:W])
            last.then_inc(pj_ready, 1)
            pe.wait_ge(mb_ready, 1)
            ps = begin(("rank",))
            MM(ps[:, 0:NT * NE], UT[:], MB[:], start=True, stop=True)
            MM(ps[:, NT * NE:2 * NT * NE], ONEB[:], MB[:], start=True, stop=True).then_inc(pj_ready, 1)
            row_job("gt2", GT2)
            row_job("shf", SHC)
            row_job("scf", GSC)
            evacuated(("row", "scf", 1))
            evacuated(("row", "scf", 0))

            def xg_transposes(slot, done):
                for k in range(KD):
                    last = TR(TP[:, k // 4, (k % 4) * C:(k % 4 + 1) * C], XG[0:C, slot, k::KD], IDENT[0:C, 0:C])
                last.then_inc(done, 1)

            def gate_up(par, slot, done):
                for m in range(2):
                    for j in range(FB):
                        col = (m * FB + j) * C
                        for k in range(KD):
                            last = MM(GU[par][:, col:col + C], WGU[slot][:, m, k, j * P:(j + 1) * P],
                                      XGT[:, par, k, :], start=(k == 0), stop=(k == KD - 1))
                last.then_inc(done, 1)

            def down(par, slot, done):
                for half in range(2):
                    for j in range(FB):
                        last = MM(YP[par][0:C, half * HALF:(half + 1) * HALF], ATT[:, par, j, :],
                                  WDN[slot][:, j, half * HALF:(half + 1) * HALF], start=(j == 0), stop=(j == FB - 1))
                last.then_inc(done, 1)

            def expert_step(it, s, first, last):
                if not (last and s == 3):
                    pe.wait_ge(xg_in[(s + 1) % 4], 16 * it + 16 * ((s + 1) // 4 + 1))
                    pe.wait_ge(xgt_ready, 4 * it + (s + 1))
                    xg_transposes((s + 1) % 4, t_ready)
                pe.wait_ge(wexp_in[s], 48 * it + 48)
                pe.wait_ge(xgt_ready, 4 * it + (s + 1))
                if not (first and s < 2):
                    pe.wait_ge(att_ready, 4 * it + (s - 1))
                gate_up(s % 2, s, gu_ready)
                if not (first and s == 0):
                    pe.wait_ge(att_ready, 4 * it + s)
                    if not (first and s < 3):
                        pe.wait_ge(y_ev, 4 * it + (s - 2))
                    down((s + 1) % 2, (s + 3) % 4, y_ready)

            pe.wait_ge(xg_in[0], 16)
            xg_transposes(0, t_ready)
            for s in range(4):
                expert_step(0, s, True, False)
            with pe.Fori(1, NE // 4 - 1) as it:
                for s in range(4):
                    expert_step(it, s, False, False)
            for s in range(4):
                expert_step(NE // 4 - 1, s, False, True)
            pe.wait_ge(att_ready, NE)
            pe.wait_ge(y_ev, NE - 2)
            down(1, 3, y_ready)
            nx = pe.value_load(NXI[:, :], min_val=0, max_val=NX)
            with pe.If(nx > 0):
                with pe.Fori(0, NX) as i:
                    with pe.If(nx > i):
                        pe.wait_ge(xxg_in, 16 * i + 16)
                        xg_transposes(0, xt_ready)
                        pe.wait_ge(xw_in, 48 * i + 48)
                        pe.wait_ge(xxgt, i + 1)
                        gate_up(0, 0, xgu)
                        pe.wait_ge(xatt, i + 1)
                        down(0, 0, xy)
                pe.nop()


_INS = ["x", "c", "w_ada", "b_ada", "norm1_g", "w_in", "gla_w_a2", "gla_b_a", "gla_norm_g", "hg_norm_g",
        "hg_lb_logits", "w_out", "norm2_g", "w_rg", "b_rg", "w_re", "b_re", "w_exp_gate", "w_exp_up",
        "w_exp_down", "w_ada_final", "b_ada_final", "norm_f_g"]


def kernel(**inputs):
    import numpy as np
    import concourse.bacc as bacc
    from concourse.bass_utils import run_bass_kernel_spmd

    nc = bacc.Bacc("TRN2", target_bir_lowering=False, num_devices=1)
    arrays, args = {}, []
    for name in _INS:
        a = np.ascontiguousarray(inputs[name])
        arrays[f"in_{name}"] = a
        args.append(nc.dram_tensor(f"in_{name}", a.shape, mybir.dt.from_np(a.dtype), kind="ExternalInput").ap())
    shape = np.asarray(inputs["x"]).shape
    args.append(nc.dram_tensor("out_x", shape, F32, kind="ExternalOutput").ap())
    layer_kernel(nc, *args)
    r = run_bass_kernel_spmd(nc, [arrays], core_ids=[0])
    return r.results[0]["out_x"]
```

```python
from contextlib import ExitStack

import concourse.bass as bass
from concourse import mybir

F32 = mybir.dt.float32
F32R = mybir.dt.float32r
BF16 = mybir.dt.bfloat16
I32 = mybir.dt.int32
U32 = mybir.dt.uint32
U8 = mybir.dt.uint8
ALU = mybir.AluOpType
ACT = mybir.ActivationFunctionType
AX = mybir.AxisListType.X

P = 128
EPS = 1e-6
C = 96
BIG = 1e30
GMIN = -40.0
LEVELS = [64, 32, 16, 8, 4]
NL = len(LEVELS)
KB = 1024
BASE = 16512


def layer_kernel(nc, x, c, w_ada, b_ada, norm1_g, w_in, gla_w_a2, gla_b_a, gla_norm_g, hg_norm_g,
                 hg_lb_logits, w_out, norm2_g, w_rg, b_rg, w_re, b_re, w_exp_gate, w_exp_up,
                 w_exp_down, w_ada_final, b_ada_final, norm_f_g, out):
    T, D = x.shape[1], x.shape[2]
    NT = T // P
    KD = D // P
    HALF = 512
    NE, FF = w_exp_gate.shape[1], w_exp_gate.shape[3]
    NG = w_rg.shape[2]
    EG = NE // NG
    FB = FF // P
    RANK = gla_w_a2.shape[1]
    NX = (2 * T) // C
    MX = (T - 1) // C
    NSLOT = (NE + NX) * C
    FILL = -(-NX * C // NT)
    GLA_UNITS, HG_UNITS = 2, 4
    UNITS = GLA_UNITS + HG_UNITS
    GQ, GK, GV, GG, GA_COL, HQ, HF, HI, HG = 0, 256, 512, 1024, 1536, 1552, 2064, 2576, 3088

    def is_gla(u):
        return u < GLA_UNITS

    def heads(u):
        return 2 if is_gla(u) else 1

    WSLOTS = 4
    chunk_col, chunk_slot, chunk_at = [], [], {}

    def k_chunks(u):
        if is_gla(u):
            return [("q", 0, GQ + u * P), ("k", 1, GK + u * P)]
        h = u - GLA_UNITS
        return [("q", 0, HQ + h * P), ("f", 1, HF + h * P)]

    def gv_chunks(u):
        if is_gla(u):
            return [("g0", 2, GG + 2 * u * P), ("g1", 3, GG + (2 * u + 1) * P),
                    ("v0", 0, GV + 2 * u * P), ("v1", 1, GV + (2 * u + 1) * P)]
        h = u - GLA_UNITS
        return [("g0", 2, HG + h * P), ("v0", 3, HI + h * P)]

    for u in range(UNITS):
        for name, slot, col in k_chunks(u) + gv_chunks(u):
            chunk_at[(u, name)] = len(chunk_col)
            chunk_col.append(col)
            chunk_slot.append(slot)

    jobs = []

    def k_jobs(u):
        if is_gla(u):
            if u == 0:
                return [("q", 0), ("k", 0), ("ga", 0), ("q", 1), ("k", 1), ("ga", 1), ("a", 0), ("a", 1)]
            return [("q", 0), ("q", 1), ("k", 0), ("k", 1), ("a", 0), ("a", 1)]
        return [("q", 0), ("q", 1), ("f", 0), ("f", 1)]

    def gv_jobs(u):
        return [("gv", i) for i in range(NT if is_gla(u) else NT // 2)]

    def gv_names(u, i):
        if is_gla(u):
            return ["v0", "v1"] if i < NT // 2 else ["g0", "g1"]
        return ["g0", "v0"]

    ADA = {"sh1": (0, 0), "sc1": (0, D), "gt1": (0, 2 * D), "sh2": (0, 3 * D), "sc2": (0, 4 * D),
           "gt2": (0, 5 * D), "shf": (1, 0), "scf": (1, D)}
    EARLY = ["sc1", "sh1"]
    UNIT_ADA = ["gt1", "sh2", "sc2", "gt2", "shf", "scf"]

    def row_jobs(v):
        return [("row", v, 0), ("row", v, 1)]

    out_order = [("wo", 0)]
    for t in range(1, NT):
        out_order.append(("wo", t))
        if t == NT // 2 + 1:
            out_order.append(("lg", 0))
        out_order.append(("h2T", t - 1))
        if t == NT // 2 + 2:
            out_order.append(("lgT", 0))
        if t == NT // 2 + 3:
            out_order.append(("rank", 0))
    out_order += [("h2T", NT - 1), ("lg", 1), ("lgT", 1), ("rank", 1)]

    jobs += [("col", v) for v in EARLY]
    start_order = []
    for j in k_jobs(0)[0:3]:
        start_order += [j, None]
    start_order.append(None)
    jobs += [("xT", 0, k) for k in range(KD)]
    k = 0
    for j in start_order:
        jobs += [("xT", 1, k), ("xT", 1, k + 1)] if j is None else [(0,) + j]
        k += 2 * (j is None)
    jobs += [(0,) + j for j in k_jobs(0)[3:]]
    jobs += [(0,) + j for j in gv_jobs(0)]
    for u in range(UNITS):
        if u + 1 < UNITS:
            jobs += [(u + 1,) + j for j in k_jobs(u + 1)]
        jobs += [("khT", u, 0), ("khT", u, 1)]
        jobs.append(("col", UNIT_ADA[u]))
        if u + 1 < UNITS:
            jobs += [(u + 1,) + j for j in gv_jobs(u + 1)]
        jobs += [("oT", u, h, g) for h in range(heads(u)) for g in range(2)]
    jobs += row_jobs("gt1")
    for kind, i in out_order:
        jobs += [(kind, i, 0), (kind, i, 1)] if kind in ("wo", "h2T") else [(kind, i)]
    jobs += row_jobs("gt2") + row_jobs("shf") + row_jobs("scf")
    number = {j: n for n, j in enumerate(jobs)}
    assert len(number) == len(jobs)

    steps, step_at = [], {}
    for u in range(UNITS):
        for t in range(NT):
            for h in range(heads(u)):
                step_at[(u, t, h)] = len(steps)
                steps.append((u, t, h))
    first_step = [step_at[(u, 0, 0)] for u in range(UNITS)] + [len(steps)]
    ITEMS = NL + 3

    with ExitStack() as ctx:
        def at(name, kb, shape, dt=F32):
            return nc.alloc_sbuf_tensor_at(name, shape, dt, offset=BASE + int(kb * KB))

        def sem(name):
            return ctx.enter_context(nc.semaphore(name))

        HT = at("HT", 0, [P, KD, T], F32R)
        HFULL = at("HFULL", 32, [P, KD, T])
        HL = at("HL", 32, [P, KD, T], F32R)
        X1 = at("X1", 0, [P, NT, D])
        OT = at("OT", 32, [P, 8, T])
        WGA = at("WGA", 196.5, [P, KD, RANK])
        WGH = at("WGH", 197.0, [P, KD, RANK], F32R)
        WGL = at("WGL", 197.5, [P, KD, RANK], F32R)
        WA2 = at("WA2", 198, [RANK, 2 * P])
        BCOL = at("BCOL", 199, [P, len(ADA), KD])
        GCOL = at("GCOL", 199.25, [P, 3, KD])
        C8 = at("C8", 199.375, [P, KD])
        IOI = at("IOI", 130, [P, P], I32)
        IOJ = at("IOJ", 130.5, [P, P], I32)
        XOR = at("XOR", 131, [P, P], I32)
        MT1 = at("MT1", 131.5, [P, P])
        MT2 = at("MT2", 132, [P, P])
        WH = at("WH", 64, [P, WSLOTS, KD, P], F32R)
        WF = at("WF", 80, [P, WSLOTS, KD, P])
        WL = at("WL", 80, [P, WSLOTS, KD, P], F32R)
        WOUT = at("WOUT", 64, [P, 8, D])
        Q = at("Q", 96, [P, 2, T])
        K = at("K", 104, [P, 2, T])
        FD = at("FD", 112, [P, T])
        B = at("B", 116, [P, T])
        GVB = at("GVB", 120, [P, NT, HALF])
        GVH = at("GVH", 120, [P, NT, 2 * P])
        AST = at("AST", 96, [P, 8, D])
        XT = at("XT", 96, [P, 2, D])
        XN = at("XN", 184, [P, 2, D])
        H2T = at("H2T", 104, [P, KD, HALF])
        XR = at("XR", 136, [P, NT, D])
        XL = at("XL", 136, [P, NL, T])
        BA = at("BA", 156, [P, T])
        BB = at("BB", 160, [P, T])
        QE = at("QE", 164, [P, T])
        KH = at("KH", 168, [P, NT, P])
        KHT = at("KHT", 172, [P, T])
        O = at("O", 172, [P, 2, NT, P])
        GA = at("GA", 180, [RANK, T])
        OTS = [at(f"OTS{i}", kb, [P, HALF]) for i, kb in enumerate((180, 182, 204.25))]
        AR = at("AR", 184, [P, 2, D])
        ACC = at("ACC", 192, [P, D])
        IDENT = at("IDENT", 196, [P, P])
        ACCB = at("ACCB", 180, [P, D])
        GT1B = at("GT1B", 196.5, [P, D])
        MASK = at("MASK", 200.5, [P, NL + 1, P], U8)
        GT2B = at("GT2B", 201.25, [P, D])
        RESET = at("RESET", 201.25, [P, T], U8)
        AT2 = at("AT2", 202.25, [P, 2, P])
        S = at("S", 203.25, [P, 2, P])
        SG = at("SG", 204.25, [P, HALF])
        ONESF = at("ONESF", 206.25, [P, P])
        UT = at("UT", 206.75, [P, P], BF16)
        small_at = [207.0]

        def small(name, shape, dt=F32):
            n = 1
            for s_ in shape[1:]:
                n *= s_
            h_ = at(name, small_at[0], shape, dt)
            small_at[0] += ((n * 4 + 31) // 32) * 32 / KB
            return h_

        GS1 = small("GS1", [P, KD])
        SH1 = small("SH1", [P, KD])
        GS2 = small("GS2", [P, KD])
        SH2 = small("SH2", [P, KD])
        GT1 = small("GT1", [P, KD])
        GT2 = small("GT2", [P, KD])
        SHC = small("SHC", [P, KD])
        GSC = small("GSC", [P, KD])
        CA = small("CA", [P, KD])
        LB = small("LB", [P, 3, HG_UNITS])
        BAN = small("BAN", [P, 2, GLA_UNITS])
        GN = small("GN", [P, 2])
        SS = small("SS", [P, 16])
        RR = small("RR", [P, 16])
        TA = small("TA", [P, 16])
        EBL = small("EBL", [P, NT])
        LBT = small("LBT", [P, 2, HG_UNITS])
        TICK = small("TICK", [P, 1])
        TOCK = small("TOCK", [P, 1])
        assert BASE + small_at[0] * KB <= nc.sbuf_usable_end
        SHF = at("SHF", 80, [P, D])
        GSF = at("GSF", 84, [P, D])
        XGT = at("XGT", 88, [P, 2, KD, C])
        YB = at("YB", 96, [P, 2, D])
        WGU = [at(f"WGU{s}", o, [P, 2, KD, FF]) for s, o in enumerate([136, 160, 32, 56])]
        WDN = [at(f"WDN{s}", o + 16, [P, FB, D]) for s, o in enumerate([136, 160, 32, 56])]
        XG = at("XG", 120, [P, 4, D])
        SIL = at("SIL", 118, [P, 2, FB, C])
        ATT = at("ATT", 116, [P, 2, FB, C])
        WRT = at("WRT", 201.25, [P, KD, NG + NE])
        LGS = at("LGS", 192, [NG + NE, T])
        rt = [120.0]

        def rtmp(name, shape, dt=F32):
            n = 1
            for s_ in shape[1:]:
                n *= s_
            h_ = at(name, rt[0], shape, dt)
            rt[0] += ((n * 4 + 31) // 32) * 32 / KB
            return h_

        LG = rtmp("LG", [P, NT, NG + NE])
        EM = rtmp("EM", [P, NT, NE])
        SCR = rtmp("SCR", [P, NT, NE])
        M1 = rtmp("M1", [P, NT, NE])
        M2 = rtmp("M2", [P, NT, NE])
        MB = rtmp("MB", [P, NT * NE], BF16)
        RK = rtmp("RK", [P, NT, NE])
        CNT = rtmp("CNT", [P, NE])
        OHG = rtmp("OHG", [P, NT, NG])
        GD = rtmp("GD", [P, NT, NG])
        PEN = rtmp("PEN", [P, NT, NG])
        V8 = rtmp("V8", [P, 10, NT])
        NXE = rtmp("NXE", [P, NE])
        XINC = rtmp("XINC", [P, NE])
        DX = rtmp("DX", [P, NE])
        CMP = rtmp("CMP", [1, NX, NE])
        XEF = rtmp("XEF", [1, NX])
        assert rt[0] <= 136
        PR = at("PR", 205.75, [P, NE])
        EC = at("EC", 205.875, [P, NE])
        ONEB = at("ONEB", 200.5, [P, P], BF16)
        XS = at("XS", 206.0, [1, NX])
        BR = at("BR", 205.25, [P, NG + NE])
        WPAIR = at("WPAIR", 205.5, [P, 2, NT])
        SLOTP = at("SLOTP", 205.6875, [P, 2, NT], U32)
        SLOT = at("SLOT", 205.5625, [P, 2, NT], U32)
        TID = at("TID", 205.625, [P, NT], U32)
        IDX = at("IDX", 200.5, [C, NE + NX], U32)
        IDXC = at("IDXC", 200.75, [C, 4], U32)
        XE = at("XE", 200.8125, [1, NX], I32)
        NXI = at("NXI", 200.9375, [1, 1], I32)
        ZT = at("ZT", 133, [C, NE + NX], U32)
        YG = at("YG", 32, [P, 4, 2, D])
        OUTT = at("OUTT", 64, [P, 2, D])

        PS = ctx.enter_context(nc.psum_tensor("PS", [P, 8 * HALF], F32))
        PJ = [PS[:, i * HALF:(i + 1) * HALF] for i in range(2)]
        LV = [PS[:, (2 + 2 * i) * HALF:(4 + 2 * i) * HALF] for i in range(2)]
        OP = [PS[:, (6 + i) * HALF:(6 + i) * HALF + P] for i in range(2)]
        TP = PS[:, 0:2 * HALF].rearrange("p (b n) -> p b n", b=2)
        SQ = PS[:, 2 * HALF:4 * HALF]
        GU = [PS[:, (2 + i) * HALF:(3 + i) * HALF] for i in range(2)]
        YP = [PS[:, (4 + 2 * i) * HALF:(6 + 2 * i) * HALF] for i in range(2)]

        xn_d = nc.dram_tensor("xn_rows", [T, D], F32, kind="Internal").ap()
        tab_d = nc.dram_tensor("slot_tokens", [NSLOT, 1], U32, kind="Internal").ap()
        ot_d = nc.dram_tensor("head_outputs", [7, P, T], F32, kind="Internal").ap()
        ys_d = nc.dram_tensor("expert_rows", [NSLOT, D], F32, kind="Internal").ap()

        x_in = [sem(f"x_in{i}") for i in range(NT // 2)]
        c_in = sem("c_in")
        small_in = sem("small_in")
        wga_in = sem("wga_in")
        br_in = sem("br_in")
        ast_in = [sem(f"ast_in{i}") for i in range(8)]
        ar_in = [sem(f"ar_in{i}") for i in range(2)]
        ar_used = sem("ar_used")
        ast_used = sem("ast_used")
        w_raw = [sem(f"w_raw{i}") for i in range(WSLOTS)]
        wh_ready = sem("wh_ready")
        wl_ready = sem("wl_ready")
        wg_high = sem("wg_high")
        wg_low = sem("wg_low")
        xh_ready = sem("xh_ready")
        xl_ready = sem("xl_ready")
        ot_st = [sem(f"ot_st{i}") for i in range(3)]
        ot_in = sem("ot_in")
        ios = sem("iotas")
        consts = sem("consts")
        pj_ready = sem("pj_ready")
        pj_free = [sem("pj_free0"), sem("pj_free1")]
        rr_ready = sem("rr_ready")
        rr_h = sem("rr_h")
        xr_ready = sem("xr_ready")
        ca_ready = sem("ca_ready")
        mod1_ready = sem("mod1_ready")
        f_ready = sem("f_ready")
        f_used = sem("f_used")
        kf_ready = sem("kf_ready")
        lf_ready = sem("lf_ready")
        b_ready = sem("b_ready")
        e_sub = sem("e_sub")
        e_exp = sem("e_exp")
        e_mul = sem("e_mul")
        lv_ready = sem("lv_ready")
        at_ready = sem("at_ready")
        o_ready = sem("o_ready")
        o_free = sem("o_free")
        silu_g = sem("silu_g")
        og_ready = sem("og_ready")
        dve = sem("dve_order")
        act_o = sem("act_order")
        wout_in = sem("wout_in")
        xt_in = [sem("xt_in0"), sem("xt_in1")]
        xn_st = [sem("xn_st0"), sem("xn_st1")]
        x1_ready = sem("x1_ready")
        ss2 = sem("ss2")
        r2 = sem("r2")
        xn_ready = sem("xn_ready")
        h2_ready = sem("h2_ready")
        wrt_in = sem("wrt_in")
        gd_ready = sem("gd_ready")
        eg_ready = sem("eg_ready")
        mb_ready = sem("mb_ready")
        slots_ready = sem("slots_ready")
        nx_ready = sem("nx_ready")
        routed = sem("routed")
        table2_st = sem("table2_st")
        table_done = sem("table_done")
        table_zero = sem("table_zero")
        zt_ready = sem("zt_ready")
        table_st = sem("table_st")
        idx_in = sem("idx_in")
        wexp_in = [sem(f"wexp_in{s}") for s in range(4)]
        xg_in = [sem(f"xg_in{s}") for s in range(4)]
        idxc = sem("idxc")
        t_ready = sem("t_ready")
        xgt_scaled = sem("xgt_scaled")
        xxgt_scaled = sem("xxgt_scaled")
        xgt_ready = sem("xgt_ready")
        gu_ready = sem("gu_ready")
        sil_ready = sem("sil_ready")
        att_ready = sem("att_ready")
        y_ready = sem("y_ready")
        y_ev = sem("y_ev")
        y_st = [sem("y_st0"), sem("y_st1")]
        xw_in, xxg_in, xt_ready, xxgt, xgu, xsil, xatt, xy, xyev, x_done, xidx = (
            sem(n) for n in ("xw_in", "xxg_in", "xt_ready", "xxgt", "xgu", "xsil", "xatt", "xy", "xyev",
                             "x_done", "xidx"))
        extras_done = sem("extras_done")
        ys_filled = sem("ys_filled")
        yg_in = [sem(f"yg_in{s}") for s in range(4)]
        x2_ready = sem("x2_ready")
        ss3 = sem("ss3")
        out_scaled = sem("out_scaled")
        out_ready = sem("out_ready")
        out_st = [sem("out_st0"), sem("out_st1")]

        x_rows = x.rearrange("a (t p) d -> p (a t) d", p=P)
        out_rows = out.rearrange("a (t p) d -> p (a t) d", p=P)
        win = w_in.rearrange("a (p k) n -> p (a k) n", k=KD)
        wo_rows = w_out.rearrange("a (v p) n -> p (a v) n", p=P)
        ada_w = [w_ada.rearrange("a (p k) n -> p (a k) n", k=KD), w_ada_final.rearrange("(p k) n -> p k n", k=KD)]

        def ada_slice(v, k):
            src, col = ADA[v]
            return ada_w[src][:, k, col:col + D]

        def col_view(vec):
            return vec.rearrange("a (p k) -> p (a k)", k=KD)

        block = ctx.enter_context(nc.Block())

        @block.sync
        def _(sp):
            def load_x(g):
                sp.dma_start(XR[:, 2 * g:2 * g + 2, :], x_rows[:, 2 * g:2 * g + 2, :]).then_inc(x_in[g], 16)

            def load_early(v):
                for k in range(KD):
                    n = EARLY.index(v) * KD + k
                    if n >= 8:
                        sp.wait_ge(ast_used, n - 7)
                    sp.dma_start(AST[:, n % 8, :], ada_slice(v, k)).then_inc(ast_in[n % 8], 16)

            def load_chunk(n):
                slot, col = chunk_slot[n], chunk_col[n]
                sp.dma_start(WF[:, slot, :, :], win[:, :, col:col + P]).then_inc(w_raw[slot], 16)

            load_early("sc1")
            load_x(0)
            load_x(1)
            load_early("sh1")
            for n in range(2):
                load_chunk(n)
            for g in range(2, NT // 2):
                load_x(g)
            for n in range(2, WSLOTS):
                load_chunk(n)
            last_use = {}
            for u in range(UNITS):
                for name in ("q", "k", "f"):
                    if (u, name) in chunk_at:
                        last_use[chunk_at[(u, name)]] = number[(u, name, 1)]
                for job in gv_jobs(u):
                    for name in gv_names(u, job[1]):
                        last_use[chunk_at[(u, name)]] = number[(u,) + job]
            for n in range(WSLOTS, len(chunk_col)):
                before = max(m for m in range(n) if chunk_slot[m] == chunk_slot[n])
                sp.wait_ge(pj_ready, last_use[before] + 1)
                load_chunk(n)
            sp.wait_ge(pj_ready, number[(UNITS - 1,) + gv_jobs(UNITS - 1)[-1]] + 1)
            for i in range(3):
                sp.wait_ge(ot_st[i], 16 * ((14 - i + 2) // 3))
            for v in range(8):
                if v >= 1:
                    sp.wait_ge(wout_in, 16 * v)
                sp.dma_start(WOUT[:, v, :], wo_rows[:, v, :]).then_inc(wout_in, 16)
                if v < 7:
                    sp.dma_start(OT[:, v, :], ot_d[v]).then_inc(ot_in, 16)
            sp.wait_ge(e_mul, ITEMS * UNITS)
            for t in range(2):
                sp.dma_start(XT[:, t, :], x_rows[:, t, :]).then_inc(xt_in[t], 16)
            sp.wait_ge(pj_ready, number[("oT", UNITS - 1, 0, 1)] + 1)

            def load_gate_up(e, s, done):
                sp.dma_start(WGU[s][:, 0], w_exp_gate[0, bass.ds(e, 1)].rearrange("a (p k) f -> p (a k) f", k=KD)).then_inc(done, 16)
                sp.dma_start(WGU[s][:, 1], w_exp_up[0, bass.ds(e, 1)].rearrange("a (p k) f -> p (a k) f", k=KD)).then_inc(done, 16)

            def load_down(e, s, done):
                sp.dma_start(WDN[s][:, :, :], w_exp_down[0, bass.ds(e, 1)].rearrange("a (j p) n -> p (a j) n", p=P)).then_inc(done, 16)

            def load_expert(e, s, done):
                load_gate_up(e, s, done)
                load_down(e, s, done)

            load_expert(0, 0, wexp_in[0])
            load_expert(1, 1, wexp_in[1])
            for t in range(NT):
                sp.wait_ge(xn_ready, t + 1)
                sp.dma_start(xn_d[t * P:(t + 1) * P, :], XN[:, t % 2, :]).then_inc(xn_st[t % 2], 16)
                if t + 2 < NT:
                    sp.dma_start(XT[:, t % 2, :], x_rows[:, t + 2, :]).then_inc(xt_in[t % 2], 16)
            sp.wait_ge(pj_ready, number[("wo", NT - 1, 1)] + 1)
            load_expert(2, 2, wexp_in[2])
            load_expert(3, 3, wexp_in[3])
            sp.wait_ge(table_done, 1)
            with nc.allow_non_contiguous_dma(reason="one index a slot"):
                sp.dma_start(IDX[:, :], tab_d.rearrange("(s c) a -> c (s a)", c=C)).then_inc(idx_in, 16)
            with sp.Fori(1, NE // 4) as it:
                for s in range(4):
                    sp.wait_ge(gu_ready, 4 * it + (s - 3))
                    load_gate_up(4 * it + s, s, wexp_in[s])
                    sp.wait_ge(y_ready, 4 * it + (s - 3))
                    load_down(4 * it + s, s, wexp_in[s])
            sp.wait_ge(y_ready, NE)
            sp.wait_ge(nx_ready, 1)
            nx = sp.value_load(NXI[:, :], min_val=0, max_val=NX)
            with sp.If(nx > 0):
                sp.sem_inc(x_done, 16)
                with sp.Fori(0, NX) as i:
                    with sp.If(nx > i):
                        sp.wait_ge(x_done, 16 * i + 16)
                        e = sp.value_load(XE[:, bass.ds(i, 1)], min_val=0, max_val=NE - 1)
                        load_expert(e, 0, xw_in)
                sp.nop()
            for t in range(NT):
                sp.wait_ge(out_ready, t + 1)
                sp.dma_start(out_rows[:, t, :], OUTT[:, t % 2, :]).then_inc(out_st[t % 2], 16)
            for s in range(2):
                sp.wait_ge(out_st[s], 16 * NT // 2)

        @block.gpsimd
        def _(pool):
            nc.gpsimd.memset(IDENT[:], 0.0).then_inc(ios, 1)
            nc.gpsimd.memset(ONESF[:], 1.0).then_inc(ios, 1)
            nc.gpsimd.memset(ZT[:], T).then_inc(zt_ready, 1)
            pool.iota(IOI[:], [[1, P]], base=0, channel_multiplier=0).then_inc(ios, 1)
            pool.iota(IOJ[:], [[0, P]], base=0, channel_multiplier=1).then_inc(ios, 1)
            pool.wait_ge(ios, 4)
            nc.gpsimd.affine_select(out=IDENT[:], in_=IDENT[:], compare_op=ALU.not_equal, fill=1.0, base=0,
                                    pattern=[[-1, P]], channel_multiplier=1).then_inc(ios, 1)
            pool.wait_ge(zt_ready, 1)
            pool.dma_start(tab_d.rearrange("(p n) a -> p (n a)", p=C), ZT[:]).then_inc(table_zero, 16)
            pool.wait_ge(x_in[NT // 2 - 1], 16)
            n = 0
            for v in UNIT_ADA:
                for k in range(KD):
                    if n >= 2:
                        pool.wait_ge(ar_used, n - 1)
                    pool.dma_start(AR[:, n % 2, :], ada_slice(v, k)).then_inc(ar_in[n % 2], 16)
                    n += 1
            pool.wait_ge(og_ready, UNITS)
            pool.wait_ge(ot_st[2], 16 * 4)
            pool.dma_start(BR[:, 0:NG], b_rg.to_broadcast([P, NG])).then_inc(br_in, 16)
            pool.dma_start(BR[:, NG:], b_re.to_broadcast([P, NE])).then_inc(br_in, 16)
            pool.iota(TID[:], [[P, NT]], base=0, channel_multiplier=1).then_inc(ios, 1)
            pool.iota(PR[:], [[-1, NE]], base=NE, channel_multiplier=0,
                      allow_small_or_imprecise_dtypes=True).then_inc(ios, 1)
            pool.iota(EC[:], [[C, NE]], base=0, channel_multiplier=0,
                      allow_small_or_imprecise_dtypes=True).then_inc(ios, 1)
            pool.iota(XS[:], [[1, NX]], base=0, channel_multiplier=0,
                      allow_small_or_imprecise_dtypes=True).then_inc(ios, 1)
            nc.gpsimd.memset(ONEB[:], 1.0).then_inc(ios, 1)
            for t in range(NT):
                pool.wait_ge(pj_ready, number[("wo", t, 0)] + 1)
                lo, hi = FILL * t, min(FILL * (t + 1), NX * C)
                pool.dma_start(ys_d[NE * C + lo:NE * C + hi, :], x[0, 0:hi - lo, :]).then_inc(ys_filled, 16)
            pool.wait_ge(table_zero, 16)
            pool.wait_ge(ios, 10)
            for g in range(2):
                pool.wait_ge(slots_ready, g + 1)
                for k in range(2):
                    for t in range(g * NT // 2, (g + 1) * NT // 2):
                        pool.indirect_dma_start(
                            out=tab_d, out_offset=bass.IndirectOffsetOnAxis(ap=SLOTP[:, k, t:t + 1], axis=0),
                            in_=TID[:, t:t + 1], in_offset=None, bounds_check=NSLOT - 1,
                            oob_is_err=False).then_inc(table_st, 16)
            pool.wait_ge(table_st, 16 * 2 * NT)
            pool.wait_ge(nx_ready, 1)
            nx = pool.value_load(NXI[:, :], min_val=0, max_val=NX)
            with pool.If(nx > 0):
                for k in range(2):
                    for t in range(NT):
                        pool.indirect_dma_start(
                            out=tab_d, out_offset=bass.IndirectOffsetOnAxis(ap=SLOT[:, k, t:t + 1], axis=0),
                            in_=TID[:, t:t + 1], in_offset=None).then_inc(table2_st, 16)
                pool.wait_ge(table2_st, 16 * 2 * NT)
            nc.gpsimd.tensor_tensor(TICK[:], IDENT[:, 0:1], IDENT[:, 0:1], ALU.add).then_inc(table_done, 1)
            pool.wait_ge(idx_in, 16)
            pool.wait_ge(routed, 1)
            for s in range(2):
                pool.wait_ge(xn_st[s], 16 * NT // 2)

            def gather(it, s, first):
                if not first:
                    pool.wait_ge(t_ready, 4 * it + (s - 3))
                nc.gpsimd.tensor_copy(IDXC[:, s:s + 1], IDX[:, bass.ds(4 * it + s, 1)]).then_inc(idxc, 1)
                pool.wait_ge(idxc, 4 * it + (s + 1))
                nc.gpsimd.tensor_tensor(TICK[:], IDENT[:, 0:1], IDENT[:, 0:1], ALU.add)
                pool.indirect_dma_start(
                    out=XG[0:C, s, :], out_offset=None, in_=xn_d,
                    in_offset=bass.IndirectOffsetOnAxis(ap=IDXC[:, s:s + 1], axis=0),
                    bounds_check=T - 1, oob_is_err=False).then_inc(xg_in[s], 16)

            for s in range(4):
                gather(0, s, True)
            with pool.Fori(1, NE // 4) as it:
                for s in range(4):
                    gather(it, s, False)
            pool.wait_ge(t_ready, NE)
            with pool.If(nx > 0):
                with pool.Fori(0, NX) as i:
                    with pool.If(nx > i):
                        pool.wait_ge(x_done, 16 * i + 16)
                        nc.gpsimd.tensor_copy(IDXC[:, 0:1], IDX[:, bass.ds(i + NE, 1)]).then_inc(xidx, 1)
                        pool.wait_ge(xidx, i + 1)
                        nc.gpsimd.tensor_tensor(TICK[:], IDENT[:, 0:1], IDENT[:, 0:1], ALU.add)
                        pool.indirect_dma_start(
                            out=XG[0:C, 0, :], out_offset=None, in_=xn_d,
                            in_offset=bass.IndirectOffsetOnAxis(ap=IDXC[:, 0:1], axis=0),
                            bounds_check=T - 1, oob_is_err=False).then_inc(xxg_in, 16)
                pool.nop()
            for s in range(2):
                pool.wait_ge(y_st[s], 16 * NE // 2)
            pool.wait_ge(extras_done, 1)
            pool.wait_ge(ys_filled, 16 * NT)
            def shift(t):
                pool.wait_ge(out_scaled, t + 1)
                nc.gpsimd.tensor_tensor(OUTT[:, t % 2, :], OUTT[:, t % 2, :], SHF[:], ALU.add).then_inc(out_ready, 1)

            for t in range(NT):
                if t >= 4:
                    pool.wait_ge(x2_ready, t - 3)
                for k in range(2):
                    pool.indirect_dma_start(
                        out=YG[:, t % 4, k, :], out_offset=None, in_=ys_d,
                        in_offset=bass.IndirectOffsetOnAxis(ap=SLOT[:, k, t:t + 1], axis=0)).then_inc(yg_in[t % 4], 16)
                if t >= 4:
                    shift(t - 4)
            for t in range(NT - 4, NT):
                shift(t)

        @block.scalar
        def _(act):
            A = nc.scalar.activation
            act.dma_start(C8[:], col_view(c)).then_inc(c_in, 16)
            act.wait_ge(c_in, 16)
            A(CA[:], C8[:], ACT.Silu).then_inc(ca_ready, 1)
            act.dma_start(BCOL[:, 0:6, :], b_ada.rearrange("a (v p k) -> p (a v) k", v=6, k=KD)).then_inc(small_in, 16)
            act.dma_start(BCOL[:, 6:8, :], b_ada_final.rearrange("(v p k) -> p v k", v=2, k=KD)).then_inc(small_in, 16)
            act.dma_start(GCOL[:, 0, :], col_view(norm1_g)).then_inc(small_in, 16)
            act.dma_start(GCOL[:, 1, :], col_view(norm2_g)).then_inc(small_in, 16)
            act.dma_start(GCOL[:, 2, :], norm_f_g.rearrange("(p k) -> p k", k=KD)).then_inc(small_in, 16)
            with nc.allow_non_contiguous_dma(reason="short vectors"):
                act.dma_start(LBT[:, :, :], hg_lb_logits.rearrange("r (h p) -> p r h", p=P)).then_inc(small_in, 16)
                act.dma_start(BAN[:, 0, :], gla_b_a.rearrange("a (u p) -> p (a u)", p=P)).then_inc(small_in, 16)
                act.dma_start(GN[:, 0:1], gla_norm_g.rearrange("a p -> p a")).then_inc(small_in, 16)
                act.dma_start(GN[:, 1:2], hg_norm_g.rearrange("a p -> p a")).then_inc(small_in, 16)
                act.dma_start(WGA[:], win[:, :, GA_COL:GA_COL + RANK]).then_inc(wga_in, 16)
            act.dma_start(WA2[:], gla_w_a2[0]).then_inc(wga_in, 16)
            act_n = [0]

            def chain(ins):
                act_n[0] += 1
                ins.then_inc(act_o, 1)
                act.wait_ge(act_o, act_n[0])

            def root_of(lo, hi, width):
                chain(A(TA[:, lo:hi], SS[:, lo:hi], ACT.Copy, scale=1.0 / width, bias=EPS))
                return A(RR[:, lo:hi], TA[:, lo:hi], ACT.Sqrt)

            def square(t):
                act.wait_ge(x_in[t // 2], 16)
                chain(A(SQ, XR[:, t, :], ACT.Square, accum_out=SS[:, t:t + 1]))

            for t in range(4):
                square(t)
            root_of(0, 4, D).then_inc(rr_ready, 1)
            act.wait_ge(table_zero, 16)

            def high(u, name):
                n = chunk_at[(u, name)]
                slot = chunk_slot[n]
                act.wait_ge(w_raw[slot], 16 * chunk_slot[0:n + 1].count(slot))
                A(WH[:, slot], WF[:, slot], ACT.Copy).then_inc(wh_ready, 1)

            def k_high(u):
                for name, _, _ in k_chunks(u):
                    high(u, name)

            high(0, "q")

            def evac(job):
                n = number[job]
                act.wait_ge(pj_ready, n + 1)
                return pj_free[n % 2]

            act.wait_ge(mod1_ready, 2)

            def x_evac(g, blocks):
                for k in blocks:
                    evac(("xT", g, k))
                    A(HT[:, k, g * HALF:(g + 1) * HALF], PJ[number[("xT", g, k)] % 2], ACT.Identity,
                      scale=GS1[:, k:k + 1], bias=SH1[:, k:k + 1]).then_inc(xh_ready, 1)
                    if g == 0 and k % 2 == 1:
                        square(4 + k // 2)

            def item(u, i):
                if i == NL + 1:
                    act.wait_ge(b_ready, u + 1)
                else:
                    act.wait_ge(e_sub, (ITEMS - 1) * u + min(i, NL + 1) + 1)
                if i < NL:
                    A(XL[:, i, :], XL[:, i, :], ACT.Exp).then_inc(e_exp, 1)
                elif i == NL:
                    chain(A(BB[:], BA[:], ACT.Exp, scale=-1.0))
                    A(BA[:], BA[:], ACT.Exp).then_inc(e_exp, 1)
                elif i == NL + 1:
                    A(QE[:], B[:], ACT.Exp).then_inc(e_exp, 1)
                else:
                    chain(A(EBL[:], B[:, P - 1::P], ACT.Exp))
                    A(KHT[:], KHT[:], ACT.Exp).then_inc(e_exp, 1)

            def k_evac(u, name, half):
                hs = slice(half * HALF, (half + 1) * HALF)
                f = evac((u, name, half))
                src = PJ[number[(u, name, half)] % 2]
                if u >= 2 and name in "qk":
                    act.wait_ge(e_mul, ITEMS * (u - 1))
                if name == "q":
                    dk = P // heads(u)
                    A(Q[:, u % 2, hs], src, ACT.Copy, scale=float(dk) ** -0.5).then_inc(f, 1)
                elif name == "k":
                    A(K[:, u % 2, hs], src, ACT.Copy).then_inc(f, 1)
                elif name == "ga":
                    A(GA[:, hs], src[0:RANK, :], ACT.Copy).then_inc(f, 1)
                elif name == "f":
                    if u > 0:
                        act.wait_ge(b_ready, u)
                    A(FD[:, hs], src, ACT.Sigmoid).then_inc(f, 1)
                else:
                    if u > 0:
                        act.wait_ge(b_ready, u)
                    if 2 * u + half > 0:
                        act.wait_ge(f_used, 2 * u + half)
                    chain(A(SG[:], src, ACT.Abs, bias=BAN[:, 0, u:u + 1]))
                    A(FD[:, hs], src, ACT.Relu, scale=-1.0, bias=BAN[:, 1, u:u + 1]).then_inc(f, 1)
                    chain(A(SG[:], SG[:], ACT.Exp, scale=-1.0))
                    A(SG[:], SG[:], ACT.Ln, bias=1.0).then_inc(f_ready, 1)

            def log_f(u):
                if not is_gla(u):
                    h = u - GLA_UNITS
                    act.wait_ge(kf_ready, h + 1)
                    A(FD[:], FD[:], ACT.Ln, scale=LB[:, 1, h:h + 1], bias=LB[:, 0, h:h + 1]).then_inc(lf_ready, 1)

            def gv_evac(u, i):
                job = (u, "gv", i)
                f = evac(job)
                src = PJ[number[job] % 2]
                tiles, part = slice(2 * (i % 4), 2 * (i % 4) + 2), i // 4
                dst = GVB[:, tiles, 2 * P * part:2 * P * (part + 1)] if is_gla(u) else GVH[:, tiles, :]
                A(dst, src.rearrange("p (t n) -> p t n", t=2), ACT.Copy).then_inc(f, 1)

            def spread(main, extra):
                done = 0
                for i, m in enumerate(main):
                    m()
                    want = len(extra) * (i + 1) // len(main)
                    while done < want:
                        extra[done]()
                        done += 1
                for e in extra[done:]:
                    e()

            x_evac(0, range(KD))
            root_of(4, 8, D).then_inc(rr_ready, 1)
            high(0, "k")
            act.wait_ge(wga_in, 32)
            A(WGH[:], WGA[:], ACT.Copy).then_inc(wg_high, 1)
            k = 0
            for j in start_order:
                if j is None:
                    x_evac(1, range(k, k + 2))
                    k += 2
                else:
                    k_evac(0, *j)
            act.wait_ge(consts, 1)
            A(LBT[:], LBT[:], ACT.Exp).then_inc(lf_ready, 1)
            for name, _, _ in gv_chunks(0)[0:2]:
                high(0, name)
            for name, half in k_jobs(0)[3:6]:
                k_evac(0, name, half)
            for name, _, _ in gv_chunks(0)[2:]:
                high(0, name)
            for name, half in k_jobs(0)[6:]:
                k_evac(0, name, half)
            its = {u: [lambda u=u, i=i: item(u, i) for i in range(ITEMS)] for u in range(UNITS)}
            spread([lambda i=i: gv_evac(0, i) for _, i in gv_jobs(0)[0:6]], its[0][:NL])
            k_high(1)
            for _, i in gv_jobs(0)[6:]:
                gv_evac(0, i)
            for name, _, _ in gv_chunks(1)[0:2]:
                high(1, name)
            for u in range(UNITS):
                rest = its[u][NL:]
                if u + 1 < UNITS:
                    ks = k_jobs(u + 1)
                    early = [j for j in ks if j[0] in ("q", "k", "ga")]
                    k_evac(u + 1, *early[0])
                    for e in rest:
                        e()
                    for j in early[1:]:
                        k_evac(u + 1, *j)
                    for j in ks[len(early):]:
                        k_evac(u + 1, *j)
                    if u == 0:
                        for name, _, _ in gv_chunks(1)[2:]:
                            high(1, name)
                else:
                    for e in rest:
                        e()
                for g in range(2):
                    f = evac(("khT", u, g))
                    A(KH[:, 4 * g:4 * g + 4, :], PJ[number[("khT", u, g)] % 2].rearrange("p (t n) -> p t n", t=4),
                      ACT.Copy).then_inc(f, 1)
                if u + 1 < UNITS:
                    log_f(u + 1)
                nh = heads(u)
                gates = GVB[:, :, 2 * P:4 * P] if is_gla(u) else GVH[:, :, 0:P]
                A(gates, gates, ACT.Silu).then_inc(silu_g, 1)
                for n in range(first_step[u], first_step[u + 1]):
                    _, t, h = steps[n]
                    act.wait_ge(o_ready, n + 1)
                    A(O[:, h, t, :], OP[n % 2], ACT.Copy)
                    A(OP[n % 2], OP[n % 2], ACT.Square, accum_out=SS[:, h * NT + t:h * NT + t + 1]).then_inc(o_free, 1)
                act.wait_ge(o_free, first_step[u + 1])
                root_of(0, nh * NT, P).then_inc(rr_h, 1)
                if 0 < u < UNITS - 2:
                    for name, _, _ in k_chunks(u + 2):
                        high(u + 2, name)
                if u + 1 < UNITS:
                    for e in its[u + 1][:NL]:
                        e()
                    act.wait_ge(og_ready, u + 1)
                    n = len(gv_jobs(u + 1)) - 2 if u == 0 else len(gv_jobs(u + 1))
                    for _, i in gv_jobs(u + 1)[0:n]:
                        gv_evac(u + 1, i)
                    if u == 0:
                        k_high(2)
                        for _, i in gv_jobs(1)[n:]:
                            gv_evac(1, i)
                for h in range(nh):
                    vb = 2 * u + h if is_gla(u) else 4 + u - GLA_UNITS
                    for g in range(2):
                        job = ("oT", u, h, g)
                        f = evac(job)
                        gain = GN[:, 0:1] if is_gla(u) else GN[:, 1:2]
                        if u == UNITS - 1:
                            A(OT[:, vb, g * HALF:(g + 1) * HALF], PJ[number[job] % 2], ACT.Copy, scale=gain).then_inc(f, 1)
                            continue
                        i = 2 * vb + g
                        if i >= 3:
                            act.wait_ge(ot_st[i % 3], 16 * (i // 3))
                        A(OTS[i % 3][:], PJ[number[job] % 2], ACT.Copy, scale=gain).then_inc(f, 1)
                        act.wait_ge(f, number[job] // 2 + 1)
                        act.dma_start(ot_d[vb, :, g * HALF:(g + 1) * HALF], OTS[i % 3][:]).then_inc(ot_st[i % 3], 16)
                if u < UNITS - 2:
                    for name, _, _ in gv_chunks(u + 2):
                        high(u + 2, name)
            def row_evac(v, dst):
                for half in range(2):
                    job = ("row", v, half)
                    f = evac(job)
                    A(dst.rearrange("p (n k) -> p k n", k=KD)[:, 4 * half:4 * half + 4, :],
                      PJ[number[job] % 2].rearrange("p (k n) -> p k n", k=4), ACT.Copy).then_inc(f, 1)

            def logits_evac(g):
                f = evac(("lg", g))
                A(LGS[:, g * HALF:(g + 1) * HALF], PJ[number[("lg", g)] % 2][0:NG + NE, :], ACT.Copy).then_inc(f, 1)

            def route_exps(g):
                hs = slice(g * NT // 2, (g + 1) * NT // 2)
                act.wait_ge(gd_ready, 2 * g + 1)
                A(GD[:, hs], GD[:, hs], ACT.Exp).then_inc(eg_ready, 1)
                act.wait_ge(gd_ready, 2 * g + 2)
                A(V8[:, 4, hs], V8[:, 3, hs], ACT.Exp).then_inc(eg_ready, 1)

            row_evac("gt1", GT1B[:])
            act.wait_ge(og_ready, UNITS)
            act.dma_start(WRT[:, :, 0:NG], w_rg.rearrange("a (p k) n -> p (a k) n", k=KD)).then_inc(wrt_in, 16)
            act.dma_start(WRT[:, :, NG:], w_re.rearrange("a (p k) n -> p (a k) n", k=KD)).then_inc(wrt_in, 16)
            for t in range(NT):
                act.wait_ge(x1_ready, t + 1)
                chain(A(SQ, X1[:, t, :], ACT.Square, accum_out=SS[:, t:t + 1]))
                root_of(t, t + 1, D).then_inc(ss2, 1)
                if t == NT // 2 + 1:
                    logits_evac(0)
                act.wait_ge(r2, t + 1)
                if t >= 2:
                    act.wait_ge(xn_st[t % 2], 16 * (t // 2))
                    act.wait_ge(pj_ready, number[("h2T", t - 2, 1)] + 1)
                A(XN[:, t % 2, :], X1[:, t, :], ACT.Copy, scale=RR[:, t:t + 1]).then_inc(xn_ready, 1)
                if t == NT - 2:
                    route_exps(0)
            logits_evac(1)
            route_exps(1)
            row_evac("gt2", GT2B[:])
            row_evac("shf", SHF[:])
            row_evac("scf", GSF[:])

            def store(m, par, row):
                act.wait_ge(y_ev, m + 1)
                act.dma_start(ys_d[bass.ds(row, C), :], YB[0:C, par, :]).then_inc(y_st[par], 16)

            def gates_up(it, s, first):
                n = 4 * it + s
                act.wait_ge(gu_ready, n + 1)
                if not (first and s < 2):
                    act.wait_ge(att_ready, 4 * it + (s - 1))
                A(SIL[:, s % 2], GU[s % 2][:, 0:FB * C].rearrange("p (j c) -> p j c", j=FB), ACT.Silu).then_inc(sil_ready, 1)
                if not (first and s == 0):
                    store(4 * it + (s - 1), (s + 1) % 2, (4 * it + (s - 1)) * C)

            for s in range(4):
                gates_up(0, s, True)
            with act.Fori(1, NE // 4) as it:
                for s in range(4):
                    gates_up(it, s, False)
            store(NE - 1, 1, (NE - 1) * C)
            nx = act.value_load(NXI[:, :], min_val=0, max_val=NX)
            for s in range(2):
                act.wait_ge(y_st[s], 16 * NE // 2)
            act.wait_ge(ys_filled, 16 * NT)
            with act.If(nx > 0):
                with act.Fori(0, NX) as i:
                    with act.If(nx > i):
                        act.wait_ge(xgu, i + 1)
                        A(SIL[:, 0], GU[0][:, 0:FB * C].rearrange("p (j c) -> p j c", j=FB), ACT.Silu).then_inc(xsil, 1)
                        act.wait_ge(xyev, i + 1)
                        act.dma_start(ys_d[bass.ds((i + NE) * C, C), :], YB[0:C, 0, :]).then_inc(x_done, 16)
                        act.wait_ge(x_done, 16 * i + 32)
                        A(TOCK[:], RR[:, 0:1], ACT.Copy)
                act.nop()
            act.sem_inc(extras_done, 1)
            for t in range(NT):
                act.wait_ge(x2_ready, t + 1)
                chain(A(SQ, X1[:, t, :], ACT.Square, accum_out=SS[:, t:t + 1]))
                root_of(t, t + 1, D).then_inc(ss3, 1)

        @block.vector
        def _(v_):
            V = nc.vector
            cnt = [0]

            def link(ins):
                cnt[0] += 1
                ins.then_inc(dve, 1)
                v_.wait_ge(dve, cnt[0])

            def inverse(lo, hi):
                r, m = RR[:, lo:hi], TA[:, lo:hi]
                link(V.reciprocal(r, r))
                link(V.tensor_tensor(m, m, r, ALU.mult))
                link(V.tensor_tensor(m, m, r, ALU.mult))
                link(V.tensor_scalar(m, m, -0.5, 1.5, ALU.mult, ALU.add))
                return V.tensor_tensor(r, r, m, ALU.mult)

            v_.wait_ge(ca_ready, 1)

            ada_n = [0]
            LAST_SLICES = 6

            def add_slice(w, arrived, count, acc, k, used, n):
                v_.wait_ge(arrived, count)
                if k == 0:
                    i = V.tensor_scalar(acc, w, CA[:, 0:1], None, ALU.mult)
                else:
                    i = V.scalar_tensor_tensor(out=acc, in0=w, scalar=CA[:, k:k + 1], in1=acc,
                                               op0=ALU.mult, op1=ALU.add)
                i.then_inc(used, 1)
                v_.wait_ge(used, n + 1)

            def unit_slice():
                n = ada_n[0]
                ada_n[0] += 1
                add_slice(AR[:, n % 2, :], ar_in[n % 2], 16 * (n // 2 + 1), ACC[:], n % KD, ar_used, n)

            def column(v, dst, gcol=None):
                n = number[("col", v)]
                v_.wait_ge(pj_ready, n + 1)
                V.tensor_tensor(dst, PJ[n % 2][:, 0:KD], BCOL[:, list(ADA).index(v), :], ALU.add).then_inc(pj_free[n % 2], 1)
                v_.wait_ge(pj_free[n % 2], n // 2 + 1)
                if gcol is not None:
                    link(V.scalar_tensor_tensor(out=dst, in0=dst, scalar=1.0, in1=gcol, op0=ALU.add, op1=ALU.mult))

            COLUMN = {"gt1": (GT1[:], None), "sh2": (SH2[:], None), "sc2": (GS2[:], GCOL[:, 1, :]),
                      "gt2": (GT2[:], None), "shf": (SHC[:], None), "scf": (GSC[:], GCOL[:, 2, :])}

            def early_slices(i, acc, ks):
                for k in ks:
                    n = i * KD + k
                    add_slice(AST[:, n % 8, :], ast_in[n % 8], 16 * (n // 8 + 1), acc[:], k, ast_used, n)

            def scale_rows(g):
                v_.wait_ge(rr_ready, g + 1)
                link(inverse(4 * g, 4 * g + 4))
                for t in range(4 * g, 4 * g + 4):
                    V.tensor_scalar(XR[:, t, :], XR[:, t, :], RR[:, t:t + 1], None, ALU.mult).then_inc(xr_ready, 1)

            early_slices(0, ACC, range(KD))
            early_slices(1, ACCB, range(2))
            scale_rows(0)
            early_slices(1, ACCB, range(2, KD))
            v_.wait_ge(small_in, 16 * 9)
            column("sc1", GS1[:], GCOL[:, 0, :])
            v_.sem_inc(mod1_ready, 1)
            column("sh1", SH1[:])
            v_.sem_inc(mod1_ready, 1)
            v_.wait_ge(small_in, 16 * 9)
            link(V.tensor_scalar(BAN[:, 1, :], BAN[:, 0, :], -1.0, None, ALU.mult))
            link(V.tensor_tensor(LB[:, 0, :], LBT[:, 0, :], LBT[:, 1, :], ALU.max))
            link(V.tensor_tensor(LBT[:, 0, :], LBT[:, 0, :], LB[:, 0, :], ALU.subtract))
            V.tensor_tensor(LBT[:, 1, :], LBT[:, 1, :], LB[:, 0, :], ALU.subtract).then_inc(consts, 1)
            def low(u, name):
                n = chunk_at[(u, name)]
                slot = chunk_slot[n]
                v_.wait_ge(wh_ready, n + 1)
                V.tensor_tensor(WL[:, slot], WF[:, slot], WH[:, slot].bitcast(F32), ALU.subtract).then_inc(wl_ready, 1)

            def x_low(g):
                hs = slice(g * HALF, (g + 1) * HALF)
                for k in range(KD):
                    n = number[("xT", g, k)]
                    v_.wait_ge(xh_ready, g * KD + k + 1)
                    V.tensor_scalar(HFULL[:, k, hs], PJ[n % 2], GS1[:, k:k + 1], SH1[:, k:k + 1],
                                    ALU.mult, ALU.add).then_inc(pj_free[n % 2], 1)
                    v_.wait_ge(pj_free[n % 2], n // 2 + 1)
                    V.tensor_tensor(HL[:, k, hs], HFULL[:, k, hs], HT[:, k, hs].bitcast(F32), ALU.subtract).then_inc(xl_ready, 1)

            low(0, "q")
            x_low(0)
            low(0, "k")
            scale_rows(1)
            v_.wait_ge(wg_high, 1)
            V.tensor_tensor(WGL[:], WGA[:], WGH[:].bitcast(F32), ALU.subtract).then_inc(wg_low, 1)
            x_low(1)
            for name, _, _ in gv_chunks(0):
                low(0, name)
            v_.wait_ge(ios, 5)
            link(V.tensor_tensor(XOR[:], IOI[:], IOJ[:], ALU.bitwise_xor))
            for l, s in enumerate(LEVELS):
                link(V.tensor_single_scalar(MT1[:], XOR[:], s, op=ALU.is_ge))
                link(V.tensor_single_scalar(MT2[:], XOR[:], 2 * s, op=ALU.is_lt))
                link(V.tensor_tensor(MASK[:, l, :], MT1[:], MT2[:], ALU.mult))
            link(V.tensor_single_scalar(MT1[:], XOR[:], 4, op=ALU.is_lt))
            link(V.tensor_tensor(MT2[:], IOI[:], IOJ[:], ALU.is_ge))
            link(V.tensor_tensor(MASK[:, NL, :], MT1[:], MT2[:], ALU.mult))
            link(V.tensor_tensor(UT[:], IOI[:], IOJ[:], ALU.is_gt))
            link(V.memset(RESET[:], 1))
            link(V.memset(RESET[:, 0::P], 0))
            link(V.memset(AT2[:], 0.0))
            def level(ap, s):
                return ap.rearrange("p (c a s) -> p c a s", a=2, s=s)

            def sub(u, i):
                if i < NL:
                    s = LEVELS[i]
                    x_, b_ = level(XL[:, i, :], s), level(B[:], s)
                    nb = T // (2 * s)
                    ref = b_[:, :, 0, s - 1:s].to_broadcast([P, nb, s])
                    V.tensor_tensor(x_[:, :, 0, :], ref, b_[:, :, 0, :], ALU.subtract)
                    V.tensor_tensor(x_[:, :, 1, :], b_[:, :, 1, :], ref, ALU.subtract).then_inc(e_sub, 1)
                elif i == NL:
                    b_ = B[:].rearrange("p (c s) -> p c s", s=4)
                    V.tensor_tensor(BA[:].rearrange("p (c s) -> p c s", s=4), b_,
                                    b_[:, :, 1:2].to_broadcast([P, T // 4, 4]), ALU.subtract).then_inc(e_sub, 1)
                elif i == NL + 2:
                    b_ = B[:].rearrange("p (c s) -> p c s", s=P)
                    V.tensor_tensor(KHT[:].rearrange("p (c s) -> p c s", s=P),
                                    b_[:, :, P - 1:P].to_broadcast([P, NT, P]), b_, ALU.subtract).then_inc(e_sub, 1)

            def mul(u, i):
                v_.wait_ge(e_exp, ITEMS * u + i + 1)
                q_, k_ = Q[:, u % 2, :], K[:, u % 2, :]
                if i < NL:
                    s = LEVELS[i]
                    x_ = level(XL[:, i, :], s)
                    V.tensor_tensor(x_[:, :, 0, :], x_[:, :, 0, :], level(k_, s)[:, :, 0, :], ALU.mult)
                    V.tensor_tensor(x_[:, :, 1, :], x_[:, :, 1, :], level(q_, s)[:, :, 1, :], ALU.mult).then_inc(e_mul, 1)
                elif i == NL:
                    V.tensor_tensor(BB[:], BB[:], k_, ALU.mult)
                    V.tensor_tensor(BA[:], BA[:], q_, ALU.mult).then_inc(e_mul, 1)
                elif i == NL + 1:
                    V.tensor_tensor(QE[:], QE[:], q_, ALU.mult).then_inc(e_mul, 1)
                else:
                    V.tensor_tensor(KHT[:], KHT[:], k_, ALU.mult).then_inc(e_mul, 1)

            def decay(u):
                if is_gla(u):
                    for half in range(2):
                        hs = slice(half * HALF, (half + 1) * HALF)
                        v_.wait_ge(f_ready, 2 * u + half + 1)
                        V.tensor_tensor(FD[:, hs], FD[:, hs], SG[:], ALU.add).then_inc(f_used, 1)
                        v_.wait_ge(f_used, 2 * u + half + 1)
                        link(V.tensor_scalar(FD[:, hs], FD[:, hs], -1.0 / 16.0, GMIN, ALU.mult, ALU.max))
                else:
                    h = u - GLA_UNITS
                    for half in range(2):
                        n = number[(u, "f", half)]
                        v_.wait_ge(pj_free[n % 2], n // 2 + 1)
                    V.tensor_scalar(K[:, u % 2, :], FD[:], LB[:, 2, h:h + 1], LB[:, 1, h:h + 1],
                                    ALU.mult, ALU.add).then_inc(kf_ready, 1)
                    v_.wait_ge(lf_ready, h + 2)
                V.tensor_tensor_scan(B[:], RESET[:], FD[:], 0.0, ALU.mult, ALU.add).then_inc(b_ready, 1)
                v_.wait_ge(b_ready, u + 1)

            def attention_step(n):
                u, t, h = steps[n]
                rows = slice(64 * h, 64 * h + 64) if is_gla(u) else slice(0, P)
                lv, a = LV[n % 2], AT2[:, n % 2, :]
                v_.wait_ge(lv_ready, n + 1)
                if n >= 2:
                    v_.wait_ge(o_ready, n - 1)
                for l, s in enumerate(LEVELS):
                    src = lv[:, l * P:(l + 1) * P]
                    link(V.copy_predicated(level(a, s)[:, :, 1, :], level(MASK[:, l, :], s)[:, :, 1, :],
                                           level(src, s)[:, :, 1, :]))
                last = V.copy_predicated(a, MASK[:, NL, :], lv[:, NL * P:(NL + 1) * P])
                if t < NT - 1:
                    if t >= 1:
                        v_.wait_ge(o_ready, step_at[(u, t - 1, h)] + 1)
                    st = lv[rows, (NL + 1) * P:(NL + 2) * P]
                    if t == 0:
                        last = V.tensor_copy(S[rows, 1, :], st)
                    else:
                        last = V.scalar_tensor_tensor(out=S[rows, (t + 1) % 2, :], in0=S[rows, t % 2, :],
                                                      scalar=EBL[rows, t:t + 1], in1=st, op0=ALU.mult, op1=ALU.add)
                last.then_inc(at_ready, 1)

            def o_post(u):
                nh = heads(u)
                v_.wait_ge(rr_h, u + 1)
                v_.wait_ge(silu_g, u + 1)
                link(inverse(0, nh * NT))
                for h in range(nh):
                    for t in range(NT):
                        gate = GVB[:, t, (2 + h) * P:(3 + h) * P] if is_gla(u) else GVH[:, t, 0:P]
                        i = h * NT + t
                        last = V.scalar_tensor_tensor(out=O[:, h, t, :], in0=O[:, h, t, :], scalar=RR[:, i:i + 1],
                                                      in1=gate, op0=ALU.mult, op1=ALU.mult)
                last.then_inc(og_ready, 1)

            decay(0)
            v_.wait_ge(lf_ready, 1)
            link(V.tensor_tensor(LB[:, 1, :], LBT[:, 0, :], LBT[:, 1, :], ALU.add))
            link(V.reciprocal(LB[:, 1, :], LB[:, 1, :]))
            link(V.tensor_tensor(LB[:, 0, :], LBT[:, 0, :], LB[:, 1, :], ALU.mult))
            link(V.tensor_scalar(LB[:, 0, :], LB[:, 0, :], 4.3e-18, None, ALU.max))
            link(V.tensor_scalar(LB[:, 1, :], LB[:, 0, :], -1.0, 1.0, ALU.mult, ALU.add))
            link(V.tensor_scalar(LB[:, 2, :], LB[:, 1, :], -1.0, None, ALU.mult))
            for i in range(NL):
                sub(0, i)
            for k in range(3):
                unit_slice()
            for i in range(NL):
                mul(0, i)
            for name, _, _ in k_chunks(1):
                low(1, name)
            for k in range(3, KD):
                unit_slice()
            for name, _, _ in gv_chunks(1)[0:2]:
                low(1, name)
            for u in range(UNITS):
                sub(u, NL)
                sub(u, NL + 1)
                if u > 0:
                    v_.wait_ge(pj_ready, number[("oT", u - 1, heads(u - 1) - 1, 1)] + 1)
                sub(u, NL + 2)
                for i in range(NL, ITEMS):
                    mul(u, i)
                if u > 0:
                    for k in range(KD - LAST_SLICES if u + 1 == UNITS else KD // 2):
                        unit_slice()
                if u + 1 < UNITS:
                    decay(u + 1)
                    if u == 0:
                        for name, _, _ in gv_chunks(1)[2:]:
                            low(1, name)
                for n in range(first_step[u], first_step[u + 1]):
                    attention_step(n)
                column(UNIT_ADA[u], *COLUMN[UNIT_ADA[u]])
                if u + 1 < UNITS:
                    for i in range(NL):
                        sub(u + 1, i)
                o_post(u)
                if 0 < u < UNITS - 2:
                    for name, _, _ in k_chunks(u + 2):
                        low(u + 2, name)
                if u + 1 < UNITS:
                    n = LAST_SLICES if u + 2 == UNITS else KD // 2
                    for i in range(NL):
                        for k in range(n * i // NL, n * (i + 1) // NL):
                            unit_slice()
                        mul(u + 1, i)
                if u < UNITS - 2:
                    for name, _, _ in (k_chunks(2) if u == 0 else []) + gv_chunks(u + 2):
                        low(u + 2, name)
            for half in range(2):
                n = number[("row", "gt1", half)]
                v_.wait_ge(pj_free[n % 2], n // 2 + 1)

            def residual(t):
                for half in range(2):
                    n = number[("wo", t, half)]
                    hs = slice(half * HALF, (half + 1) * HALF)
                    v_.wait_ge(pj_ready, n + 1)
                    V.tensor_tensor(X1[:, t, hs], PJ[n % 2], GT1B[:, hs], ALU.mult).then_inc(pj_free[n % 2], 1)
                    v_.wait_ge(pj_free[n % 2], n // 2 + 1)
                    if half == 0:
                        v_.wait_ge(xt_in[t % 2], 16 * (t // 2 + 1))
                    i = V.tensor_tensor(X1[:, t, hs], X1[:, t, hs], XT[:, t % 2, hs], ALU.add)
                i.then_inc(x1_ready, 1)

            def h2_evac(t):
                for half in range(2):
                    n = number[("h2T", t, half)]
                    v_.wait_ge(pj_ready, n + 1)
                    dst = H2T[:, 4 * half:4 * half + 4, t % 4 * P:(t % 4 + 1) * P]
                    ks = slice(4 * half, 4 * half + 4)
                    V.tensor_tensor(dst, PJ[n % 2].rearrange("p (k n) -> p k n", k=4),
                                    GS2[:, ks].rearrange("p (k a) -> p k a", a=1).to_broadcast([P, 4, P]),
                                    ALU.mult).then_inc(pj_free[n % 2], 1)
                    v_.wait_ge(pj_free[n % 2], n // 2 + 1)
                    V.tensor_tensor(dst, dst, SH2[:, ks].rearrange("p (k a) -> p k a", a=1).to_broadcast([P, 4, P]),
                                    ALU.add).then_inc(h2_ready, 1)

            W = NG + NE
            TH = NT // 2

            def bc_t(ap, w, n=TH):
                return ap.rearrange("p (a w) -> p a w", a=1).to_broadcast([P, n, w])

            def bc_w(ap, w):
                return ap.rearrange("p (t a) -> p t a", a=1).to_broadcast([P, TH, w])

            def bc_g(ap):
                return ap.rearrange("p t (g a) -> p (t g) a", a=1).to_broadcast([P, TH * NG, EG])

            def choose(g):
                hs = slice(g * TH, (g + 1) * TH)
                n = number[("lgT", g)]
                v_.wait_ge(pj_ready, n + 1)
                V.tensor_tensor(LG[:, hs], PJ[n % 2][:, 0:TH * W].rearrange("p (t w) -> p t w", t=TH),
                                bc_t(BR[:], W), ALU.add).then_inc(pj_free[n % 2], 1)
                v_.wait_ge(pj_free[n % 2], n // 2 + 1)
                g_, e_ = LG[:, hs, 0:NG], LG[:, hs, NG:W]
                vm, vd, v1, v2, vq = (V8[:, i, hs] for i in (0, 3, 5, 6, 7))
                gd, ohg, pen, em, scr = GD[:, hs], OHG[:, hs], PEN[:, hs], EM[:, hs], SCR[:, hs]
                link(V.tensor_reduce(vm, g_, AX, ALU.max))
                link(V.tensor_tensor(gd, g_, bc_w(vm, NG), ALU.subtract))
                link(V.scalar_tensor_tensor(out=ohg, in0=gd, scalar=0.0, in1=bc_t(PR[:, NE - NG:NE], NG),
                                            op0=ALU.is_ge, op1=ALU.mult))
                v_.sem_inc(gd_ready, 1)
                link(V.tensor_reduce(vm, ohg, AX, ALU.max))
                link(V.tensor_tensor(ohg, ohg, bc_w(vm, NG), ALU.is_equal))
                link(V.tensor_scalar(pen, ohg, -1.0, BIG, ALU.add, ALU.mult))
                em4 = em.rearrange("p t (g e) -> p (t g) e", g=NG)
                link(V.tensor_copy(em, e_))
                link(V.tensor_tensor(em4, em4, bc_g(ohg), ALU.mult))
                link(V.tensor_tensor(em4, em4, bc_g(pen), ALU.add))

                def pick(mx, oh):
                    link(V.tensor_reduce(mx, em, AX, ALU.max))
                    link(V.tensor_tensor(scr, em, bc_w(mx, NE), ALU.is_ge))
                    link(V.tensor_tensor(scr, scr, bc_t(PR[:], NE), ALU.mult))
                    link(V.tensor_reduce(vq, scr, AX, ALU.max))
                    link(V.tensor_tensor(oh, scr, bc_w(vq, NE), ALU.is_equal))

                pick(v1, M1[:, hs])
                link(V.scalar_tensor_tensor(out=em, in0=M1[:, hs], scalar=-3.0 * BIG, in1=em, op0=ALU.mult, op1=ALU.add))
                pick(v2, M2[:, hs])
                V.tensor_tensor(MB[:, g * TH * NE:(g + 1) * TH * NE].rearrange("p (t e) -> p t e", t=TH),
                                M1[:, hs], M2[:, hs], ALU.add).then_inc(mb_ready, 1)
                link(V.tensor_tensor(vd, v2, v1, ALU.subtract))
                v_.sem_inc(gd_ready, 1)

            def ranks(g):
                n = number[("rank", g)]
                v_.wait_ge(pj_ready, n + 1)
                if g == 1:
                    link(V.tensor_copy(CNT[:], PJ[n % 2][:, TH * NE:(TH + 1) * NE]))
                V.tensor_copy(RK[:, g * TH:(g + 1) * TH].rearrange("p t e -> p (t e)"),
                              PJ[n % 2][:, 0:TH * NE]).then_inc(pj_free[n % 2], 1)
                v_.wait_ge(pj_free[n % 2], n // 2 + 1)

            def picked_slots(hs, dst):
                for k, mk in enumerate((M1, M2)):
                    link(V.tensor_tensor(EM[:, hs], SCR[:, hs], mk[:, hs], ALU.mult))
                    link(V.tensor_reduce(V8[:, 7, hs], EM[:, hs], AX, ALU.add))
                    last = V.tensor_copy(dst[:, k, hs], V8[:, 7, hs])
                    if k == 0:
                        link(last)
                return last

            def slots(g):
                hs = slice(g * TH, (g + 1) * TH)
                link(V.tensor_scalar(SCR[:, hs], RK[:, hs], float(C), float(NSLOT), ALU.is_ge, ALU.mult))
                link(V.tensor_tensor(SCR[:, hs], SCR[:, hs], RK[:, hs], ALU.add))
                link(V.tensor_tensor(SCR[:, hs], SCR[:, hs], bc_t(EC[:], NE), ALU.add))
                picked_slots(hs, SLOTP).then_inc(slots_ready, 1)
                v_.wait_ge(slots_ready, g + 1)

            v_.wait_ge(ios, 10)
            v_.wait_ge(br_in, 32)
            for t in range(NT):
                residual(t)
                if t >= 1:
                    h2_evac(t - 1)
                v_.wait_ge(ss2, t + 1)
                inverse(t, t + 1).then_inc(r2, 1)
                if t == NT - 2:
                    choose(0)
            ranks(0)
            h2_evac(NT - 1)
            slots(0)
            choose(1)
            ranks(1)
            slots(1)
            link(V.tensor_single_scalar(NXE[:], CNT[:], float(C), op=ALU.is_gt))
            for m in range(2, MX + 1):
                link(V.scalar_tensor_tensor(out=NXE[:], in0=CNT[:], scalar=float(C * m), in1=NXE[:],
                                            op0=ALU.is_gt, op1=ALU.add))
            link(V.memset(DX[:], 1.0))
            link(V.tensor_tensor_scan(XINC[:], DX[:], NXE[:], 0.0, ALU.mult, ALU.add))
            link(V.tensor_tensor(DX[:], XINC[:], NXE[:], ALU.subtract))
            link(V.tensor_scalar(DX[:], DX[:], float(NE - 1), float(C), ALU.add, ALU.mult))
            link(V.tensor_tensor(DX[:], DX[:], EC[:], ALU.subtract))
            link(V.tensor_single_scalar(SCR[:], RK[:], float(C), op=ALU.is_ge))
            link(V.tensor_tensor(SCR[:], SCR[:], bc_t(DX[:], NE, NT), ALU.mult))
            link(V.tensor_tensor(SCR[:], SCR[:], RK[:], ALU.add))
            link(V.tensor_tensor(SCR[:], SCR[:], bc_t(EC[:], NE, NT), ALU.add))
            link(picked_slots(slice(0, NT), SLOT))
            link(V.tensor_tensor(CMP[:], XINC[0:1, :].rearrange("p (a e) -> p a e", a=1).to_broadcast([1, NX, NE]),
                                 XS[:].rearrange("p (x a) -> p x a", a=1).to_broadcast([1, NX, NE]), ALU.is_le))
            link(V.tensor_reduce(XEF[:], CMP[:], AX, ALU.add))
            link(V.tensor_scalar(XE[:], XEF[:], float(NE - 1), None, ALU.min))
            V.tensor_copy(NXI[:], XINC[0:1, NE - 1:NE]).then_inc(nx_ready, 1)
            vs, vp, ve = (V8[:, i, :] for i in (1, 2, 4))
            v_.wait_ge(eg_ready, 4)
            link(V.tensor_reduce(vs, GD[:], AX, ALU.add))
            link(V.reciprocal(vp, vs))
            link(V.tensor_scalar(vs, ve, 1.0, None, ALU.add))
            link(V.reciprocal(vs, vs))
            link(V.tensor_tensor(WPAIR[:, 0, :], vp, vs, ALU.mult))
            link(V.tensor_tensor(WPAIR[:, 1, :], WPAIR[:, 0, :], ve, ALU.mult))
            V.memset(XG[0:C], 0.0).then_inc(routed, 1)
            v_.wait_ge(routed, 1)
            for v in ("gt2", "shf", "scf"):
                for half in range(2):
                    n = number[("row", v, half)]
                    v_.wait_ge(pj_free[n % 2], n // 2 + 1)

            def xgt_evac(slot, scaled, count, done):
                for b in range(2):
                    dst = XGT[:, slot, 4 * b:4 * b + 4, :]
                    ks = slice(4 * b, 4 * b + 4)
                    i = V.tensor_tensor(dst, TP[:, b, 0:4 * C].rearrange("p (k n) -> p k n", k=4),
                                        GS2[:, ks].rearrange("p (k a) -> p k a", a=1).to_broadcast([P, 4, C]), ALU.mult)
                i.then_inc(scaled, 1)
                v_.wait_ge(scaled, count)
                for b in range(2):
                    dst = XGT[:, slot, 4 * b:4 * b + 4, :]
                    ks = slice(4 * b, 4 * b + 4)
                    i = V.tensor_tensor(dst, dst, SH2[:, ks].rearrange("p (k a) -> p k a", a=1).to_broadcast([P, 4, C]),
                                        ALU.add)
                i.then_inc(done, 1)

            def act_mul(par, done):
                V.tensor_tensor(ATT[:, par], SIL[:, par],
                                GU[par][:, FB * C:2 * FB * C].rearrange("p (j c) -> p j c", j=FB), ALU.mult).then_inc(done, 1)

            def y_evac(par, done):
                V.tensor_tensor(YB[0:C, par, 0:HALF], YP[par][0:C, 0:HALF], GT2B[0:C, 0:HALF], ALU.mult)
                V.tensor_tensor(YB[0:C, par, HALF:D], YP[par][0:C, HALF:D], GT2B[0:C, HALF:D], ALU.mult).then_inc(done, 1)

            def expert_step(it, s, first, last):
                n = 4 * it + s
                if not (last and s == 3):
                    v_.wait_ge(t_ready, 4 * it + (s + 2))
                    if not (first and s == 0):
                        v_.wait_ge(gu_ready, 4 * it + s)
                    xgt_evac((s + 1) % 2, xgt_scaled, 4 * it + (s + 2), xgt_ready)
                v_.wait_ge(sil_ready, 4 * it + (s + 1))
                if not (first and s < 2):
                    v_.wait_ge(y_ready, 4 * it + (s - 1))
                act_mul(s % 2, att_ready)
                if not (first and s == 0):
                    par = (s + 1) % 2
                    v_.wait_ge(y_ready, 4 * it + s)
                    if not (first and s < 3):
                        v_.wait_ge(y_st[par], 16 * (2 * it) + 16 * ((s - 1) // 2))
                    y_evac(par, y_ev)

            v_.wait_ge(t_ready, 1)
            xgt_evac(0, xgt_scaled, 1, xgt_ready)
            for s in range(4):
                expert_step(0, s, True, False)
            with v_.Fori(1, NE // 4 - 1) as it:
                for s in range(4):
                    expert_step(it, s, False, False)
            for s in range(4):
                expert_step(NE // 4 - 1, s, False, True)
            v_.wait_ge(y_ready, NE)
            v_.wait_ge(y_st[1], 16 * (NE // 2 - 1))
            y_evac(1, y_ev)
            v_.wait_ge(y_st[0], 16 * (NE // 2))
            nx = v_.value_load(NXI[:, :], min_val=0, max_val=NX)
            with v_.If(nx > 0):
                with v_.Fori(0, NX) as i:
                    with v_.If(nx > i):
                        v_.wait_ge(xt_ready, i + 1)
                        xgt_evac(0, xxgt_scaled, i + 1, xxgt)
                        v_.wait_ge(xsil, i + 1)
                        act_mul(0, xatt)
                        v_.wait_ge(xy, i + 1)
                        y_evac(0, xyev)
                v_.nop()
            def add_rows(t):
                for k in range(2):
                    if k == 0:
                        v_.wait_ge(yg_in[t % 4], 32 * (t // 4 + 1))
                    i = V.scalar_tensor_tensor(out=X1[:, t, :], in0=YG[:, t % 4, k, :], scalar=WPAIR[:, k, t:t + 1],
                                               in1=X1[:, t, :], op0=ALU.mult, op1=ALU.add)
                    if k == 0:
                        link(i)
                    else:
                        i.then_inc(x2_ready, 1)

            add_rows(0)
            for t in range(NT):
                if t + 1 < NT:
                    add_rows(t + 1)
                v_.wait_ge(ss3, t + 1)
                link(inverse(t, t + 1))
                if t >= 2:
                    v_.wait_ge(out_st[t % 2], 16 * (t // 2))
                V.scalar_tensor_tensor(out=OUTT[:, t % 2, :], in0=X1[:, t, :], scalar=RR[:, t:t + 1], in1=GSF[:],
                                       op0=ALU.mult, op1=ALU.mult).then_inc(out_scaled, 1)

        @block.tensor
        def _(pe):
            MM, TR = nc.tensor.matmul, nc.tensor.transpose

            def begin(job):
                n = number[job]
                if n >= 2:
                    pe.wait_ge(pj_free[n % 2], n // 2)
                return PJ[n % 2]

            def evacuated(job):
                n = number[job]
                pe.wait_ge(pj_free[n % 2], n // 2 + 1)

            def col_job(v, acc, summed, count):
                pe.wait_ge(summed, count)
                ps = begin(("col", v))
                for k in range(KD):
                    last = MM(ps[:, k:k + 1], acc[:, k::KD], ONESF[:, 0:1], start=True, stop=True)
                last.then_inc(pj_ready, 1)

            def row_job(v, col):
                for half in range(2):
                    ps = begin(("row", v, half))
                    for k in range(4):
                        kk = 4 * half + k
                        last = MM(ps[:, k * P:(k + 1) * P], col[:, kk:kk + 1].to_broadcast([P, P]), IDENT[:], start=True, stop=True)
                    last.then_inc(pj_ready, 1)

            pe.wait_ge(ios, 5)
            col_job("sc1", ACC, ast_used, KD)
            col_job("sh1", ACCB, ast_used, 2 * KD)

            def x_transposes(g, blocks):
                pe.wait_ge(xr_ready, 4 * g + 4)
                for k in blocks:
                    ps = begin(("xT", g, k))
                    for t in range(4):
                        last = TR(ps[:, t * P:(t + 1) * P], XR[:, 4 * g + t, k::KD], IDENT[:])
                    last.then_inc(pj_ready, 1)

            def chunk(u, name):
                n = chunk_at[(u, name)]
                pe.wait_ge(wl_ready, n + 1)
                return chunk_slot[n]

            def product(ps, wh, wl, xh, xl, first, last):
                MM(ps, wh, xh, start=first, stop=False)
                MM(ps, wh, xl, start=False, stop=False)
                return MM(ps, wl, xh, start=False, stop=last)

            def k_job(u, name, half):
                hs = slice(half * HALF, (half + 1) * HALF)
                if name == "a":
                    if half == 0:
                        for h in range(2):
                            evacuated((0, "ga", h))
                    ps = begin((u, name, half))
                    MM(ps, WA2[:, u * P:(u + 1) * P], GA[:, hs], start=True, stop=True).then_inc(pj_ready, 1)
                    return
                if name == "ga":
                    pe.wait_ge(wg_low, 1)
                    ps = begin((u, name, half))[0:RANK, :]
                else:
                    slot = chunk(u, name)
                    ps = begin((u, name, half))
                for k in range(KD):
                    if (u, name) == (0, "q"):
                        pe.wait_ge(xl_ready, half * KD + k + 1)
                    wh, wl = (WGH[:, k, :], WGL[:, k, :]) if name == "ga" else (WH[:, slot, k, :], WL[:, slot, k, :])
                    last = product(ps, wh, wl, HT[:, k, hs], HL[:, k, hs], k == 0, k == KD - 1)
                last.then_inc(pj_ready, 1)

            def gv_job(u, i):
                s0 = min(chunk(u, name) for name in gv_names(u, i))
                ps = begin((u, "gv", i))
                for tt in range(2):
                    ts = slice((2 * (i % 4) + tt) * P, (2 * (i % 4) + tt + 1) * P)
                    dst = ps[:, 2 * tt * P:2 * (tt + 1) * P].rearrange("p (c n) -> p c n", c=2)
                    for k in range(KD):
                        last = product(dst, HT[:, k, ts], HL[:, k, ts], WH[:, s0:s0 + 2, k, :],
                                       WL[:, s0:s0 + 2, k, :], k == 0, k == KD - 1)
                last.then_inc(pj_ready, 1)

            def levels(n):
                u, t, h = steps[n]
                rows = slice(64 * h, 64 * h + 64) if is_gla(u) else slice(0, P)
                ts = slice(t * P, (t + 1) * P)
                if n >= 2:
                    pe.wait_ge(at_ready, n - 1)
                lv = LV[n % 2]
                for l in range(NL):
                    MM(lv[:, l * P:(l + 1) * P], XL[rows, l, ts], XL[rows, l, ts], start=True, stop=True)
                last = MM(lv[:, NL * P:(NL + 1) * P], BB[rows, ts], BA[rows, ts], start=True, stop=True)
                if t < NT - 1:
                    last = MM(lv[rows, (NL + 1) * P:(NL + 2) * P], KH[:, t, rows], values(u, t, h), start=True, stop=True)
                last.then_inc(lv_ready, 1)

            def values(u, t, h):
                return GVB[:, t, h * P:(h + 1) * P] if is_gla(u) else GVH[:, t, P:2 * P]

            def output(n):
                u, t, h = steps[n]
                rows = slice(64 * h, 64 * h + 64) if is_gla(u) else slice(0, P)
                pe.wait_ge(at_ready, n + 1)
                if n >= 2:
                    pe.wait_ge(o_free, n - 1)
                last = MM(OP[n % 2], AT2[:, n % 2, :], values(u, t, h), start=True, stop=(t == 0))
                if t > 0:
                    last = MM(OP[n % 2], QE[rows, t * P:(t + 1) * P], S[rows, t % 2, :], start=False, stop=True)
                last.then_inc(o_ready, 1)

            x_transposes(0, range(KD))
            k = 0
            for j in start_order:
                if j is None:
                    x_transposes(1, range(k, k + 2))
                    k += 2
                else:
                    k_job(0, *j)
            for name, half in k_jobs(0)[3:]:
                k_job(0, name, half)
            for _, i in gv_jobs(0):
                gv_job(0, i)
            for u in range(UNITS):
                if u + 1 < UNITS:
                    for name, half in k_jobs(u + 1):
                        k_job(u + 1, name, half)
                pe.wait_ge(e_mul, ITEMS * (u + 1))
                for g in range(2):
                    ps = begin(("khT", u, g))
                    for t in range(4):
                        last = TR(ps[:, t * P:(t + 1) * P], KHT[:, (4 * g + t) * P:(4 * g + t + 1) * P], IDENT[:])
                    last.then_inc(pj_ready, 1)
                for g in range(2):
                    evacuated(("khT", u, g))
                for _, i in gv_jobs(u)[-2:]:
                    evacuated((u, "gv", i))
                lo, hi = first_step[u], first_step[u + 1]
                levels(lo)
                for n in range(lo + 1, hi):
                    levels(n)
                    output(n - 1)
                output(hi - 1)
                col_job(UNIT_ADA[u], ACC, ar_used, KD * (u + 1))
                if u + 1 < UNITS:
                    for _, i in gv_jobs(u + 1):
                        gv_job(u + 1, i)
                pe.wait_ge(og_ready, u + 1)
                for h in range(heads(u)):
                    for g in range(2):
                        ps = begin(("oT", u, h, g))
                        for t in range(4):
                            last = TR(ps[:, t * P:(t + 1) * P], O[:, h, 4 * g + t, :], IDENT[:])
                        last.then_inc(pj_ready, 1)
            row_job("gt1", GT1)
            for g in range(2):
                evacuated(("oT", UNITS - 1, 0, g))
            pe.wait_ge(wout_in, 16 * 8)
            pe.wait_ge(ot_in, 16 * 7)
            W = NG + NE

            def transpose_xn(t):
                pe.wait_ge(xn_ready, t + 1)
                for half in range(2):
                    ps = begin(("h2T", t, half))
                    for k in range(4):
                        last = TR(ps[:, k * P:(k + 1) * P], XN[:, t % 2, 4 * half + k::KD], IDENT[:])
                    last.then_inc(pj_ready, 1)

            for kind, i in out_order:
                if kind == "wo":
                    for half in range(2):
                        ps = begin(("wo", i, half))
                        for v in range(8):
                            last = MM(ps, OT[:, v, i * P:(i + 1) * P], WOUT[:, v, half * HALF:(half + 1) * HALF],
                                      start=(v == 0), stop=(v == 7))
                        last.then_inc(pj_ready, 1)
                elif kind == "h2T":
                    transpose_xn(i)
                elif kind == "lg":
                    pe.wait_ge(h2_ready, NT * (i + 1))
                    pe.wait_ge(wrt_in, 32)
                    ps = begin(("lg", i))
                    for k in range(KD):
                        last = MM(ps[0:W, :], WRT[:, k, :], H2T[:, k, :], start=(k == 0), stop=(k == KD - 1))
                    last.then_inc(pj_ready, 1)
                elif kind == "lgT":
                    evacuated(("lg", i))
                    ps = begin(("lgT", i))
                    for t in range(4):
                        last = TR(ps[:, t * W:(t + 1) * W], LGS[:, (4 * i + t) * P:(4 * i + t + 1) * P], IDENT[0:W, 0:W])
                    last.then_inc(pj_ready, 1)
                else:
                    pe.wait_ge(mb_ready, i + 1)
                    ps = begin(("rank", i))
                    lo, hi = 4 * i, 4 * i + 4
                    last = MM(ps[:, 0:4 * NE], UT[:], MB[:, lo * NE:hi * NE], start=True, stop=False)
                    for j in range(1, hi):
                        a = max(lo, j)
                        last = MM(ps[:, (a - lo) * NE:4 * NE], ONEB[:], MB[:, (a - j) * NE:(hi - j) * NE],
                                  start=False, stop=(j == hi - 1))
                    if i == 1:
                        for t in range(NT):
                            last = MM(ps[:, 4 * NE:5 * NE], ONEB[:], MB[:, t * NE:(t + 1) * NE],
                                      start=(t == 0), stop=(t == NT - 1))
                    last.then_inc(pj_ready, 1)
            row_job("gt2", GT2)
            row_job("shf", SHC)
            row_job("scf", GSC)
            evacuated(("row", "scf", 1))
            evacuated(("row", "scf", 0))

            def xg_transposes(slot, done):
                for k in range(KD):
                    last = TR(TP[:, k // 4, (k % 4) * C:(k % 4 + 1) * C], XG[0:C, slot, k::KD], IDENT[0:C, 0:C])
                last.then_inc(done, 1)

            def gate_up(par, slot, done):
                for m in range(2):
                    for j in range(FB):
                        col = (m * FB + j) * C
                        for k in range(KD):
                            last = MM(GU[par][:, col:col + C], WGU[slot][:, m, k, j * P:(j + 1) * P],
                                      XGT[:, par, k, :], start=(k == 0), stop=(k == KD - 1))
                last.then_inc(done, 1)

            def down(par, slot, done):
                for half in range(2):
                    for j in range(FB):
                        last = MM(YP[par][0:C, half * HALF:(half + 1) * HALF], ATT[:, par, j, :],
                                  WDN[slot][:, j, half * HALF:(half + 1) * HALF], start=(j == 0), stop=(j == FB - 1))
                last.then_inc(done, 1)

            def expert_step(it, s, first, last):
                if not (last and s == 3):
                    pe.wait_ge(xg_in[(s + 1) % 4], 16 * it + 16 * ((s + 1) // 4 + 1))
                    pe.wait_ge(xgt_ready, 4 * it + (s + 1))
                    xg_transposes((s + 1) % 4, t_ready)
                pe.wait_ge(wexp_in[s], 48 * it + 48)
                pe.wait_ge(xgt_ready, 4 * it + (s + 1))
                if not (first and s < 2):
                    pe.wait_ge(att_ready, 4 * it + (s - 1))
                gate_up(s % 2, s, gu_ready)
                if not (first and s == 0):
                    pe.wait_ge(att_ready, 4 * it + s)
                    if not (first and s < 3):
                        pe.wait_ge(y_ev, 4 * it + (s - 2))
                    down((s + 1) % 2, (s + 3) % 4, y_ready)

            pe.wait_ge(xg_in[0], 16)
            xg_transposes(0, t_ready)
            for s in range(4):
                expert_step(0, s, True, False)
            with pe.Fori(1, NE // 4 - 1) as it:
                for s in range(4):
                    expert_step(it, s, False, False)
            for s in range(4):
                expert_step(NE // 4 - 1, s, False, True)
            pe.wait_ge(att_ready, NE)
            pe.wait_ge(y_ev, NE - 2)
            down(1, 3, y_ready)
            nx = pe.value_load(NXI[:, :], min_val=0, max_val=NX)
            with pe.If(nx > 0):
                with pe.Fori(0, NX) as i:
                    with pe.If(nx > i):
                        pe.wait_ge(xxg_in, 16 * i + 16)
                        xg_transposes(0, xt_ready)
                        pe.wait_ge(xw_in, 48 * i + 48)
                        pe.wait_ge(xxgt, i + 1)
                        gate_up(0, 0, xgu)
                        pe.wait_ge(xatt, i + 1)
                        down(0, 0, xy)
                pe.nop()


_INS = ["x", "c", "w_ada", "b_ada", "norm1_g", "w_in", "gla_w_a2", "gla_b_a", "gla_norm_g", "hg_norm_g",
        "hg_lb_logits", "w_out", "norm2_g", "w_rg", "b_rg", "w_re", "b_re", "w_exp_gate", "w_exp_up",
        "w_exp_down", "w_ada_final", "b_ada_final", "norm_f_g"]


def kernel(**inputs):
    import numpy as np
    import concourse.bacc as bacc
    from concourse.bass_utils import run_bass_kernel_spmd

    nc = bacc.Bacc("TRN2", target_bir_lowering=False, num_devices=1)
    arrays, args = {}, []
    for name in _INS:
        a = np.ascontiguousarray(inputs[name])
        arrays[f"in_{name}"] = a
        args.append(nc.dram_tensor(f"in_{name}", a.shape, mybir.dt.from_np(a.dtype), kind="ExternalInput").ap())
    shape = np.asarray(inputs["x"]).shape
    args.append(nc.dram_tensor("out_x", shape, F32, kind="ExternalOutput").ap())
    layer_kernel(nc, *args)
    r = run_bass_kernel_spmd(nc, [arrays], core_ids=[0])
    return r.results[0]["out_x"]
```
